# Optimizing a Trainium2 kernel written in Bass

```python
import math
import jax, jax.numpy as jnp
from jax import lax
import numpy as np

D_MODEL = 1024
BATCH = 1
SEQ = 128
DEPTH = 2
DEC_BATCH = 1
DEC_SEQ = 256
PAST_LEN = 128

GRID_W = 64
N_MIXERS = 2
N_LAYERS_A = (DEPTH + 1) // 2
N_LAYERS_B = DEPTH // 2
CONV_W = 5
CHUNK = 64
E_A = 2 * D_MODEL
H_A = 4
DH_A = E_A // H_A
QKV_BLOCK = 4
E_B = 2 * D_MODEL
P_B = 64
H_B = E_B // P_B
G_B = 4
HG_B = H_B // G_B
D_STATE = 128
MOE_GROUPS = 4
MOE_EXPERTS = 4
TOP_K_E = 2
D_FF_E = 256
ALPHA = (2.0 * DEPTH) ** 0.25
BETA = (8.0 * DEPTH) ** -0.25
EPS = 1e-5

kernel_name = 'hybrid_mlstm_ssd_hmoe_diffusion_step'

def _layer_norm(x, w, b):
    xf = x.astype(jnp.float32)
    mu = jnp.mean(xf, axis=-1, keepdims=True)
    var = jnp.mean(jnp.square(xf - mu), axis=-1, keepdims=True)
    y = (xf - mu) * lax.rsqrt(var + EPS) * w.astype(jnp.float32) + b.astype(jnp.float32)
    return y.astype(x.dtype)

def _rms_norm(x, w):
    xf = x.astype(jnp.float32)
    return xf * lax.rsqrt(jnp.mean(jnp.square(xf), axis=-1, keepdims=True) + EPS) * w.astype(jnp.float32)

def _dwconv(x, w, b):
    y = lax.conv_general_dilated(x, w[:, None, :].astype(x.dtype), window_strides=(1,),
                                 padding=[(CONV_W // 2, CONV_W // 2)],
                                 dimension_numbers=('NWC', 'WIO', 'NWC'),
                                 feature_group_count=x.shape[-1])
    return y + b

def _flip(t):
    return jnp.flip(t, axis=1)

def _grid_to_cols(x):
    b, l, d = x.shape
    rows = l // GRID_W
    return x.reshape(b, rows, GRID_W, d).transpose(0, 2, 1, 3).reshape(b, l, d)

def _cols_to_grid(x):
    b, l, d = x.shape
    rows = l // GRID_W
    return x.reshape(b, GRID_W, rows, d).transpose(0, 2, 1, 3).reshape(b, l, d)

def _mlstm_chunk_scan(q, k, v, ig, lf, C0, n0, m0):
    bsz, l, h, dh = q.shape
    nc = l // CHUNK
    scale = dh ** -0.5
    mask = jnp.tril(jnp.ones((CHUNK, CHUNK), dtype=bool))

    def chunks(t):
        t = t.astype(jnp.float32).reshape((bsz, nc, CHUNK) + t.shape[2:])
        return jnp.moveaxis(jnp.moveaxis(t, 1, 0), 2, 3)

    def step(carry, inp):
        C, n, m = carry
        qc, kc, vc, ic, fc = inp
        qc = qc * scale
        b = jnp.cumsum(fc, axis=-1)
        logw = jnp.where(mask, b[..., :, None] - b[..., None, :] + ic[..., None, :], -jnp.inf)
        inter = b + m[..., None]
        m_s = jnp.maximum(inter, jnp.max(logw, axis=-1))
        s = jnp.einsum('bhsd,bhrd->bhsr', qc, kc) * jnp.exp(logw - m_s[..., None])
        w_inter = jnp.exp(inter - m_s)
        num = w_inter[..., None] * jnp.einsum('bhsd,bhde->bhse', qc, C) + jnp.einsum('bhsr,bhre->bhse', s, vc)
        den = w_inter * jnp.einsum('bhsd,bhd->bhs', qc, n) + jnp.sum(s, axis=-1)
        h_out = num / jnp.maximum(jnp.abs(den), jnp.exp(-m_s))[..., None]
        b_last = b[..., -1]
        logk = b_last[..., None] - b + ic
        m_new = jnp.maximum(b_last + m, jnp.max(logk, axis=-1))
        decay = jnp.exp(b_last + m - m_new)
        wk = jnp.exp(logk - m_new[..., None])
        C_new = decay[..., None, None] * C + jnp.einsum('bhr,bhrd,bhre->bhde', wk, kc, vc)
        n_new = decay[..., None] * n + jnp.einsum('bhr,bhrd->bhd', wk, kc)
        return (C_new, n_new, m_new), h_out

    carry0 = (C0.astype(jnp.float32), n0.astype(jnp.float32), m0.astype(jnp.float32))
    (C, n, m), hs = lax.scan(step, carry0, (chunks(q), chunks(k), chunks(v), chunks(ig), chunks(lf)))
    hs = hs.transpose(1, 0, 3, 2, 4).reshape(bsz, l, h, dh)
    return hs, C, n, m

def _ssd_chunk_scan(x, dt, A, Bm, Cm, h0):
    bsz, l = x.shape[:2]
    nc = l // CHUNK
    mask = jnp.tril(jnp.ones((CHUNK, CHUNK), dtype=bool))

    def chunks(t):
        return jnp.moveaxis(t.astype(jnp.float32).reshape((bsz, nc, CHUNK) + t.shape[2:]), 1, 0)

    def step(hst, inp):
        xc, dtc, Bc, Cc = inp
        acs = jnp.cumsum(dtc * A, axis=1)
        seg = acs[:, :, None] - acs[:, None, :]
        decay = jnp.exp(jnp.where(mask[None, :, :, None, None], seg, -jnp.inf))
        cb = jnp.einsum('bsgn,brgn->bsrg', Cc, Bc)
        w = cb[..., None] * decay * dtc[:, None]
        y = jnp.einsum('bsrgh,brghp->bsghp', w, xc)
        y = y + jnp.einsum('bsgn,bghpn->bsghp', Cc, hst) * jnp.exp(acs)[..., None]
        a_last = acs[:, -1]
        wr = jnp.exp(a_last[:, None] - acs) * dtc
        h_new = jnp.exp(a_last)[..., None, None] * hst + jnp.einsum('brgh,brghp,brgn->bghpn', wr, xc, Bc)
        return h_new, y

    hst, ys = lax.scan(step, h0.astype(jnp.float32), (chunks(x), chunks(dt), chunks(Bm), chunks(Cm)))
    return jnp.moveaxis(ys, 0, 1).reshape(x.shape), hst

def _mlstm_mixer(h, w_in, conv_w, conv_b, w_q, w_k, w_v, w_gates, b_gates, norm_w, skip, w_down, C0, n0, m0):
    bsz, l, _ = h.shape
    xu, z = jnp.split(h @ w_in, 2, axis=-1)
    xc = jax.nn.silu(_dwconv(xu, conv_w, conv_b))

    def blockdiag(t, w):
        return jnp.einsum('blnc,ncd->blnd', t.reshape(bsz, l, E_A // QKV_BLOCK, QKV_BLOCK), w).reshape(bsz, l, E_A)

    q = blockdiag(xc, w_q)
    k = blockdiag(xc, w_k)
    v = blockdiag(xu, w_v)
    gates = (jnp.concatenate([q, k, v], axis=-1) @ w_gates + b_gates).astype(jnp.float32)
    gates = gates.reshape(bsz, l, 2, 2, H_A)
    ig = gates[:, :, :, 0]
    lf = jax.nn.log_sigmoid(gates[:, :, :, 1])
    qh, kh, vh = (t.reshape(bsz, l, H_A, DH_A) for t in (q, k, v))
    hf, Cf, nf, mf = _mlstm_chunk_scan(qh, kh, vh, ig[:, :, 0], lf[:, :, 0], C0[:, 0], n0[:, 0], m0[:, 0])
    hb, Cb, nb, mb = _mlstm_chunk_scan(_flip(qh), _flip(kh), _flip(vh), _flip(ig[:, :, 1]), _flip(lf[:, :, 1]),
                                       C0[:, 1], n0[:, 1], m0[:, 1])
    hs = hf + _flip(hb)
    mu = jnp.mean(hs, axis=-1, keepdims=True)
    var = jnp.mean(jnp.square(hs - mu), axis=-1, keepdims=True)
    hn = ((hs - mu) * lax.rsqrt(var + EPS)).reshape(bsz, l, E_A) * norm_w
    out = ((hn + skip * xc) * jax.nn.silu(z)).astype(h.dtype) @ w_down
    return out, jnp.stack([Cf, Cb], axis=1), jnp.stack([nf, nb], axis=1), jnp.stack([mf, mb], axis=1)

def _ssd_mixer(h, w_in, conv_w, conv_b, dt_bias, a_log, d_skip, norm_w, w_out, h0):
    bsz, l, _ = h.shape
    gn = G_B * D_STATE
    proj = h @ w_in
    z = proj[..., :E_B]
    xbc = jax.nn.silu(_dwconv(proj[..., E_B:2 * E_B + 2 * gn], conv_w, conv_b))
    dt_raw = proj[..., 2 * E_B + 2 * gn:]
    x = xbc[..., :E_B].reshape(bsz, l, G_B, HG_B, P_B)
    Bm = xbc[..., E_B:E_B + gn].reshape(bsz, l, G_B, D_STATE)
    Cm = xbc[..., E_B + gn:].reshape(bsz, l, G_B, D_STATE)
    dt = jax.nn.softplus(dt_raw.astype(jnp.float32).reshape(bsz, l, 2, G_B, HG_B)
                         + dt_bias.astype(jnp.float32).reshape(2, G_B, HG_B))
    A = -jnp.exp(a_log.astype(jnp.float32)).reshape(2, G_B, HG_B)
    h0g = h0.reshape(bsz, 2, G_B, HG_B, P_B, D_STATE)
    yf, sf = _ssd_chunk_scan(x, dt[:, :, 0], A[0], Bm, Cm, h0g[:, 0])
    yb, sb = _ssd_chunk_scan(_flip(x), _flip(dt[:, :, 1]), A[1], _flip(Bm), _flip(Cm), h0g[:, 1])
    y = yf + _flip(yb) + d_skip.reshape(G_B, HG_B)[..., None] * x
    y = _rms_norm(y.reshape(bsz, l, E_B) * jax.nn.silu(z), norm_w)
    out = y.astype(h.dtype) @ w_out
    return out, jnp.stack([sf, sb], axis=1).reshape(bsz, 2, H_B, P_B, D_STATE)

def _hier_moe(h, w_rg, b_rg, w_re, b_re, w_gate, w_up, w_down):
    glog = (h @ w_rg + b_rg).astype(jnp.float32)
    gp, gi = lax.top_k(jax.nn.softmax(glog, axis=-1), 1)
    oh_g = jax.nn.one_hot(gi[..., 0], MOE_GROUPS, dtype=jnp.float32)
    elog = (jnp.einsum('bld,gde->blge', h, w_re) + b_re).astype(jnp.float32)
    elog_sel = jnp.einsum('blge,blg->ble', elog, oh_g)
    ev, ei = lax.top_k(elog_sel, TOP_K_E)
    ew = jax.nn.softmax(ev, axis=-1) * gp
    we = jnp.einsum('blk,blke->ble', ew, jax.nn.one_hot(ei, MOE_EXPERTS, dtype=jnp.float32))
    combine = (oh_g[..., None] * we[:, :, None, :]).astype(h.dtype)
    a = jax.nn.silu(jnp.einsum('bld,gedf->blgef', h, w_gate)) * jnp.einsum('bld,gedf->blgef', h, w_up)
    return jnp.einsum('blgef,gefd->bld', a * combine[..., None], w_down)

def setup_inputs(seed: int = 0) -> dict:
    key = jax.random.key(seed)
    ks = iter(jax.random.split(key, 48))
    f32 = jnp.float32

    def nrm(shape, scale):
        return scale * jax.random.normal(next(ks), shape, f32)

    gn = G_B * D_STATE
    b_i = nrm((N_LAYERS_A, 2, 1, H_A), 0.1)
    b_f = jnp.linspace(3.0, 6.0, H_A, dtype=f32) + nrm((N_LAYERS_A, 2, 1, H_A), 0.1)
    dt0 = jnp.exp(jax.random.uniform(next(ks), (N_LAYERS_B, 2, H_B), f32, math.log(1e-3), math.log(1e-1)))
    return {
        'x_prompt': nrm((BATCH, SEQ, D_MODEL), 1.0),
        'x_sample': nrm((DEC_BATCH, DEC_SEQ, D_MODEL), 1.0),
        'state_mlstm_C': nrm((DEC_BATCH, N_LAYERS_A, 2, H_A, DH_A, DH_A), 0.02),
        'state_mlstm_n': nrm((DEC_BATCH, N_LAYERS_A, 2, H_A, DH_A), 0.1),
        'state_mlstm_m': nrm((DEC_BATCH, N_LAYERS_A, 2, H_A), 0.5),
        'state_ssd': nrm((DEC_BATCH, N_LAYERS_B, 2, H_B, P_B, D_STATE), 0.1),
        'c': nrm((DEC_BATCH, D_MODEL), 1.0),
        'c_ctx': nrm((D_MODEL,), 1.0),
        'ada_w': nrm((DEPTH, D_MODEL, 6 * D_MODEL), 0.5 * D_MODEL ** -0.5),
        'ada_b': nrm((DEPTH, 6 * D_MODEL), 0.02),
        'ln_w': 1.0 + nrm((DEPTH, 2, D_MODEL), 0.01),
        'ln_b': nrm((DEPTH, 2, D_MODEL), 0.01),
        'a_w_in': nrm((N_LAYERS_A, D_MODEL, 2 * E_A), D_MODEL ** -0.5),
        'a_conv_w': nrm((N_LAYERS_A, CONV_W, E_A), CONV_W ** -0.5),
        'a_conv_b': nrm((N_LAYERS_A, E_A), 0.01),
        'a_w_q': nrm((N_LAYERS_A, E_A // QKV_BLOCK, QKV_BLOCK, QKV_BLOCK), QKV_BLOCK ** -0.5),
        'a_w_k': nrm((N_LAYERS_A, E_A // QKV_BLOCK, QKV_BLOCK, QKV_BLOCK), QKV_BLOCK ** -0.5),
        'a_w_v': nrm((N_LAYERS_A, E_A // QKV_BLOCK, QKV_BLOCK, QKV_BLOCK), QKV_BLOCK ** -0.5),
        'a_w_gates': nrm((N_LAYERS_A, 3 * E_A, 4 * H_A), (3 * E_A) ** -0.5),
        'a_b_gates': jnp.concatenate([b_i, b_f], axis=2).reshape(N_LAYERS_A, 4 * H_A),
        'a_norm_w': 1.0 + nrm((N_LAYERS_A, E_A), 0.01),
        'a_skip': 1.0 + nrm((N_LAYERS_A, E_A), 0.01),
        'a_w_down': nrm((N_LAYERS_A, E_A, D_MODEL), BETA * E_A ** -0.5),
        'b_w_in': nrm((N_LAYERS_B, D_MODEL, 2 * E_B + 2 * gn + 2 * H_B), D_MODEL ** -0.5),
        'b_conv_w': nrm((N_LAYERS_B, CONV_W, E_B + 2 * gn), CONV_W ** -0.5),
        'b_conv_b': nrm((N_LAYERS_B, E_B + 2 * gn), 0.01),
        'b_dt_bias': dt0 + jnp.log(-jnp.expm1(-dt0)),
        'b_a_log': jnp.log(jax.random.uniform(next(ks), (N_LAYERS_B, 2, H_B), f32, 1.0, 16.0)),
        'b_d_skip': 1.0 + nrm((N_LAYERS_B, H_B), 0.01),
        'b_norm_w': 1.0 + nrm((N_LAYERS_B, E_B), 0.01),
        'b_w_out': nrm((N_LAYERS_B, E_B, D_MODEL), BETA * E_B ** -0.5),
        'moe_w_rg': nrm((DEPTH, D_MODEL, MOE_GROUPS), D_MODEL ** -0.5),
        'moe_b_rg': nrm((DEPTH, MOE_GROUPS), 0.01),
        'moe_w_re': nrm((DEPTH, MOE_GROUPS, D_MODEL, MOE_EXPERTS), D_MODEL ** -0.5),
        'moe_b_re': nrm((DEPTH, MOE_GROUPS, MOE_EXPERTS), 0.01),
        'moe_w_gate': nrm((DEPTH, MOE_GROUPS, MOE_EXPERTS, D_MODEL, D_FF_E), D_MODEL ** -0.5),
        'moe_w_up': nrm((DEPTH, MOE_GROUPS, MOE_EXPERTS, D_MODEL, D_FF_E), D_MODEL ** -0.5),
        'moe_w_down': nrm((DEPTH, MOE_GROUPS, MOE_EXPERTS, D_FF_E, D_MODEL), BETA * D_FF_E ** -0.5),
    }

def reference(x_prompt, x_sample, state_mlstm_C, state_mlstm_n, state_mlstm_m, state_ssd, c, c_ctx,
              ada_w, ada_b, ln_w, ln_b,
              a_w_in, a_conv_w, a_conv_b, a_w_q, a_w_k, a_w_v, a_w_gates, a_b_gates, a_norm_w, a_skip, a_w_down,
              b_w_in, b_conv_w, b_conv_b, b_dt_bias, b_a_log, b_d_skip, b_norm_w, b_w_out,
              moe_w_rg, moe_b_rg, moe_w_re, moe_b_re, moe_w_gate, moe_w_up, moe_w_down):
    xp, xs = x_prompt, x_sample
    bp = xp.shape[0]
    new_C, new_n, new_m, new_s = [], [], [], []
    for i in range(DEPTH):
        j = i // N_MIXERS
        mp = (jax.nn.silu(c_ctx) @ ada_w[i] + ada_b[i]).reshape(6, D_MODEL)
        ms = (jax.nn.silu(c) @ ada_w[i] + ada_b[i]).reshape(-1, 6, 1, D_MODEL)
        hp = xp * (1.0 + mp[1]) + mp[0]
        hs = xs * (1.0 + ms[:, 1]) + ms[:, 0]
        if i % N_MIXERS == 0:
            wa = (a_w_in[j], a_conv_w[j], a_conv_b[j], a_w_q[j], a_w_k[j], a_w_v[j], a_w_gates[j], a_b_gates[j],
                  a_norm_w[j], a_skip[j], a_w_down[j])
            yp, Cn, nn_, mn = _mlstm_mixer(hp, *wa,
                                          jnp.zeros((bp, 2, H_A, DH_A, DH_A), jnp.float32),
                                          jnp.zeros((bp, 2, H_A, DH_A), jnp.float32),
                                          jnp.zeros((bp, 2, H_A), jnp.float32))
            ys, _, _, _ = _mlstm_mixer(hs, *wa, state_mlstm_C[:, j], state_mlstm_n[:, j], state_mlstm_m[:, j])
            new_C.append(Cn)
            new_n.append(nn_)
            new_m.append(mn)
        else:
            wb = (b_w_in[j], b_conv_w[j], b_conv_b[j], b_dt_bias[j], b_a_log[j], b_d_skip[j], b_norm_w[j], b_w_out[j])
            yp, sn = _ssd_mixer(hp, *wb, jnp.zeros((bp, 2, H_B, P_B, D_STATE), jnp.float32))
            ys, _ = _ssd_mixer(_grid_to_cols(hs), *wb, state_ssd[:, j])
            ys = _cols_to_grid(ys)
            new_s.append(sn)
        xp = _layer_norm(ALPHA * xp + mp[2] * yp, ln_w[i, 0], ln_b[i, 0])
        xs = _layer_norm(ALPHA * xs + ms[:, 2] * ys, ln_w[i, 0], ln_b[i, 0])
        wm = (moe_w_rg[i], moe_b_rg[i], moe_w_re[i], moe_b_re[i], moe_w_gate[i], moe_w_up[i], moe_w_down[i])
        fp = _hier_moe(xp * (1.0 + mp[4]) + mp[3], *wm)
        fs = _hier_moe(xs * (1.0 + ms[:, 4]) + ms[:, 3], *wm)
        xp = _layer_norm(ALPHA * xp + mp[5] * fp, ln_w[i, 1], ln_b[i, 1])
        xs = _layer_norm(ALPHA * xs + ms[:, 5] * fs, ln_w[i, 1], ln_b[i, 1])
    return (xp, xs, jnp.stack(new_C, axis=1), jnp.stack(new_n, axis=1), jnp.stack(new_m, axis=1), jnp.stack(new_s, axis=1))


_drawn_inputs = setup_inputs


def setup_inputs(seed=0):
    import zlib

    import numpy as np

    out = dict(_drawn_inputs(seed))
    spreads = {}
    factors = {'state_mlstm_C': 8.0,
     'state_mlstm_n': 8.0,
     'state_mlstm_m': 8.0,
     'state_ssd': 30.336,
     'ln_w': 2.727,
     'a_conv_b': 3.425,
     'a_norm_w': 31.179,
     'a_skip': 54.72,
     'b_conv_b': 11.269,
     'b_d_skip': 64.0,
     'b_norm_w': 64.0,
     'moe_b_rg': 8.0,
     'moe_b_re': 37.479,
     'ln_b': 3.563}
    for name, (base, spread) in spreads.items():
        noise = np.random.default_rng([zlib.crc32(name.encode()), seed]).standard_normal(out[name].shape)
        drawn = base * np.exp(spread * noise) if base else spread * noise
        out[name] = __import__('jax').numpy.asarray(drawn.astype(out[name].dtype))
    for name, factor in factors.items():
        out[name] = (out[name] * factor).astype(out[name].dtype)
    return out
```

```python
from contextlib import ExitStack

import concourse.bass as bass
from concourse import mybir

F32 = mybir.dt.float32
ALU = mybir.AluOpType
ACT = mybir.ActivationFunctionType
X = mybir.AxisListType.X

P = 128
TP, TS = 128, 256
T = TP + TS
NT = T // P
STREAMS = ((0, TP), (TP, T))
D = 1024
KD = D // P
E2 = 2048
KE = E2 // P
DEPTH = 2
ALPHA = (2.0 * DEPTH) ** 0.25
EPS = 1e-5
TAPS = 5
PAD = TAPS // 2
W_PAD = T + 4 * PAD
H = 4
DH = E2 // H
KH = DH // P
G = 4
HG = 8
PH = 64
GRID = 64
ROWS = TS // GRID
NG = 4
NE = 4
FF = 256
NEXP = NG * NE
BIG = 1e30
RING = 3
ARENA = 37120
SLAB = 2048


def program(nc, i_, o_):
    ctx = ExitStack()
    with ctx:
        def sb(name, cols, parts=P):
            return ctx.enter_context(nc.sbuf_tensor(name, [parts, cols], F32))

        sems = {}

        def sem(name):
            if name not in sems:
                sems[name] = ctx.enter_context(nc.semaphore(name))
            return sems[name]

        banks = [ctx.enter_context(nc.psum_tensor(f"bank{b}", [P, 512], F32)) for b in range(8)]

        SMALL = 16 * 24

        def v3(ap, n):
            return ap.rearrange("p (n c) -> p n c", n=n)

        def v4(ap, a, b):
            return ap.rearrange("p (a b c) -> p a b c", a=a, b=b)

        xT = v3(sb("xT", KD * T)[:, :], KD)
        hT = v3(sb("hT", KD * T)[:, :], KD)
        ring = sb("ring", RING * SLAB)
        par = v3(sb("par", 5 * P)[:, :], 5)
        mod = sb("mod", DEPTH * 48 * 2)[:, :].rearrange("p (l j v) -> p l j v", l=DEPTH, v=2)
        csil = sb("csil", 2 * KD)
        ident = sb("ident", P)
        ones = sb("ones", P)
        ones_d = sb("ones_d", P)
        strip_f = sb("strip_f", 3 * P)
        strip_b = sb("strip_b", 3 * P)
        blockmask = sb("blockmask", P)
        gates_w = sb("gates_w", 3 * KE * 16)
        route_w = sb("route_w", DEPTH * KD * 20)[:, :].rearrange("p (l k c) -> p l k c", l=DEPTH, k=KD)
        route_b = sb("route_b", DEPTH * 20, 1)
        b_gates = sb("b_gates", 4, H)
        m0 = sb("m0", 2, H)
        m_new = sb("m_new", 2, H)
        dt_bias = sb("dt_bias", 1, 64)
        a_log = sb("a_log", 1, 64)
        a_neg = sb("a_neg", 1, 64)
        d_skip = sb("d_skip", KE)
        rank = sb("rank", 4)
        nrow = sb("nrow", P, 32)
        sm = sb("sm", 308)
        nT = sm[:, 128:160].rearrange("p (d h j) -> p d h j", d=2, h=H)
        c_wi = sm[:, 160:176].rearrange("p (t d h) -> p t d h", t=2, d=2)
        c_nM = sm[:, 176:200].rearrange("p (t d h) -> p t d h", t=NT, d=2)
        c_fl = sm[:, 200:224].rearrange("p (t d h) -> p t d h", t=NT, d=2)
        c_wk = sm[:, 224:232]
        den, rden, qn = sm[:, 232:238], sm[:, 238:244], sm[:, 244:248]
        cwt = v3(sm[:, 248:264], H)
        cw = lambda h, t, d: cwt[:, h, 2 * t + d:2 * t + d + 1]
        bst = sm[:, 264:270]
        h_mv = v3(sm[:, 270:294], NT * H)
        h_rs = sm[:, 294:306]
        acs_end = sm[0:64, 306:307]

        arena = sb("arena", ARENA)
        at = [0]

        def region(cols, start=None):
            if start is not None:
                at[0] = start
            a = at[0]
            at[0] += cols
            assert at[0] <= ARENA, at[0]
            return arena[:, a:a + cols], a

        a_xc, _ = region(KE * T, 0)
        a_xc = v3(a_xc, KE)
        xu_r, xu_at = region(KE * W_PAD)
        a_xu = v3(xu_r, KE)
        q_r, _ = region(KE * T)
        a_qT = v3(q_r, KE)
        a_sz = v3(q_r, KE)
        k_r, _ = region(KE * T)
        a_kT = v3(k_r, KE)
        v_r, _ = region(NT * E2)
        a_v = v3(v_r, NT)
        scan_at = at[0]
        e_r, _ = region(2 * 2 * 5 * P)
        a_E = v4(e_r, 2, 2)
        a_pT, _ = region(5 * P)
        a_tmp = v3(region(2 * 512)[0], 2)
        a_kw = v3(region(2 * 512)[0], 2)
        a_cst = v3(region(2 * 512)[0], 2)
        a_cbuf = v3(region(2 * (W_PAD - 2 * PAD), scan_at)[0], 2)
        a_vb = v3(region(2 * T)[0], 2)
        a_bd = region(2 * 3 * P)[0].rearrange("p (s q b c) -> p s q b c", s=2, q=3, c=4)
        a_wq = region(3 * KE * 4)[0].rearrange("p (q k c) -> p q k c", q=3, k=KE)
        a_h = v3(region(NT * E2, xu_at)[0], NT)
        a_rowG = v3(region(4 * T, xu_at)[0][0:H, :], 4)
        a_u = v3(region(2 * T)[0][0:H, :], 2)
        a_lf = v3(region(2 * T)[0][0:H, :], 2)
        a_b = v3(region(2 * T)[0][0:H, :], 2)
        a_nM = v3(region(2 * T)[0][0:H, :], 2)
        a_wi = v3(region(2 * T)[0][0:H, :], 2)
        a_fl = v3(region(2 * T)[0][0:H, :], 2)
        a_a = v3(gates_w[0:H, :], 2)
        a_gtok = v3(sm[:, 0:48], NT)
        a_col = sm[:, 48:48 + 80]
        prow = v3(region(5 * P, scan_at)[0], 5)
        x_tok = v3(region(NT * D, 0)[0], NT)

        b_xs = v3(region(KE * T, 0)[0], KE)
        b_bc = v3(region(2 * G * T)[0], 2 * G)
        bx_r, _ = region(NT * E2)
        b_x = v3(bx_r, NT)
        b_sq = v3(bx_r, KE)
        y_r, y_at = region(NT * E2)
        b_y = v3(y_r, NT)
        b_h0 = v3(region(2 * E2)[0], 2)
        z_r, z_at = region(KE * T)
        b_z = v3(z_r, KE)
        b_acs = region(T)[0][0:64, :]
        b_col = region(9 * 64)[0]
        b_E = v4(region(4 * 512)[0], 2, 2)
        b_cb = v3(region(2 * 5 * P)[0], 2)
        b_t = v3(region(2 * 512)[0], 2)
        b_t2 = b_E[:, 0]
        b_pre = v3(region(4 * W_PAD, y_at)[0], 4)
        b_cbuf = v3(region(2 * (W_PAD - 2 * PAD))[0], 2)
        b_dt, b_u, b_l, b_eq, b_es = (region(T)[0][0:64, :] for _ in range(5))
        b_Bt = v3(region(G * P)[0], G)
        b_wx = v3(region(2 * E2 // G, y_at)[0], 2)
        b_st = v3(region(2 * 512)[0], 2)

        m_acc = v3(region(KD * T, 0)[0], KD)
        m_cbc = v3(region(NEXP * T)[0], NEXP)
        m_cT = region(T)[0][0:NEXP, :]
        m_sg = v3(region(2 * T)[0], 2)
        m_a = v3(region(2 * T)[0], 2)
        m_L = v3(region(NT * 20)[0], NT)
        m_c = v3(region(NT * 16)[0], NT)
        r_mx, r_mp, r_m1, r_m2, r_gs, r_w1, r_w2, r_e2 = (region(NT)[0] for _ in range(8))
        r_eg, r_ohg, r_t4, r_sel, r_oh1, r_oh2 = (v3(region(NT * 4)[0], NT) for _ in range(6))
        r_t16 = v4(region(NT * 16)[0], NT, NG)
        l_t = v3(region(2 * T, 30000)[0], 2)
        l_v = region(T)[0]
        l_rs = region(T)[0]
        y_out = v3(region(2 * 512)[0], 2)

        ada_b = lambda l, j: par[:, 0, 48 * l + j:48 * l + j + 1]
        a_cw = lambda j, c: par[:, 1, 16 * j + c:16 * j + c + 1]
        a_cb = lambda c: par[:, 1, 80 + c:81 + c]
        a_nw = lambda c: par[:, 1, 96 + c:97 + c]
        a_sk = lambda c: par[:, 1, 112 + c:113 + c]
        ln_w = lambda l, i, k: par[:, 2, 16 * l + 8 * i + k:16 * l + 8 * i + k + 1]
        ln_b = lambda l, i, k: par[:, 2, 32 + 16 * l + 8 * i + k:33 + 16 * l + 8 * i + k]
        b_cbias = lambda c: par[:, 2, 64 + c:65 + c]
        b_nw = lambda c: par[:, 2, 88 + c:89 + c]
        b_cw = lambda j, c: par[:, 3, 24 * j + c:24 * j + c + 1]
        n0T = par[:, 4, 0:32]
        PROWS = (112, 128, 104, 120, 32)

        slabs = []
        ada_w, a_in, a_dn, b_in, b_dn = i_["ada_w"], i_["a_w_in"], i_["a_w_down"], i_["b_w_in"], i_["b_w_out"]

        def kslab(w, c0, k0=0, n=256):
            return w[k0 * P:(k0 + KD) * P, c0:c0 + n].rearrange("(k p) c -> p k c", p=P)

        ada_at = [0]

        def add_ada(n):
            for _ in range(n):
                l, s = divmod(ada_at[0], 24)
                slabs.append(("ada", kslab(ada_w[l], 256 * s)))
                ada_at[0] += 1

        add_ada(8)
        for s in range(8):
            slabs.append(("xu", kslab(a_in[0], 256 * s)))
            add_ada(2)
        for h in range(H):
            for d in range(2):
                slabs.append(("C0", i_["state_mlstm_C"][0, 0, d, h].rearrange("(k p) c -> p k c", p=P)))
        for s in range(8):
            slabs.append(("z", kslab(a_in[0], E2 + 256 * s)))
            add_ada(2)
        for s in range(4):
            for k in range(2):
                slabs.append(("down", kslab(a_dn[0], 256 * s, 8 * k)))
                add_ada(1)
        slabs.append(("pad", None))
        while len(slabs) % RING:
            slabs.append(("pad", None))
        moe_at = [len(slabs)]
        for _ in range(3 * NEXP):
            slabs.append(("moe", None))
        slabs.append(("dt", kslab(b_in[0], 5120, 0, 64)))
        for s in list(range(8, 12)):
            slabs.append(("bc", kslab(b_in[0], E2 + 256 * s)))
        for s in range(8):
            slabs.append(("x", kslab(b_in[0], E2 + 256 * s)))
        for d in range(2):
            slabs.append(("h0", i_["state_ssd"][0, 0, d].rearrange("(k j) p n -> (j p) k n", j=2)))
        for s in range(8):
            slabs.append(("zb", kslab(b_in[0], 256 * s)))
        for s in range(4):
            for k in range(2):
                slabs.append(("out", kslab(b_dn[0], 256 * s, 8 * k)))
        while len(slabs) % RING:
            slabs.append(("pad", None))
        moe_at.append(len(slabs))
        for _ in range(3 * NEXP):
            slabs.append(("moe", None))

        def slot(n):
            return ring[:, (n % RING) * SLAB:(n % RING + 1) * SLAB]

        slab_in = [sem(f"slab_in{s}") for s in range(RING)]
        landed, per_slot = [], [0] * RING
        for n, (kind, _) in enumerate(slabs):
            if kind != "pad":
                per_slot[n % RING] += 16
            landed.append(per_slot[n % RING])
        slab_free = {}

        filled = sem("filled")
        n_filled = [0]
        group = {}
        stage_n = {}
        occupant = [None] * 8
        next_bank = [0]

        def read(stage):
            return sem(stage + "_read")

        def claim(pe, stage, bank=None, reads=1):
            k = stage_n.get(stage, 0)
            stage_n[stage] = k + 1
            if bank is None:
                bank = next_bank[0] % 6
                next_bank[0] += 1
            if occupant[bank]:
                pe.wait_ge(*occupant[bank])
            occupant[bank] = (read(stage), reads * (k + 1))
            return (stage, k, bank), banks[bank]

        def finish(ins, key=None):
            n_filled[0] += 1
            ins.then_inc(filled, 1)
            if key:
                group[key[:2]] = (key[2], n_filled[0])

        def await_bank(eng, stage, k):
            b, n = group[stage, k]
            eng.wait_ge(filled, n)
            return banks[b]

        block = ctx.enter_context(nc.Block())
        mm = nc.tensor.matmul

        @block.tensor
        def _(pe):
            n_slab = [0]

            def slab(kind):
                n = n_slab[0]
                while slabs[n][0] == "pad":
                    n += 1
                assert slabs[n][0] == kind, (n, slabs[n][0], kind)
                n_slab[0] = n + 1
                pe.wait_ge(slab_in[n % RING], landed[n])
                return n, slot(n)

            def used(n):
                slab_free[n] = n_filled[0]

            ada_n = [0]
            ada_key = [None]

            def ada_slab():
                l, s = divmod(ada_n[0], 24)
                if ada_n[0] in (0, 8, 24):
                    ada_key[0] = claim(pe, "ada", bank=7)[0]
                ada_n[0] += 1
                n, w = slab("ada")
                w = v3(w, KD)
                for j in (0, 1):
                    c = 2 * (2 * s + j)
                    for k in range(KD):
                        last = mm(banks[7][:, c:c + 2], w[:, k, P * j:P * j + P], csil[:, k:2 * KD:KD],
                                  start=k == 0, stop=k == KD - 1)
                finish(last, ada_key[0] if ada_n[0] in (8, 24, 48) else None)
                used(n)

            def project(stage, kind, ready):
                n, w = slab(kind)
                w = v3(w, KD)
                for j in (0, 1):
                    key, ps = claim(pe, stage)
                    for k in range(KD):
                        ready(k)
                        last = mm(ps[:, 0:T], w[:, k, P * j:P * j + P], hT[:, k, :], start=k == 0, stop=k == KD - 1)
                    finish(last, key)
                used(n)

            def project_back(stage, kind, src, ready):
                for s in range(4):
                    keys = [claim(pe, stage) for _ in range(2)]
                    for half in (0, 1):
                        n, w = slab(kind)
                        w = v3(w, KD)
                        for j in (0, 1):
                            for k in range(KD):
                                ready(8 * half + k)
                                last = mm(keys[j][1][:, 0:T], w[:, k, P * j:P * j + P], src[:, 8 * half + k, :],
                                          start=half == 0 and k == 0, stop=half == 1 and k == KD - 1,
                                          skip_group_check=True)
                            finish(last, keys[j][0] if half else None)
                        used(n)
                        if kind == "down":
                            ada_slab()

            def layer_norm(L):
                key, ps = claim(pe, "mean" + L, reads=KD)
                for k in range(KD):
                    pe.wait_ge(sem("r_ready" + L), k + 1)
                    last = mm(ps[:, 0:T], ones_d[:, :], xT[:, k, :], start=k == 0, stop=k == KD - 1)
                finish(last, key)
                key, ps = claim(pe, "var" + L)
                for k in range(KD):
                    pe.wait_ge(sem("sq_ready" + L), k + 1)
                    last = mm(ps[:, 0:T], ones_d[:, :], hT[:, k, :], start=k == 0, stop=k == KD - 1)
                finish(last, key)

            def moe(l):
                L = f"_{l}"
                key, ps = claim(pe, "route" + L)
                for t in range(NT):
                    for k in range(KD):
                        if t == 0:
                            pe.wait_ge(sem("h_ready"), 8 * (2 * l + 1) + k + 1)
                        mm(ps[:, 20 * t:20 * t + 20], hT[:, k, P * t:P * t + P], route_w[:, l, k, :],
                           start=k == 0, stop=False)
                    last = mm(ps[:, 20 * t:20 * t + 20], ones[0:1, :], route_b[0:1, 20 * l:20 * l + 20],
                              start=False, stop=True)
                finish(last, key)
                pe.wait_ge(sem("comb_ready"), l + 1)
                key, ps = claim(pe, "combT" + L)
                for t in range(NT):
                    last = nc.tensor.transpose(ps[0:NEXP, P * t:P * t + P], m_c[:, t, :], ident[:, :])
                finish(last, key)
                pe.wait_ge(read("combT" + L), 1)
                for e in range(NEXP):
                    key, ps = claim(pe, "combB" + L)
                    finish(mm(ps[:, 0:T], ident[0:NEXP, e:e + 1].to_broadcast([NEXP, P]), m_cT,
                              start=True, stop=True), key)
                for b in range(8):
                    if occupant[b]:
                        pe.wait_ge(*occupant[b])
                        occupant[b] = None
                base, n0 = n_filled[0], moe_at[l]
                group["moe" + L] = base
                in0 = [landed[n0 + s] for s in range(3)]
                wg, wu, wd = (slot(n0 + s) for s in range(3))

                def expert(e, first):
                    for s, w in ((0, wg), (1, wu)):
                        pe.wait_ge(slab_in[s], e * 16 + in0[s])
                        if not first:
                            pe.wait_ge(sem(("gate", "up")[s] + L + "_read"), e * 2)
                        for j in (0, 1):
                            for k in range(KD):
                                last = mm(banks[2 * s + j][:, 0:T], v3(w, KD)[:, k, P * j:P * j + P], hT[:, k, :],
                                          start=k == 0, stop=k == KD - 1)
                            last.then_inc(filled, 1)
                    pe.wait_ge(slab_in[2], e * 16 + in0[2])
                    pe.wait_ge(sem("up" + L + "_read"), e * 2 + 2)
                    for m in range(KD):
                        if not first or m >= 4:
                            pe.wait_ge(sem("dn" + L + "_read"), e * 8 + (0 if m < 4 else m - 3))
                        for f in (0, 1):
                            last = mm(banks[4 + m % 4][:, 0:T], v3(wd, 2)[:, f, P * m:P * m + P], m_a[:, f, :],
                                      start=f == 0, stop=f == 1)
                        last.then_inc(filled, 1)

                expert(0, True)
                with pe.Fori(1, NEXP) as e:
                    expert(e, False)
                n_filled[0] += 12 * NEXP
                occupant[0] = occupant[1] = (sem("gate" + L + "_read"), 2 * NEXP)
                occupant[2] = occupant[3] = (sem("up" + L + "_read"), 2 * NEXP)
                for b in range(4, 8):
                    occupant[b] = (sem("dn" + L + "_read"), 8 * NEXP)
                n_slab[0] = n0 + 3 * NEXP
                for s in range(3):
                    slab_free[n0 + 3 * NEXP - 3 + s] = n_filled[0] - (10, 8, 0)[s]

            pe.wait_ge(sem("consts"), 1)
            pe.wait_ge(sem("prow_in"), 16 * 13)
            for i in range(5):
                key, ps = claim(pe, "par")
                finish(nc.tensor.transpose(ps[:, 0:PROWS[i]], prow[0:PROWS[i], i, :],
                                           ident[0:PROWS[i], 0:PROWS[i]]), key)
            pe.wait_ge(sem("x_in"), 32)
            for k in range(KD):
                key, ps = claim(pe, "xT")
                for t in range(NT):
                    last = nc.tensor.transpose(ps[:, P * t:P * t + P], x_tok[:, t, P * k:P * k + P], ident[:, :])
                finish(last, key)

            pe.wait_ge(sem("csil_ready"), 1)
            for _ in range(8):
                ada_slab()
            for s in range(8):
                project("xu", "xu", lambda k: pe.wait_ge(sem("h_ready"), k + 1) if s == 0 else None)
                ada_slab()
                ada_slab()

            gkey, gps = claim(pe, "gates", bank=6)

            def gates(c):
                pe.wait_ge(read("qT"), c + 1)
                pe.wait_ge(read("kT"), c + 1)
                pe.wait_ge(read("vT"), c + 1)
                if c == 0:
                    pe.wait_ge(sem("small_in"), SMALL)
                for t in range(NT):
                    for i, src in enumerate((a_qT[:, c, :], a_kT[:, c, :], a_vb[:, c % 2, :])):
                        last = mm(gps[:, 16 * t:16 * t + 16], src[:, P * t:P * t + P],
                                  gates_w[:, (KE * i + c) * 16:(KE * i + c + 1) * 16],
                                  start=c == 0 and i == 0 and t == 0, stop=c == KE - 1 and i == 2,
                                  skip_group_check=True)
                if c == KE - 1:
                    finish(last, gkey)
                key, ps = claim(pe, "v")
                for t in range(NT):
                    last = nc.tensor.transpose(ps[:, P * t:P * t + P], a_vb[:, c % 2, P * t:P * t + P], ident[:, :])
                finish(last, key)

            for c in range(KE):
                pe.wait_ge(sem("bd_ready"), c + 1)
                pe.wait_ge(sem("xc_ready"), c + 1)
                for i, st in enumerate(("qT", "kT", "vT")):
                    key, ps = claim(pe, st)
                    if i < 2:
                        rhs = a_xc[:, c, :]
                        last = mm(ps[:, 0:T], a_bd[:, c % 2, i].rearrange("p b c -> p (b c)"), rhs,
                                  start=True, stop=True)
                    else:
                        for (t0, t1), o in zip(STREAMS, (PAD, TP + 3 * PAD)):
                            last = mm(ps[:, t0:t1], a_bd[:, c % 2, i].rearrange("p b c -> p (b c)"),
                                      a_xu[:, c, o:o + t1 - t0], start=True, stop=True)
                    finish(last, key)
                if c:
                    gates(c - 1)
            gates(KE - 1)

            pe.wait_ge(read("gates"), 1)
            for kind in range(4):
                key, ps = claim(pe, "grow")
                for t in range(NT):
                    last = nc.tensor.transpose(ps[0:H, P * t:P * t + P], a_gtok[:, t, 4 * kind:4 * kind + 4],
                                               ident[:, :])
                finish(last, key)
            pe.wait_ge(sem("rows_ready"), 1)
            key, ps = claim(pe, "col")
            for q, src in enumerate((a_nM, a_wi, a_fl)):
                for t in range(NT):
                    for d in range(2):
                        o = ((q * NT + t) * 2 + d) * 4
                        nc.tensor.transpose(ps[:, o:o + 4], src[:, d, P * t:P * t + P], ident[0:H, 0:H])
            for d in range(2):
                last = nc.tensor.transpose(ps[:, 72 + 4 * d:76 + 4 * d], a_u[:, d, 0:P], ident[0:H, 0:H])
            finish(last, key)

            def scores(h):
                for d in range(2):
                    key, ps = claim(pe, "abc")
                    finish(mm(ps[:, 0:T], ident[0:H, h:h + 1].to_broadcast([H, P]), a_a[:, d, :],
                              start=True, stop=True), key)
                key, ps = claim(pe, "scP")
                for j in range(KH):
                    last = mm(ps[:, 0:TP], a_qT[:, KH * h + j, 0:TP], a_kT[:, KH * h + j, 0:TP],
                              start=j == 0, stop=j == KH - 1)
                finish(last, key)
                key, ps = claim(pe, "scS")
                for t in (1, 2):
                    for j in range(KH):
                        last = mm(ps[:, TS * (t - 1):TS * t], a_qT[:, KH * h + j, P * t:P * t + P],
                                  a_kT[:, KH * h + j, TP:T], start=j == 0, stop=j == KH - 1)
                finish(last, key)
                key, ps = claim(pe, "qn")
                for t in (1, 2):
                    for j in range(KH):
                        last = mm(ps[:, 2 * t - 2:2 * t], a_qT[:, KH * h + j, P * t:P * t + P],
                                  n0T[:, KH * h + j:32:16], start=j == 0, stop=j == KH - 1)
                finish(last, key)

            scores(0)
            for h in range(H):
                if h + 1 < H:
                    scores(h + 1)
                for d in range(2):
                    n, w = slab("C0")
                    w = v3(w, KH)
                    for t in (1, 2):
                        key, ps = claim(pe, f"qc{d}")
                        for j in range(KH):
                            last = mm(ps[:, :], a_qT[:, KH * h + j, P * t:P * t + P], w[:, j, :],
                                      start=j == 0, stop=j == KH - 1)
                        finish(last, key)
                    used(n)
                pe.wait_ge(sem("p_ready"), h + 1)
                key, ps = claim(pe, "pTS")
                for t in range(2):
                    for r in range(2):
                        o = P * (2 * t + r)
                        last = nc.tensor.transpose(ps[:, o:o + P], a_E[:, h % 2, 0, P + TS * t + P * r:2 * P + TS * t + P * r],
                                                   ident[:, :])
                finish(last, key)
                key, ps = claim(pe, "pTP")
                finish(nc.tensor.transpose(ps[:, 0:P], a_E[:, h % 2, 0, 0:P], ident[:, :]), key)
                key, ps = claim(pe, "kt", reads=2)
                for j in range(KH):
                    last = nc.tensor.transpose(ps[:, P * j:P * j + P], a_kT[:, KH * h + j, 0:TP], ident[:, :])
                finish(last, key)
                pe.wait_ge(read("pTS"), h + 1)
                pe.wait_ge(read("pTP"), h + 1)
                for t in range(NT):
                    key, ps = claim(pe, "pv")
                    rs = (0,) if t == 0 else (0, 1)
                    for r in rs:
                        lhs = a_pT[:, 4 * P:5 * P] if t == 0 else a_pT[:, P * (2 * t - 2 + r):P * (2 * t - 1 + r)]
                        last = mm(ps[:, :], lhs, a_v[:, 0 if t == 0 else 1 + r, DH * h:DH * h + DH],
                                  start=r == 0, stop=r == rs[-1])
                    finish(last, key)
                pe.wait_ge(read("kt"), 2 * h + 2)
                for d in range(2):
                    for j in range(KH):
                        key, ps = claim(pe, "cn")
                        finish(mm(ps[:, :], a_kw[:, d, P * j:P * j + P], a_v[:, 0, DH * h:DH * h + DH],
                                  start=True, stop=True), key)
                key, ps = claim(pe, "nn")
                for d in range(2):
                    for j in range(KH):
                        last = mm(ps[:, KH * d + j:KH * d + j + 1], a_kw[:, d, P * j:P * j + P], ones[:, 0:1],
                                  start=True, stop=True)
                finish(last, key)
            pe.wait_ge(read("nn"), H)
            key, ps = claim(pe, "nrow")
            finish(nc.tensor.transpose(ps[0:32, 0:P], sm[:, 128:160], ident[:, :]), key)

            for s in range(8):
                project("z", "z", lambda k: None)
                ada_slab()
                ada_slab()
            for c in range(KE):
                key, ps = claim(pe, "hn")
                pe.wait_ge(sem("hn_ready"), NT * (c // KH + 1))
                for t in range(NT):
                    last = nc.tensor.transpose(ps[:, P * t:P * t + P], a_h[:, t, P * c:P * c + P], ident[:, :])
                finish(last, key)
            project_back("yA", "down", a_xc, lambda k: pe.wait_ge(sem("gA_ready"), k + 1))
            layer_norm("00")
            moe(0)
            layer_norm("01")

            n, w = slab("dt")
            w = v3(w[:, 0:KD * 64], KD)
            key, ps = claim(pe, "dt")
            for k in range(KD):
                pe.wait_ge(sem("h_ready"), 16 + k + 1)
                last = mm(ps[0:64, 0:T], w[:, k, :], hT[:, k, :], start=k == 0, stop=k == KD - 1)
            finish(last, key)
            used(n)
            for s in range(4):
                project("xbc", "bc", lambda k: None)
            for s in range(8):
                project("xbc", "x", lambda k: None)
            pe.wait_ge(sem("brows_ready"), 1)
            key, ps = claim(pe, "bcol0")
            for t in range(NT):
                nc.tensor.transpose(ps[:, 64 * t:64 * t + 64], b_acs[:, P * t:P * t + P], ident[0:64, 0:64])
                last = nc.tensor.transpose(ps[:, 192 + 64 * t:256 + 64 * t], b_dt[:, P * t:P * t + P],
                                           ident[0:64, 0:64])
            finish(last, key)
            key, ps = claim(pe, "bcol1")
            for t in range(NT):
                last = nc.tensor.transpose(ps[:, 64 * t:64 * t + 64], b_es[:, P * t:P * t + P], ident[0:64, 0:64])
            finish(last, key)
            for d in range(2):
                n, w = slab("h0")
                for c4 in range(4):
                    key, ps = claim(pe, "h0")
                    for i in range(4):
                        c = 4 * c4 + i
                        last = nc.tensor.transpose(ps[:, P * i:P * i + P], w[:, P * c:P * c + P], ident[:, :])
                    finish(last, key)
                used(n)
            pe.wait_ge(sem("xs_ready"), 8)
            key, ps = claim(pe, "Bt")
            for g in range(G):
                last = nc.tensor.transpose(ps[:, P * g:P * g + P], b_bc[:, g, 0:TP], ident[:, :])
            finish(last, key)
            for c in range(KE):
                pe.wait_ge(sem("xs_ready"), 8 + c + 1)
                key, ps = claim(pe, "xt")
                for t in range(NT):
                    last = nc.tensor.transpose(ps[:, P * t:P * t + P], b_xs[:, c, P * t:P * t + P], ident[:, :])
                finish(last, key)
            pe.wait_ge(read("Bt"), 1)
            for g in range(G):
                for d in range(2):
                    pe.wait_ge(sem("wx_ready"), 2 * g + d + 1)
                    key, ps = claim(pe, "sn")
                    for i in range(4):
                        last = mm(ps[:, P * i:P * i + P], b_wx[:, d, P * i:P * i + P], b_Bt[:, g, :],
                                  start=True, stop=True)
                    finish(last, key)
            for g in range(G):
                key, ps = claim(pe, "cbP", bank=4)
                finish(mm(ps[:, 0:TP], b_bc[:, g, 0:TP], b_bc[:, G + g, 0:TP], start=True, stop=True), key)
                key, ps = claim(pe, "cbS", bank=3)
                for r in range(2):
                    last = mm(ps[:, TS * r:TS * r + TS], b_bc[:, g, TP + P * r:TP + P * r + P], b_bc[:, G + g, TP:T],
                              start=True, stop=True)
                finish(last, key)
                ykeys = [claim(pe, f"y{t}", bank=5 + t) for t in range(NT)]

                def broadcast(u):
                    d, hh = u % 2, u // 2
                    key, ps = claim(pe, "acsb", bank=u % 4)
                    row = 32 * d + HG * g + hh
                    finish(mm(ps[:, 0:T], ident[0:64, row:row + 1].to_broadcast([64, P]), b_acs,
                              start=True, stop=True), key)

                broadcast(0)
                broadcast(1)
                for hh in range(HG):
                    if hh + 1 < HG:
                        broadcast(2 * hh + 2)
                        broadcast(2 * hh + 3)
                    pe.wait_ge(sem("w_ready"), 2 * (HG * g + hh) + 2)
                    Ef, Eb = b_E[:, hh % 2, 0, :], b_E[:, hh % 2, 1, :]
                    xh = lambda t: b_x[:, t, 512 * g + PH * hh:512 * g + PH * hh + PH]
                    for t, parts in ((0, ((Ef, 0, 0), (Eb, 0, 0))),
                                     (1, ((Ef, 128, 1), (Eb, 128, 1), (Eb, 256, 2))),
                                     (2, ((Ef, 256, 1), (Ef, 384, 2), (Eb, 384, 2)))):
                        for i, (E, o, r) in enumerate(parts):
                            last = mm(ykeys[t][1][:, PH * hh:PH * hh + PH], E[:, o:o + P], xh(r),
                                      start=i == 0, stop=i == len(parts) - 1)
                        finish(last, ykeys[t][0] if hh == HG - 1 else None)
                    group["w_used", HG * g + hh] = n_filled[0]
                for d in range(2):
                    for t in (1, 2):
                        key, ps = claim(pe, "inter", bank=2 * (d) + (t - 1))
                        finish(mm(ps[:, :], b_bc[:, G + g, P * t:P * t + P], b_h0[:, d, 512 * g:512 * g + 512],
                                  start=True, stop=True), key)
            for s in range(8):
                project("zb", "zb", lambda k: None)
            for c in range(KE):
                key, ps = claim(pe, "yT")
                pe.wait_ge(read("y2"), c // 4 + 1)
                for t in range(NT):
                    last = nc.tensor.transpose(ps[:, P * t:P * t + P], b_y[:, t, P * c:P * c + P], ident[:, :])
                finish(last, key)
            key, ps = claim(pe, "msq")
            for c in range(KE):
                pe.wait_ge(sem("gsq_ready"), c + 1)
                last = mm(ps[:, 0:T], ones_d[:, :], b_sq[:, c, :], start=c == 0, stop=c == KE - 1)
            finish(last, key)
            project_back("yB", "out", b_xs, lambda k: pe.wait_ge(sem("gB_ready"), k + 1))
            layer_norm("10")
            moe(1)
            layer_norm("11")
            for t in range(NT):
                for m in range(2):
                    pe.wait_ge(sem("x_final"), KD)
                    key, ps = claim(pe, "out")
                    for i in range(4):
                        last = nc.tensor.transpose(ps[:, P * i:P * i + P], xT[:, 4 * m + i, P * t:P * t + P],
                                                   ident[:, :])
                    finish(last, key)



        @block.sync
        def _(sp):
            sp.dma_start(x_tok[:, 0, :], i_["x_prompt"][0]).then_inc(sem("x_in"), 16)
            sp.dma_start(x_tok[:, 1:3, :], i_["x_sample"][0].rearrange("(t p) c -> p t c", p=P)).then_inc(sem("x_in"), 16)

            def free(n):
                while n >= 0 and slabs[n][0] == "pad":
                    n -= RING
                if n >= 0:
                    sp.wait_ge(filled, slab_free[n])

            n = 0
            while n < len(slabs):
                kind, src = slabs[n]
                if kind == "moe":
                    l = moe_at.index(n)
                    wg = i_["moe_w_gate"][l].rearrange("g e k f -> (g e) k f")
                    wu = i_["moe_w_up"][l].rearrange("g e k f -> (g e) k f")
                    wd = i_["moe_w_down"][l].rearrange("g e f k -> (g e) f k")
                    base = group[f"moe_{l}"]

                    def expert(e, first):
                        for s, w in enumerate((wg, wu, wd)):
                            if first:
                                free(n + s - RING)
                            else:
                                sp.wait_ge(filled, e * 12 + (base + (2, 4, 12)[s] - 12))
                            dst = slot(n + s)
                            src = w[e].rearrange("(k p) f -> p k f", p=P)
                            sp.dma_start(v3(dst, KD if s < 2 else 2), src).then_inc(slab_in[s], 16)

                    expert(0, True)
                    with sp.Fori(1, NEXP) as e:
                        expert(e, False)
                    n += 3 * NEXP
                    continue
                if kind != "pad":
                    free(n - RING)
                    k, c = src.shape[1], src.shape[2]
                    sp.dma_start(v3(slot(n)[:, 0:k * c], k), src).then_inc(slab_in[n % RING], 16)
                n += 1

        @block.gpsimd
        def _(pool):
            pl = nc.gpsimd
            n_link = [0]

            def link(ins):
                n_link[0] += 1
                ins.then_inc(sem("pool_step"), 1)
                pool.wait_ge(sem("pool_step"), n_link[0])

            pl.memset(ones[:, :], 1.0)
            pl.memset(ones_d[:, :], 1.0 / D)
            for j in range(4):
                pl.memset(rank[:, j:j + 1], float(4 - j))
            pl.memset(blockmask[:, :], 1.0)
            pl.memset(strip_f[:, :], 0.0)
            pl.memset(strip_b[:, :], 0.0)
            link(pl.memset(ident[:, :], 0.0))
            pl.affine_select(out=ident[:, :], in_=ident[:, :], compare_op=ALU.not_equal, fill=1.0, base=0,
                             pattern=[[-1, P]], channel_multiplier=1)
            pl.affine_select(out=strip_f[:, :], in_=strip_f[:, :], compare_op=ALU.is_ge, fill=-BIG, base=P,
                             pattern=[[-1, 3 * P]], channel_multiplier=1)
            pl.affine_select(out=strip_b[:, :], in_=strip_b[:, :], compare_op=ALU.is_ge, fill=-BIG, base=-P,
                             pattern=[[1, 3 * P]], channel_multiplier=-1)
            bm = blockmask[:, :].rearrange("p (b c) -> p b c", c=4)
            link(pl.affine_select(out=bm, in_=bm, compare_op=ALU.is_ge, fill=0.0, base=0,
                                  pattern=[[-4, 32], [0, 4]], channel_multiplier=1))
            link(pl.affine_select(out=bm, in_=bm, compare_op=ALU.is_ge, fill=0.0, base=3,
                                  pattern=[[4, 32], [0, 4]], channel_multiplier=-1))
            pl.memset(ones[:, 0:1], 1.0).then_inc(sem("consts"), 1)
            pl.memset(xu_r, 0.0).then_inc(sem("pads"), 1)

            small = []
            for q, name in enumerate(("a_w_q", "a_w_k", "a_w_v")):
                small.append((a_wq[:, q], i_[name][0].rearrange("(k b) c d -> (b c) k d", b=32)))
            small.append((gates_w[:, :].rearrange("p (k c) -> p k c", c=16),
                          i_["a_w_gates"][0].rearrange("(k p) c -> p k c", p=P)))
            small.append((b_gates[:, :], i_["a_b_gates"][0].rearrange("(k h) -> h k", h=H)))
            small.append((m0[:, :], i_["state_mlstm_m"][0, 0].rearrange("d h -> h d")))
            for l in range(DEPTH):
                small.append((route_w[:, l, :, 0:4], i_["moe_w_rg"][l].rearrange("(k p) c -> p k c", p=P)))
                for g in range(NG):
                    small.append((route_w[:, l, :, 4 + 4 * g:8 + 4 * g],
                                  i_["moe_w_re"][l, g].rearrange("(k p) c -> p k c", p=P)))
                small.append((route_b[:, 20 * l:20 * l + 4], i_["moe_b_rg"][l:l + 1]))
                small.append((route_b[:, 20 * l + 4:20 * l + 20],
                              i_["moe_b_re"][l:l + 1].rearrange("l g e -> l (g e)")))
            small.append((dt_bias[:, :], i_["b_dt_bias"][0].rearrange("d (h o) -> (d h) o", o=1)))
            small.append((a_log[:, :], i_["b_a_log"][0].rearrange("d (h o) -> (d h) o", o=1)))
            for j in range(2):
                small.append((d_skip[64 * j:64 * j + 64, :],
                              i_["b_d_skip"][0:1, j::2].to_broadcast([64, KE])))
            assert 16 * len(small) == SMALL
            for dst, src in small:
                pool.dma_start(dst, src, allow_slow_non_contiguous=True).then_inc(sem("small_in"), 16)

            pool.wait_ge(sem("small_in"), SMALL)
            for c in range(KE):
                if c >= 2:
                    pool.wait_ge(filled, group["vT", c - 2][1])
                for q in range(3):
                    ins = pl.tensor_tensor(out=a_bd[:, c % 2, q], in0=a_wq[:, q, c, :].unsqueeze(1).to_broadcast([P, 32, 4]),
                                           in1=bm, op=ALU.mult)
                ins.then_inc(sem("bd_ready"), 1)

            def clear_acc(l):
                pool.wait_ge(sem("h_ready"), 8 * (2 * l + 1) + 1)
                pl.memset(m_acc.rearrange("p k t -> p (k t)"), 0.0).then_inc(sem("acc_clear"), 1)

            clear_acc(0)
            pool.wait_ge(sem("h_ready"), 17)
            pl.memset(b_pre.rearrange("p k t -> p (k t)"), 0.0).then_inc(sem("pads"), 1)
            pool.wait_ge(read("bcol1"), 1)
            for g in range(G):
                pool.wait_ge(read("xt"), 4 * g + 4)
                for d in range(2):
                    if g:
                        pool.wait_ge(filled, group["sn", 2 * (g - 1) + d][1])
                    pl.tensor_tensor(out=b_wx[:, d, :].rearrange("p (h c) -> p h c", h=HG),
                                     in0=b_x[:, 0, 512 * g:512 * g + 512].rearrange("p (h c) -> p h c", h=HG),
                                     in1=b_col[:, 512 + 32 * d + HG * g:512 + 32 * d + HG * g + HG]
                                     .unsqueeze(2).to_broadcast([P, HG, PH]), op=ALU.mult).then_inc(sem("wx_ready"), 1)
            clear_acc(1)

        @block.scalar
        def _(act):
            ac = nc.scalar.activation
            n_link = [0]

            def link(ins):
                n_link[0] += 1
                ins.then_inc(sem("act_step"), 1)
                act.wait_ge(sem("act_step"), n_link[0])

            prows = (
                (0, 0, 96, i_["ada_b"].rearrange("l (j p) -> (l j) p", p=P)),
                (0, 96, 8, i_["c_ctx"].rearrange("(j p) -> j p", p=P)),
                (0, 104, 8, i_["c"].rearrange("o (j p) -> (o j) p", p=P)),
                (1, 0, 80, i_["a_conv_w"][0].rearrange("w (j p) -> (w j) p", p=P)),
                (1, 80, 16, i_["a_conv_b"].rearrange("o (j p) -> (o j) p", p=P)),
                (1, 96, 16, i_["a_norm_w"].rearrange("o (j p) -> (o j) p", p=P)),
                (1, 112, 16, i_["a_skip"].rearrange("o (j p) -> (o j) p", p=P)),
                (2, 0, 32, i_["ln_w"].rearrange("l i (j p) -> (l i j) p", p=P)),
                (2, 32, 32, i_["ln_b"].rearrange("l i (j p) -> (l i j) p", p=P)),
                (2, 64, 24, i_["b_conv_b"].rearrange("o (j p) -> (o j) p", p=P)),
                (2, 88, 16, i_["b_norm_w"].rearrange("o (j p) -> (o j) p", p=P)),
                (3, 0, 120, i_["b_conv_w"][0].rearrange("w (j p) -> (w j) p", p=P)),
                (4, 0, 32, i_["state_mlstm_n"][0, 0].rearrange("d h (j p) -> (d h j) p", p=P)),
            )
            for tile, r0, n, src in prows:
                act.dma_start(prow[r0:r0 + n, tile, :], src).then_inc(sem("prow_in"), 16)

            act.wait_ge(read("par"), 1)
            ac(csil[:, :], par[:, 0, 96:112], ACT.Silu).then_inc(sem("csil_ready"), 1)
            for k in range(KD):
                ps = await_bank(act, "xT", k)
                ac(xT[:, k, :], ps[:, 0:T], ACT.Copy).then_inc(read("xT"), 1)

            def modulate(l, shift, permuted, k):
                for v, (t0, t1) in enumerate(STREAMS):
                    out, src = hT[:, k, t0:t1], xT[:, k, t0:t1]
                    if permuted and v:
                        out = out.rearrange("p (w r) -> p r w", r=ROWS)
                        src = src.rearrange("p (r w) -> p r w", r=ROWS)
                    last = ac(out, src, ACT.Identity, bias=mod[:, l, shift + k, v:v + 1],
                              scale=mod[:, l, shift + 8 + k, v:v + 1])
                last.then_inc(sem("h_ready"), 1)

            act.wait_ge(sem("mod_ready"), 1)
            act.wait_ge(read("xT"), KD)
            for k in range(KD):
                modulate(0, 0, False, k)

            act.wait_ge(sem("pads"), 1)

            def conv_silu(c, cbuf, bias, out, ready):
                act.wait_ge(sem("conv_ready"), c + 1)
                ac(out[:, 0:TP], cbuf[:, 0:TP], ACT.Silu, bias=bias)
                ac(out[:, TP:T], cbuf[:, TP + 2 * PAD:], ACT.Silu, bias=bias).then_inc(sem(ready), 1)

            def padded(dst, ps, stage):
                ac(dst[:, PAD:PAD + TP], ps[:, 0:TP], ACT.Copy)
                ac(dst[:, TP + 3 * PAD:T + 3 * PAD], ps[:, TP:T], ACT.Copy).then_inc(read(stage), 1)

            for c in range(KE):
                padded(a_xu[:, c, :], await_bank(act, "xu", c), "xu")
                if c:
                    conv_silu(c - 1, a_cbuf[:, (c - 1) % 2, :], a_cb(c - 1), a_xc[:, c - 1, :], "xc_ready")
            conv_silu(KE - 1, a_cbuf[:, (KE - 1) % 2, :], a_cb(KE - 1), a_xc[:, KE - 1, :], "xc_ready")

            for c in range(KE):
                ps = await_bank(act, "qT", c)
                ac(a_qT[:, c, :], ps[:, 0:T], ACT.Copy).then_inc(read("qT"), 1)
                ps = await_bank(act, "vT", c)
                if c >= 2:
                    act.wait_ge(filled, group["v", c - 2][1])
                ac(a_vb[:, c % 2, :], ps[:, 0:T], ACT.Copy).then_inc(read("vT"), 1)

            act.wait_ge(sem("gate_x"), 1)
            link(ac(a_u, a_u, ACT.Exp))
            ac(a_u, a_u, ACT.Ln, bias=1.0).then_inc(sem("gate_ln"), 1)
            for c in range(KE):
                ac(a_xc[:, c, :], a_xc[:, c, :], ACT.Copy, scale=a_sk(c)).then_inc(sem("skip_ready"), 1)
            act.wait_ge(sem("gate_m"), 1)
            for d in range(2):
                ac(a_wi[:, d, TP:T], a_nM[:, d, TP:T], ACT.Exp, bias=m0[:, d:d + 1])
                end = TP - 1 if d == 0 else 0
                ac(a_u[:, d, 0:TP], a_a[:, d, 0:TP], ACT.Exp, bias=a_nM[:, d, end:end + 1])
            ac(a_fl, a_fl, ACT.Exp).then_inc(sem("rows_ready"), 1)
            act.dma_start(o_["m"][0, 0].rearrange("d h -> h d"), m_new[:, :], allow_slow_non_contiguous=True).then_inc(sem("out_m"), 16)

            def weights_exp(h):
                for d in range(2):
                    act.wait_ge(read("abc"), 2 * h + d + 1)
                    ac(a_E[:, h % 2, d, :], a_E[:, h % 2, d, :], ACT.Exp).then_inc(sem("e_ready"), 1)

            weights_exp(0)
            for h in range(H):
                if h + 1 < H:
                    weights_exp(h + 1)
                act.wait_ge(sem("cw_ready"), h + 1)
                if h:
                    act.wait_ge(read("pv"), NT * h)
                for t in range(2):
                    ps = await_bank(act, "qc0", 2 * h + t)
                    ac(a_tmp[:, t, :], ps[:, :], ACT.Copy, scale=cw(h, t, 0)).then_inc(read("qc0"), 1)
                if h:
                    act.wait_ge(filled, group["pv", NT * h - 1][1])
                ps = await_bank(act, "pTS", h)
                ac(a_pT[:, 0:4 * P], ps[:, :], ACT.Copy).then_inc(read("pTS"), 1)
                ps = await_bank(act, "pTP", h)
                ac(a_pT[:, 4 * P:5 * P], ps[:, 0:P], ACT.Copy).then_inc(read("pTP"), 1)
                for d in range(2):
                    for j in range(KH):
                        n = (2 * h + d) * KH + j
                        ps = await_bank(act, "cn", n)
                        if n >= 2:
                            act.wait_ge(sem(f"out_c{n % 2}"), 16 * (n // 2))
                        ac(a_cst[:, n % 2, :], ps[:, :], ACT.Copy).then_inc(read("cn"), 1)
                        act.wait_ge(read("cn"), n + 1)
                        act.dma_start(o_["C"][0, 0, d, h, P * j:P * j + P, :], a_cst[:, n % 2, :]).then_inc(sem(f"out_c{n % 2}"), 16)
            act.wait_ge(sem("hvar_ready"), 1)
            ac(h_rs, h_rs, ACT.Sqrt).then_inc(sem("hsqrt"), 1)
            act.wait_ge(read("nrow"), 1)
            act.dma_start(o_["n"][0, 0].rearrange("d h (j p) -> (d h j) p", p=P), nrow[:, :]).then_inc(sem("out_n"), 16)
            for c in range(KE):
                ps = await_bank(act, "z", c)
                ac(a_sz[:, c, :], ps[:, 0:T], ACT.Silu).then_inc(read("z"), 1)

            def layer_norm(L, l, i, after):
                for k in range(KD):
                    act.wait_ge(read("mean" + L), k + 1)
                    ac(hT[:, k, :], xT[:, k, :], ACT.Square).then_inc(sem("sq_ready" + L), 1)
                act.wait_ge(read("var" + L), 1)
                ac(l_rs, l_v, ACT.Sqrt).then_inc(sem("ln_sqrt"), 1)
                for k in range(KD):
                    act.wait_ge(sem("xn_ready" + L), k + 1)
                    ins = ac(xT[:, k, :], xT[:, k, :], ACT.Identity, bias=ln_b(l, i, k))
                    if after is None:
                        ins.then_inc(sem("x_final"), 1)
                    else:
                        link(ins)
                        modulate(*after, k)

            def moe(l):
                L = f"_{l}"
                act.wait_ge(sem("route_a"), 2 * l + 1)
                ac(r_eg, r_eg, ACT.Exp).then_inc(sem("route_b"), 1)
                act.wait_ge(sem("route_a"), 2 * l + 2)
                ac(r_e2, r_e2, ACT.Exp).then_inc(sem("route_b"), 1)
                for e in range(NEXP):
                    ps = await_bank(act, "combB" + L, e)
                    ac(m_cbc[:, e, :], ps[:, 0:T], ACT.Copy).then_inc(read("combB" + L), 1)
                base = group["moe" + L]

                def expert(e, first):
                    for j in (0, 1):
                        act.wait_ge(filled, e * 12 + (base + 1 + j))
                        if j == 0 and not first:
                            act.wait_ge(read("up" + L), e * 2)
                        ac(m_sg[:, j, :], banks[j][:, 0:T], ACT.Silu).then_inc(read("gate" + L), 1)

                expert(0, True)
                with act.Fori(1, NEXP) as e:
                    expert(e, False)

            act.wait_ge(sem("mod_ready"), 2)
            layer_norm("00", 0, 0, (0, 24, False))
            moe(0)
            act.wait_ge(sem("mod_ready"), 3)
            layer_norm("01", 0, 1, (1, 0, True))

            ac(a_neg[:, :], a_log[:, :], ACT.Exp).then_inc(sem("dt_a"), 1)
            act.wait_ge(sem("dt_x"), 1)
            link(ac(b_u, b_u, ACT.Exp))
            ac(b_l, b_u, ACT.Ln, bias=1.0).then_inc(sem("dt_ln"), 1)
            act.wait_ge(sem("pads"), 2)

            def b_silu(c):
                out, w = (b_bc[:, c, :], 16 + c) if c < 8 else (b_xs[:, c - 8, :], c - 8)
                act.wait_ge(sem("bconv_ready"), c + 1)
                cb = b_cbuf[:, c % 2, :]
                ac(out[:, 0:TP], cb[:, 0:TP], ACT.Silu, bias=b_cbias(w))
                ac(out[:, TP:T], cb[:, TP + 2 * PAD:], ACT.Silu, bias=b_cbias(w)).then_inc(sem("xs_ready"), 1)

            for c in range(24):
                ps = await_bank(act, "xbc", c)
                if c >= 4:
                    act.wait_ge(sem("bconv_ready"), c - 3)
                padded(b_pre[:, c % 4, :], ps, "xbc")
                if c:
                    b_silu(c - 1)
            b_silu(23)
            act.wait_ge(sem("acs_ready"), 1)
            ac(b_u[:, 0:TP], b_acs[:, 0:TP], ACT.Exp, bias=acs_end, scale=-1.0).then_inc(sem("wr_exp"), 1)
            ac(b_es[:, TP:T], b_acs[:, TP:T], ACT.Exp).then_inc(sem("es_exp"), 1)
            for c in range(8):
                ps = await_bank(act, "h0", c)
                ac(b_h0[:, c // 4, 512 * (c % 4):512 * (c % 4) + 512], ps[:, :], ACT.Copy).then_inc(read("h0"), 1)
            ps = await_bank(act, "Bt", 0)
            ac(b_Bt.rearrange("p g n -> p (g n)"), ps[:, :], ACT.Copy).then_inc(read("Bt"), 1)
            for c in range(KE):
                ps = await_bank(act, "xt", c)
                ac(b_x[:, :, P * c:P * c + P], v3(ps[:, 0:T], NT), ACT.Copy).then_inc(read("xt"), 1)
            for g in range(G):
                for d in range(2):
                    n = 2 * g + d
                    ps = await_bank(act, "sn", n)
                    if n >= 2:
                        act.wait_ge(sem(f"out_s{n % 2}"), 16 * (n // 2))
                    ac(b_st[:, n % 2, :], ps[:, :], ACT.Copy).then_inc(read("sn"), 1)
                    act.wait_ge(read("sn"), n + 1)
                    act.dma_start(o_["s"][0, 0, d, HG * g:HG * g + HG].rearrange("(k j) p n -> (j p) k n", j=2),
                                  v3(b_st[:, n % 2, :], 4)).then_inc(sem(f"out_s{n % 2}"), 16)
            for g in range(G):
                if g >= 2:
                    act.wait_ge(sem("w_ready"), 2 * HG * (g - 1))
                ps = await_bank(act, "cbP", g)
                ac(b_cb[:, g % 2, 0:P], ps[:, 0:P], ACT.Copy).then_inc(read("cbP"), 1)
                ps = await_bank(act, "cbS", g)
                ac(b_cb[:, g % 2, P:5 * P], ps[:, :], ACT.Copy).then_inc(read("cbS"), 1)
                for u in range(2 * HG):
                    act.wait_ge(read("acsb"), 2 * HG * g + u + 1)
                    e = b_E[:, (u // 2) % 2, u % 2, :]
                    ac(e, e, ACT.Exp).then_inc(sem("be_ready"), 1)
            for c in range(KE):
                ps = await_bank(act, "zb", c)
                ac(b_z[:, c, :], ps[:, 0:T], ACT.Silu).then_inc(read("zb"), 1)
            for c in range(KE):
                act.wait_ge(sem("g_ready"), c + 1)
                ac(b_sq[:, c, :], b_xs[:, c, :], ACT.Square).then_inc(sem("gsq_ready"), 1)
                ac(b_xs[:, c, :], b_xs[:, c, :], ACT.Copy, scale=b_nw(c)).then_inc(sem("gB_ready"), 1)
            act.wait_ge(read("msq"), 1)
            ac(l_rs, l_v, ACT.Sqrt).then_inc(sem("rms_sqrt"), 1)
            layer_norm("10", 1, 0, (1, 24, False))
            moe(1)
            layer_norm("11", 1, 1, None)
            for t in range(NT):
                for m in range(2):
                    n = 2 * t + m
                    ps = await_bank(act, "out", n)
                    if n >= 2:
                        act.wait_ge(sem(f"out_y{n % 2}"), 16 * (n // 2))
                    ac(y_out[:, n % 2, :], ps[:, :], ACT.Copy).then_inc(read("out"), 1)
                    act.wait_ge(read("out"), n + 1)
                    dst = o_["yp"][0] if t == 0 else o_["ys"][0, P * t - P:P * t]
                    act.dma_start(dst[:, 512 * m:512 * m + 512], y_out[:, n % 2, :]).then_inc(sem(f"out_y{n % 2}"), 16)
            act.wait_ge(sem("out_m"), 16)
            act.wait_ge(sem("out_n"), 16)
            for s in range(2):
                act.wait_ge(sem(f"out_c{s}"), 16 * H * KH)
                act.wait_ge(sem(f"out_s{s}"), 16 * G)
                act.wait_ge(sem(f"out_y{s}"), 16 * NT)

        @block.vector
        def _(dve):
            ve = nc.vector
            n_link = [0]

            def step(ins):
                n_link[0] += 1
                ins.then_inc(sem("dve_step"), 1)

            def settle():
                dve.wait_ge(sem("dve_step"), n_link[0])

            def link(ins):
                step(ins)
                settle()

            for i in range(5):
                ps = await_bank(dve, "par", i)
                ve.tensor_copy(par[:, i, 0:PROWS[i]], ps[:, 0:PROWS[i]]).then_inc(read("par"), 1)

            def ada(part, l, j0, j1):
                ps = await_bank(dve, "ada", part)
                bias = par[:, 0, 48 * l + j0:48 * l + j1].unsqueeze(2).to_broadcast([P, j1 - j0, 2])
                ve.tensor_tensor(out=mod[:, l, j0:j1, :], in0=ps[:, 2 * j0:2 * j1].rearrange("p (j v) -> p j v", v=2),
                                 in1=bias, op=ALU.add).then_inc(read("ada"), 1)
                dve.wait_ge(read("ada"), part + 1)
                for s in (8, 32):
                    if j0 <= s < j1:
                        last = ve.tensor_scalar(mod[:, l, s:s + 8, :], mod[:, l, s:s + 8, :], 1.0, None, ALU.add)
                last.then_inc(sem("mod_ready"), 1)

            dve.wait_ge(read("par"), 5)
            ada(0, 0, 0, 16)

            def conv(c, src, dst, w, ready):
                last = ve.tensor_scalar(dst, src[:, 0:W_PAD - 2 * PAD], w(0), None, ALU.mult)
                for j in range(1, TAPS):
                    link(last)
                    last = ve.scalar_tensor_tensor(out=dst, in0=src[:, j:j + W_PAD - 2 * PAD], scalar=w(j), in1=dst,
                                                   op0=ALU.mult, op1=ALU.add)
                last.then_inc(sem(ready), 1)

            for c in range(KE):
                dve.wait_ge(read("xu"), c + 1)
                if c >= 2:
                    dve.wait_ge(sem("xc_ready"), c - 1)
                conv(c, a_xu[:, c, :], a_cbuf[:, c % 2, :], lambda j: a_cw(j, c), "conv_ready")
            ada(1, 0, 16, 48)
            for c in range(KE):
                ps = await_bank(dve, "kT", c)
                ve.tensor_copy(a_kT[:, c, :], ps[:, 0:T]).then_inc(read("kT"), 1)
                ps = await_bank(dve, "v", c)
                ve.tensor_copy(a_v[:, :, P * c:P * c + P], v3(ps[:, 0:T], NT)).then_inc(read("v"), 1)
            ps = await_bank(dve, "gates", 0)
            ve.tensor_copy(sm[:, 0:48], ps[:, 0:48]).then_inc(read("gates"), 1)
            for kind in range(4):
                ps = await_bank(dve, "grow", kind)
                ve.tensor_scalar(a_rowG[:, kind, :], ps[0:H, 0:T], b_gates[:, kind:kind + 1], None,
                                 ALU.add).then_inc(read("grow"), 1)
            dve.wait_ge(read("grow"), 4)
            ig, fg = a_rowG[:, 0:4:2, :], a_rowG[:, 1:4:2, :]
            ve.scalar_tensor_tensor(out=a_u, in0=fg, scalar=-1.0, in1=fg, op0=ALU.mult,
                                    op1=ALU.min).then_inc(sem("gate_x"), 1)
            dve.wait_ge(sem("gate_ln"), 1)
            link(ve.scalar_tensor_tensor(out=a_lf, in0=fg, scalar=0.0, in1=a_u, op0=ALU.min, op1=ALU.subtract))

            def both_ways(f):
                for d in range(2):
                    for v, (t0, t1) in enumerate(STREAMS):
                        view = (lambda ap, t0=t0, t1=t1: ap[:, t0:t1]) if d == 0 else \
                            (lambda ap, t0=t0, t1=t1: ap[:, t0:t1][:, ::-1])
                        step(f(d, v, view, t1 - t0))
                settle()

            both_ways(lambda d, v, view, n: ve.tensor_tensor_scan(
                out=view(a_b[:, d]), data0=ones[0:H, 0:1].to_broadcast([H, n]), data1=view(a_lf[:, d]), initial=0.0,
                op0=ALU.mult, op1=ALU.add))
            link(ve.tensor_tensor(out=a_a, in0=ig, in1=a_b, op=ALU.subtract))
            both_ways(lambda d, v, view, n: ve.tensor_tensor_scan(
                out=view(a_nM[:, d]), data0=view(a_a[:, d]), data1=view(a_a[:, d]),
                initial=m0[:, d:d + 1] if v else 0.0, op0=ALU.max, op1=ALU.max))
            step(ve.memset(a_wi[:, :, 0:TP], 0.0))
            for d in range(2):
                end = TP - 1 if d == 0 else 0
                step(ve.tensor_tensor(out=m_new[:, d:d + 1], in0=a_b[:, d, end:end + 1], in1=a_nM[:, d, end:end + 1],
                                      op=ALU.add))
            link(ve.scalar_tensor_tensor(out=a_fl, in0=a_nM, scalar=-1.0, in1=a_b, op0=ALU.mult, op1=ALU.subtract))
            ve.tensor_scalar(a_nM, a_nM, -1.0, None, ALU.mult).then_inc(sem("gate_m"), 1)

            ps = await_bank(dve, "col", 0)
            link(ve.tensor_scalar(c_wi.rearrange("p t d h -> p (t d h)"), ps[:, 32:48], DH ** -0.5, None, ALU.mult))
            step(ve.tensor_copy(c_nM.rearrange("p t d h -> p (t d h)"), ps[:, 0:24]))
            step(ve.tensor_copy(c_wk, ps[:, 72:80]))
            ve.tensor_copy(c_fl.rearrange("p t d h -> p (t d h)"), ps[:, 48:72]).then_inc(read("col"), 1)
            dve.wait_ge(read("col"), 1)
            settle()

            TILES = ((0, 0, P), (1, P, TS), (2, P + TS, TS))

            def strip(d, t):
                s = (strip_f, strip_b)[d]
                return s[:, P:2 * P] if t == 0 else s[:, P:3 * P] if t == 1 else s[:, 0:2 * P]

            def weights(h):
                E = a_E[:, h % 2]
                if h >= 2:
                    dve.wait_ge(filled, group["pTP", h - 2][1])
                for d in range(2):
                    ps = await_bank(dve, "abc", 2 * h + d)
                    for t, o, n in TILES:
                        src = ps[:, 0:TP] if t == 0 else ps[:, TP:T]
                        ins = ve.scalar_tensor_tensor(out=E[:, d, o:o + n], in0=src, scalar=c_nM[:, t, d, h:h + 1],
                                                      in1=strip(d, t), op0=ALU.add, op1=ALU.min)
                    ins.then_inc(read("abc"), 1)
                for t, o, n in TILES:
                    b = await_bank(dve, "scP" if t == 0 else "scS", h)
                    src = b[:, 0:TP] if t == 0 else b[:, TS * (t - 1):TS * t]
                    for d in range(2):
                        if t == 0:
                            dve.wait_ge(sem("e_ready"), 2 * h + d + 1)
                        ins = ve.scalar_tensor_tensor(out=E[:, d, o:o + n], in0=src, scalar=DH ** -0.5,
                                                      in1=E[:, d, o:o + n], op0=ALU.mult, op1=ALU.mult,
                                                      accum_out=den[:, 2 * t + d:2 * t + d + 1])
                        if d and t == 0:
                            ins.then_inc(read("scP"), 1)
                        elif d and t == 2:
                            ins.then_inc(read("scS"), 1)
                dve.wait_ge(read("scS"), h + 1)
                dve.wait_ge(read("scP"), h + 1)
                ps = await_bank(dve, "qn", h)
                wi = c_wi[:, :, :, h]
                ve.tensor_tensor(out=qn.rearrange("p (t d) -> p t d", d=2), in0=ps[:, 0:4].rearrange("p (t d) -> p t d", d=2),
                                 in1=wi, op=ALU.mult).then_inc(read("qn"), 1)
                dve.wait_ge(read("qn"), h + 1)
                settle()
                link(ve.tensor_tensor(out=den[:, 2:6], in0=den[:, 2:6], in1=qn, op=ALU.add))
                link(ve.scalar_tensor_tensor(out=den[:, :], in0=den[:, :], scalar=-1.0, in1=den[:, :], op0=ALU.mult,
                                             op1=ALU.max))
                link(ve.tensor_tensor(out=den.rearrange("p (t d) -> p t d", d=2),
                                      in0=den.rearrange("p (t d) -> p t d", d=2), in1=c_fl[:, :, :, h], op=ALU.max))
                link(ve.reciprocal(rden, den))
                ve.tensor_tensor(out=cwt[:, h, :].rearrange("p (t d) -> p t d", d=2),
                                 in0=rden[:, 2:6].rearrange("p (t d) -> p t d", d=2), in1=wi,
                                 op=ALU.mult).then_inc(sem("cw_ready"), 1)
                for t, o, n in TILES:
                    ins = ve.tensor_scalar(E[:, 0, o:o + n], E[:, 0, o:o + n], rden[:, 2 * t:2 * t + 1], None, ALU.mult)
                link(ins)
                for t, o, n in TILES:
                    ins = ve.scalar_tensor_tensor(out=E[:, 0, o:o + n], in0=E[:, 1, o:o + n],
                                                  scalar=rden[:, 2 * t + 1:2 * t + 2], in1=E[:, 0, o:o + n],
                                                  op0=ALU.mult, op1=ALU.add)
                ins.then_inc(sem("p_ready"), 1)

            weights(0)
            for h in range(H):
                if h + 1 < H:
                    weights(h + 1)
                dve.wait_ge(sem("cw_ready"), h + 1)
                for t in range(2):
                    dve.wait_ge(read("qc0"), 2 * h + t + 1)
                    ps = await_bank(dve, "qc1", 2 * h + t)
                    ve.scalar_tensor_tensor(out=a_tmp[:, t, :], in0=ps[:, :], scalar=cw(h, t, 1), in1=a_tmp[:, t, :],
                                            op0=ALU.mult, op1=ALU.add).then_inc(read("qc1"), 1)
                ps = await_bank(dve, "kt", h)
                if h:
                    dve.wait_ge(filled, group["nn", h - 1][1])
                for d in range(2):
                    ve.tensor_scalar(a_kw[:, d, :], ps[:, :], c_wk[:, 4 * d + h:4 * d + h + 1], None,
                                     ALU.mult).then_inc(read("kt"), 1)
                for t in range(NT):
                    ps = await_bank(dve, "pv", NT * h + t)
                    out = a_h[:, t, DH * h:DH * h + DH]
                    if t == 0:
                        ve.tensor_copy(out, ps[:, :]).then_inc(read("pv"), 1)
                    else:
                        dve.wait_ge(read("qc1"), 2 * h + t)
                        ve.tensor_tensor(out=out, in0=ps[:, :], in1=a_tmp[:, t - 1, :], op=ALU.add).then_inc(read("pv"), 1)
                for t in range(NT):
                    dve.wait_ge(read("pv"), NT * h + t + 1)
                    link(ve.bn_stats(bst[:, 0:6], a_h[:, t, DH * h:DH * h + DH]))
                    link(ve.bn_aggr(h_mv[:, NT * h + t, :], bst[:, 0:6]))
                ps = await_bank(dve, "nn", h)
                ve.tensor_copy(nT[:, :, h, :], ps[:, 0:8].rearrange("p (d j) -> p d j", d=2)).then_inc(read("nn"), 1)
            ve.tensor_scalar(h_rs, h_mv[:, :, 1], EPS, None, ALU.add).then_inc(sem("hvar_ready"), 1)
            ps = await_bank(dve, "nrow", 0)
            ve.tensor_copy(nrow[:, :], ps[0:32, 0:P]).then_inc(read("nrow"), 1)
            dve.wait_ge(sem("hsqrt"), 1)
            link(ve.reciprocal(h_rs, h_rs))
            for h in range(H):
                for t in range(NT):
                    n = NT * h + t
                    hh = a_h[:, t, DH * h:DH * h + DH]
                    ve.tensor_scalar(hh, hh, h_mv[:, n, 0:1], h_rs[:, n:n + 1], ALU.subtract,
                                     ALU.mult).then_inc(sem("hn_ready"), 1)
            dve.wait_ge(sem("skip_ready"), KE)
            for c in range(KE):
                ps = await_bank(dve, "hn", c)
                xc = a_xc[:, c, :]
                ve.scalar_tensor_tensor(out=xc, in0=ps[:, 0:T], scalar=a_nw(c), in1=xc, op0=ALU.mult,
                                        op1=ALU.add).then_inc(read("hn"), 1)
                dve.wait_ge(read("hn"), c + 1)
                dve.wait_ge(read("z"), c + 1)
                ve.tensor_tensor(out=xc, in0=xc, in1=a_sz[:, c, :], op=ALU.mult).then_inc(sem("gA_ready"), 1)

            def residual(L, l, gate, m, src, stage, buf, permuted=False):
                for v, (t0, t1) in enumerate(STREAMS):
                    out, s = buf[:, t0:t1], src[:, t0:t1]
                    if permuted and v:
                        out = out.rearrange("p (r w) -> p r w", r=ROWS)
                        s = s.rearrange("p (w r) -> p r w", r=ROWS)
                    ins = ve.tensor_scalar(out, s, mod[:, l, gate + m, v:v + 1], None, ALU.mult)
                if stage is None:
                    link(ins)
                else:
                    ins.then_inc(read(stage), 1)
                    dve.wait_ge(read(stage), m + 1)
                ve.scalar_tensor_tensor(out=xT[:, m, :], in0=xT[:, m, :], scalar=ALPHA, in1=buf, op0=ALU.mult,
                                        op1=ALU.add).then_inc(sem("r_ready" + L), 1)

            ln_n = [0]

            def layer_norm(L, l, i):
                ps = await_bank(dve, "mean" + L, 0)
                dve.wait_ge(sem("r_ready" + L), KD)
                for k in range(KD):
                    ve.tensor_tensor(out=xT[:, k, :], in0=xT[:, k, :], in1=ps[:, 0:T],
                                     op=ALU.subtract).then_inc(read("mean" + L), 1)
                ps = await_bank(dve, "var" + L, 0)
                ve.tensor_scalar(l_v, ps[:, 0:T], EPS, None, ALU.add).then_inc(read("var" + L), 1)
                ln_n[0] += 1
                dve.wait_ge(sem("ln_sqrt"), ln_n[0])
                dve.wait_ge(read("mean" + L), KD)
                dve.wait_ge(sem("sq_ready" + L), KD)
                link(ve.reciprocal(l_rs, l_rs))
                for k in range(KD):
                    ve.scalar_tensor_tensor(out=xT[:, k, :], in0=xT[:, k, :], scalar=ln_w(l, i, k), in1=l_rs,
                                            op0=ALU.mult, op1=ALU.mult).then_inc(sem("xn_ready" + L), 1)

            def bc(ap, n):
                return ap.unsqueeze(len(ap.shape)).to_broadcast(list(ap.shape) + [n])

            rk = rank[:, :].unsqueeze(1).to_broadcast([P, NT, 4])

            def first_max(src, mx, out, tmp):
                link(ve.tensor_reduce(mx, src, X, ALU.max))
                link(ve.tensor_tensor(out=tmp, in0=src, in1=bc(mx, 4), op=ALU.is_equal))
                link(ve.tensor_tensor(out=tmp, in0=tmp, in1=rk, op=ALU.mult))
                link(ve.tensor_reduce(r_mp, tmp, X, ALU.max))
                link(ve.tensor_tensor(out=out, in0=tmp, in1=bc(r_mp, 4), op=ALU.is_equal))

            def moe(l):
                L = f"_{l}"
                ps = await_bank(dve, "route" + L, 0)
                ve.tensor_copy(m_L.rearrange("p t c -> p (t c)"), ps[:, 0:60]).then_inc(read("route" + L), 1)
                dve.wait_ge(read("route" + L), 1)
                lg, le = m_L[:, :, 0:4], m_L[:, :, 4:20].rearrange("p t (g e) -> p t g e", g=NG)
                first_max(lg, r_mx, r_ohg, r_t4)
                ve.tensor_tensor(out=r_eg, in0=lg, in1=bc(r_mx, 4), op=ALU.subtract).then_inc(sem("route_a"), 1)
                for t in range(NT):
                    ins = (ve.tensor_tensor(out=r_t16[:, t], in0=le[:, t], in1=bc(r_ohg[:, t], 4), op=ALU.mult))
                link(ins)
                link(ve.tensor_reduce(r_sel, r_t16.rearrange("p t g e -> p t e g"), X, ALU.add))
                first_max(r_sel, r_m1, r_oh1, r_t4)
                link(ve.scalar_tensor_tensor(out=r_sel, in0=r_oh1, scalar=-BIG, in1=r_sel, op0=ALU.mult, op1=ALU.add))
                first_max(r_sel, r_m2, r_oh2, r_t4)
                ve.tensor_tensor(out=r_e2, in0=r_m2, in1=r_m1, op=ALU.subtract).then_inc(sem("route_a"), 1)
                dve.wait_ge(sem("route_b"), 2 * l + 2)
                link(ve.tensor_reduce(r_gs, r_eg, X, ALU.add))
                link(ve.scalar_tensor_tensor(out=r_w1, in0=r_e2, scalar=1.0, in1=r_gs, op0=ALU.add, op1=ALU.mult))
                link(ve.reciprocal(r_w1, r_w1))
                link(ve.tensor_tensor(out=r_w2, in0=r_w1, in1=r_e2, op=ALU.mult))
                step(ve.tensor_tensor(out=r_oh1, in0=r_oh1, in1=bc(r_w1, 4), op=ALU.mult))
                link(ve.tensor_tensor(out=r_oh2, in0=r_oh2, in1=bc(r_w2, 4), op=ALU.mult))
                link(ve.tensor_tensor(out=r_oh1, in0=r_oh1, in1=r_oh2, op=ALU.add))
                for t in range(NT):
                    ins = ve.tensor_tensor(out=m_c[:, t, :].rearrange("p (g e) -> p g e", g=NG), in0=bc(r_ohg[:, t], 4),
                                           in1=r_oh1[:, t].unsqueeze(1).to_broadcast([P, NG, NE]), op=ALU.mult)
                ins.then_inc(sem("comb_ready"), 1)
                ps = await_bank(dve, "combT" + L, 0)
                ve.tensor_copy(m_cT, ps[0:NEXP, 0:T]).then_inc(read("combT" + L), 1)
                dve.wait_ge(read("combB" + L), NEXP)
                dve.wait_ge(sem("acc_clear"), l + 1)
                base = group["moe" + L]
                cflat = m_cbc.rearrange("p e t -> p (e t)")

                def expert(e, first):
                    for j in (0, 1):
                        dve.wait_ge(read("gate" + L), e * 2 + (j + 1))
                        if j == 0:
                            dve.wait_ge(filled, e * 12 + base)
                        ve.tensor_tensor(out=m_sg[:, j, :], in0=m_sg[:, j, :], in1=cflat[:, 0:T] if first else cflat[:, bass.ds(e * T, T)],
                                         op=ALU.mult).then_inc(sem("comb_used" + L), 1)
                        dve.wait_ge(sem("comb_used" + L), e * 2 + (j + 1))
                        dve.wait_ge(filled, e * 12 + (base + 3 + j))
                        ve.tensor_tensor(out=m_a[:, j, :], in0=m_sg[:, j, :], in1=banks[2 + j][:, 0:T],
                                         op=ALU.mult).then_inc(read("up" + L), 1)
                    if not first:
                        dve.wait_ge(read("dn" + L), e * 8)
                    for m in range(KD):
                        dve.wait_ge(filled, e * 12 + (base + 5 + m))
                        ve.tensor_tensor(out=m_acc[:, m, :], in0=m_acc[:, m, :], in1=banks[4 + m % 4][:, 0:T],
                                         op=ALU.add).then_inc(read("dn" + L), 1)

                expert(0, True)
                with dve.Fori(1, NEXP) as e:
                    expert(e, False)
                dve.wait_ge(read("dn" + L), 8 * NEXP)
                for m in range(KD):
                    if m >= 2:
                        dve.wait_ge(sem(f"r_ready{l}1"), m - 1)
                    residual(f"{l}1", l, 40, m, m_acc[:, m, :], None, l_t[:, m % 2, :])

            for m in range(KD):
                if m >= 2:
                    dve.wait_ge(sem("r_ready00"), m - 1)
                residual("00", 0, 16, m, await_bank(dve, "yA", m)[:, 0:T], "yA", l_t[:, m % 2, :])
            ada(2, 1, 0, 48)
            layer_norm("00", 0, 0)
            moe(0)
            layer_norm("01", 0, 1)

            ps = await_bank(dve, "dt", 0)
            ve.tensor_scalar(b_dt, ps[0:64, 0:T], dt_bias[:, :], None, ALU.add).then_inc(read("dt"), 1)
            dve.wait_ge(read("dt"), 1)
            ve.scalar_tensor_tensor(out=b_u, in0=b_dt, scalar=-1.0, in1=b_dt, op0=ALU.mult,
                                    op1=ALU.min).then_inc(sem("dt_x"), 1)
            dve.wait_ge(sem("dt_ln"), 1)
            link(ve.tensor_scalar(b_es, b_u, 1.0, None, ALU.add))
            link(ve.tensor_scalar(b_eq, b_es, 1.0, None, ALU.is_equal))
            step(ve.scalar_tensor_tensor(out=b_es, in0=b_es, scalar=-1.0, in1=b_eq, op0=ALU.add, op1=ALU.add))
            link(ve.tensor_tensor(out=b_l, in0=b_l, in1=b_eq, op=ALU.add))
            link(ve.reciprocal(b_es, b_es))
            link(ve.tensor_tensor(out=b_l, in0=b_l, in1=b_es, op=ALU.mult))
            link(ve.tensor_tensor(out=b_l, in0=b_l, in1=b_u, op=ALU.mult))
            link(ve.scalar_tensor_tensor(out=b_dt, in0=b_dt, scalar=0.0, in1=b_l, op0=ALU.max, op1=ALU.add))
            dve.wait_ge(sem("dt_a"), 1)
            link(ve.tensor_scalar(b_l, b_dt, a_neg[:, :], -1.0, ALU.mult, ALU.mult))
            for d in range(2):
                q = slice(32 * d, 32 * d + 32)
                for t0, t1 in STREAMS:
                    view = (lambda ap: ap[q, t0:t1]) if d == 0 else (lambda ap: ap[q, t0:t1][:, ::-1])
                    step(ve.tensor_tensor_scan(out=view(b_acs), data0=ones[q, 0:1].to_broadcast([32, t1 - t0]),
                                               data1=view(b_l), initial=0.0, op0=ALU.mult, op1=ALU.add))
            settle()
            for d in range(2):
                q = slice(32 * d, 32 * d + 32)
                end = TP - 1 if d == 0 else 0
                ins = ve.tensor_copy(acs_end[q, :], b_acs[q, end:end + 1])
            ins.then_inc(sem("acs_ready"), 1)

            def rows_done():
                dve.wait_ge(sem("wr_exp"), 1)
                dve.wait_ge(sem("es_exp"), 1)
                ve.tensor_tensor(out=b_es[:, 0:TP], in0=b_u[:, 0:TP], in1=b_dt[:, 0:TP],
                                 op=ALU.mult).then_inc(sem("brows_ready"), 1)

            for c in range(24):
                w = 16 + c if c < 8 else c - 8
                dve.wait_ge(read("xbc"), c + 1)
                if c >= 2:
                    dve.wait_ge(sem("xs_ready"), c - 1)
                conv(c, b_pre[:, c % 4, :], b_cbuf[:, c % 2, :], lambda j: b_cw(j, w), "bconv_ready")
            rows_done()
            ps = await_bank(dve, "bcol0", 0)
            step(ve.tensor_scalar(b_col[:, 0:192], ps[:, 0:192], -1.0, None, ALU.mult))
            ve.tensor_copy(b_col[:, 192:384], ps[:, 192:384]).then_inc(read("bcol0"), 1)
            ps = await_bank(dve, "bcol1", 0)
            step(ve.tensor_copy(b_col[:, 512:576], ps[:, 0:64]))
            ve.tensor_copy(b_col[:, 384:512], ps[:, 64:192]).then_inc(read("bcol1"), 1)
            dve.wait_ge(read("bcol0"), 1)
            dve.wait_ge(read("bcol1"), 1)
            settle()
            nacs = lambda t, r: b_col[:, 64 * t + r:64 * t + r + 1]
            dtc = lambda t, r: b_col[:, 192 + 64 * t + r:193 + 64 * t + r]

            for g in range(G):
                dve.wait_ge(read("cbP"), g + 1)
                dve.wait_ge(read("cbS"), g + 1)

                def segments(d):
                    cb = b_cb[:, g % 2, :]
                    if d == 0:
                        return ((0, 0, P, 0, strip_b[:, P:2 * P], cb[:, 0:P]),
                                (1, P, 2 * P, TP, strip_b[:, P:3 * P], cb[:, P:3 * P]),
                                (2, 3 * P, P, 2 * P, strip_b[:, P:2 * P], cb[:, 4 * P:5 * P]))
                    return ((0, 0, P, 0, strip_f[:, P:2 * P], cb[:, 0:P]),
                            (1, P, P, TP, strip_f[:, P:2 * P], cb[:, P:2 * P]),
                            (2, 2 * P, 2 * P, TP, strip_f[:, 0:2 * P], cb[:, 3 * P:5 * P]))

                def args(hh):
                    n = HG * g + hh
                    if n >= 2:
                        dve.wait_ge(filled, group["w_used", n - 2])
                    for d in range(2):
                        r = 32 * d + n
                        ps = await_bank(dve, "acsb", 2 * n + d)
                        for i, (t, o, w, s0, mask, _) in enumerate(segments(d)):
                            ins = ve.scalar_tensor_tensor(out=b_E[:, hh % 2, d, o:o + w], in0=ps[:, s0:s0 + w],
                                                          scalar=nacs(t, r), in1=mask, op0=ALU.add, op1=ALU.min)
                        ins.then_inc(read("acsb"), 1)

                args(0)
                for hh in range(HG):
                    if hh + 1 < HG:
                        args(hh + 1)
                    n = HG * g + hh
                    for d in range(2):
                        r = 32 * d + n
                        dve.wait_ge(sem("be_ready"), 2 * n + d + 1)
                        for i, (t, o, w, _, _, cbs) in enumerate(segments(d)):
                            e = b_E[:, hh % 2, d, o:o + w]
                            ins = ve.scalar_tensor_tensor(out=e, in0=e, scalar=dtc(t, r), in1=cbs, op0=ALU.mult,
                                                          op1=ALU.mult)
                        ins.then_inc(sem("w_ready"), 1)
                ps = await_bank(dve, "y0", g)
                if g == 0:
                    for s in range(2):
                        dve.wait_ge(sem(f"out_s{s}"), 16 * G)
                ve.tensor_copy(b_y[:, 0, 512 * g:512 * g + 512], ps[:, :]).then_inc(read("y0"), 1)
                for d in range(2):
                    for t in (1, 2):
                        n = 4 * g + 2 * d + t - 1
                        ps = await_bank(dve, "inter", n)
                        c0 = 384 + 64 * (t - 1) + 32 * d + HG * g
                        out = b_t[:, t - 1, :] if d == 0 else b_t2[:, t - 1, :]
                        ve.tensor_tensor(out=out.rearrange("p (h c) -> p h c", h=HG),
                                         in0=ps[:, :].rearrange("p (h c) -> p h c", h=HG),
                                         in1=bc(b_col[:, c0:c0 + HG], PH), op=ALU.mult).then_inc(read("inter"), 1)
                dve.wait_ge(read("inter"), 4 * g + 4)
                for t in (1, 2):
                    step(ve.tensor_tensor(out=b_t[:, t - 1, :], in0=b_t[:, t - 1, :], in1=b_t2[:, t - 1, :], op=ALU.add))
                settle()
                for t in (1, 2):
                    ps = await_bank(dve, f"y{t}", g)
                    ve.tensor_tensor(out=b_y[:, t, 512 * g:512 * g + 512], in0=ps[:, :], in1=b_t[:, t - 1, :],
                                     op=ALU.add).then_inc(read(f"y{t}"), 1)
            for c in range(KE):
                ps = await_bank(dve, "yT", c)
                xs = b_xs[:, c, :]
                ve.scalar_tensor_tensor(out=xs, in0=xs, scalar=d_skip[:, c:c + 1], in1=ps[:, 0:T], op0=ALU.mult,
                                        op1=ALU.add).then_inc(read("yT"), 1)
                dve.wait_ge(read("yT"), c + 1)
                dve.wait_ge(read("zb"), c + 1)
                ve.tensor_tensor(out=xs, in0=xs, in1=b_z[:, c, :], op=ALU.mult).then_inc(sem("g_ready"), 1)
            ps = await_bank(dve, "msq", 0)
            ve.tensor_scalar(l_v, ps[:, 0:T], float(D) / E2, EPS, ALU.mult, ALU.add).then_inc(read("msq"), 1)
            dve.wait_ge(sem("rms_sqrt"), 1)
            link(ve.reciprocal(l_rs, l_rs))
            for m in range(KD):
                ps = await_bank(dve, "yB", m)
                if m >= 2:
                    dve.wait_ge(sem("r_ready10"), m - 1)
                ve.tensor_tensor(out=b_t[:, m % 2, 0:T], in0=ps[:, 0:T], in1=l_rs, op=ALU.mult).then_inc(read("yB"), 1)
                dve.wait_ge(read("yB"), m + 1)
                residual("10", 1, 16, m, b_t[:, m % 2, 0:T], None, l_t[:, m % 2, :], permuted=True)
            layer_norm("10", 1, 0)
            moe(1)
            layer_norm("11", 1, 1)


_INS = ["x_prompt", "x_sample", "state_mlstm_C", "state_mlstm_n", "state_mlstm_m", "state_ssd", "c", "c_ctx",
        "ada_w", "ada_b", "ln_w", "ln_b", "a_w_in", "a_conv_w", "a_conv_b", "a_w_q", "a_w_k", "a_w_v", "a_w_gates",
        "a_b_gates", "a_norm_w", "a_skip", "a_w_down", "b_w_in", "b_conv_w", "b_conv_b", "b_dt_bias", "b_a_log",
        "b_d_skip", "b_norm_w", "b_w_out", "moe_w_rg", "moe_b_rg", "moe_w_re", "moe_b_re", "moe_w_gate",
        "moe_w_up", "moe_w_down"]
_OUTS = {"yp": (1, TP, D), "ys": (1, TS, D), "C": (1, 1, 2, H, DH, DH), "n": (1, 1, 2, H, DH), "m": (1, 1, 2, H),
         "s": (1, 1, 2, G * HG, PH, P)}


def kernel(**inputs):
    import numpy as np
    import concourse.bacc as bacc
    from concourse.bass_utils import run_bass_kernel_spmd

    nc = bacc.Bacc("TRN2", target_bir_lowering=False, num_devices=1)
    arrays, ins, outs = {}, {}, {}
    for name in _INS:
        a = np.ascontiguousarray(inputs[name])
        arrays["in_" + name] = a
        ins[name] = nc.dram_tensor("in_" + name, a.shape, mybir.dt.from_np(a.dtype), kind="ExternalInput").ap()
    for name, shape in _OUTS.items():
        outs[name] = nc.dram_tensor("out_" + name, shape, F32, kind="ExternalOutput").ap()
    program(nc, ins, outs)
    r = run_bass_kernel_spmd(nc, [arrays], core_ids=[0]).results[0]
    return tuple(r["out_" + name] for name in _OUTS)
```

```python
from contextlib import ExitStack

import concourse.bass as bass
from concourse import mybir

F32 = mybir.dt.float32
ALU = mybir.AluOpType
ACT = mybir.ActivationFunctionType
X = mybir.AxisListType.X

P = 128
TP, TS = 128, 256
T = TP + TS
NT = T // P
STREAMS = ((0, TP), (TP, T))
D = 1024
KD = D // P
E2 = 2048
KE = E2 // P
DEPTH = 2
ALPHA = (2.0 * DEPTH) ** 0.25
EPS = 1e-5
TAPS = 5
PAD = TAPS // 2
W_PAD = T + 4 * PAD
H = 4
DH = E2 // H
KH = DH // P
G = 4
HG = 8
PH = 64
GRID = 64
ROWS = TS // GRID
NG = 4
NE = 4
FF = 256
NEXP = NG * NE
BIG = 1e30
FF = 256
CH = 128
MAXQ = (2 * T + NG * NE * (CH - 1)) // CH
MAXP = (MAXQ + 1) // 2
MINP = T // CH
RING = 6
ARENA = 37120
SLAB = 1024


def program(nc, i_, o_):
    ctx = ExitStack()
    with ctx:
        def sb(name, cols, parts=P):
            return ctx.enter_context(nc.sbuf_tensor(name, [parts, cols], F32))

        sems = {}

        def sem(name):
            if name not in sems:
                sems[name] = ctx.enter_context(nc.semaphore(name))
            return sems[name]

        banks = [ctx.enter_context(nc.psum_tensor(f"bank{b}", [P, 512], F32)) for b in range(8)]

        OUT_C, OUT_S = H * KH, G
        SMALL = 16 * 24

        def v3(ap, n):
            return ap.rearrange("p (n c) -> p n c", n=n)

        def v4(ap, a, b):
            return ap.rearrange("p (a b c) -> p a b c", a=a, b=b)

        xT = v3(sb("xT", KD * T)[:, :], KD)
        hT = v3(sb("hT", KD * T)[:, :], KD)
        ring = sb("ring", RING * SLAB)
        par = v3(sb("par", 5 * P)[:, :], 5)
        mod = sb("mod", DEPTH * 48 * 2)[:, :].rearrange("p (l j v) -> p l j v", l=DEPTH, v=2)
        csil = sb("csil", 2 * KD + 30)
        pick = sb("pick", 2)
        ident = sb("ident", P)
        ones = sb("ones", P)
        ones_d = sb("ones_d", P)
        strip_f = sb("strip_f", 3 * P)
        strip_b = sb("strip_b", 3 * P)
        gates_w = sb("gates_w", 3 * KE * 16)
        route_w = sb("route_w", DEPTH * KD * 20)[:, :].rearrange("p (l k c) -> p l k c", l=DEPTH, k=KD)
        route_b = sb("route_b", DEPTH * 20, 1)
        b_gates = sb("b_gates", 4, H)
        m0 = sb("m0", 2, H)
        m_new = sb("m_new", 2, H)
        dt_bias = sb("dt_bias", 1, 64)
        a_log = sb("a_log", 1, 64)
        a_neg = sb("a_neg", 1, 64)
        d_skip = sb("d_skip", KE)
        rank = sb("rank", 4)
        before = sb("before", P)
        chunk_no = sb("chunk_no", 2 * MAXP, 1)
        slots = ctx.enter_context(nc.sbuf_tensor("slots", [P, 2 * NT], mybir.dt.uint32))
        plan = ctx.enter_context(nc.sbuf_tensor("plan", [1, 2 * MAXP + 1], mybir.dt.int32))
        xg = nc.dram_tensor("xg", [2 * MAXP * CH, D], F32, kind="Internal").ap()
        yg = nc.dram_tensor("yg", [2 * MAXP * CH, D], F32, kind="Internal").ap()
        sm = sb("sm", 308)
        nT = sm[:, 128:160].rearrange("p (d h j) -> p d h j", d=2, h=H)
        c_wi = sm[:, 160:176].rearrange("p (t d h) -> p t d h", t=2, d=2)
        c_nM = sm[:, 176:200].rearrange("p (t d h) -> p t d h", t=NT, d=2)
        c_fl = sm[:, 200:224].rearrange("p (t d h) -> p t d h", t=NT, d=2)
        c_wk = sm[:, 224:232]
        den, rden, qn = sm[:, 232:238], sm[:, 238:244], sm[:, 244:248]
        cwt = v3(sm[:, 248:264], H)
        cw = lambda h, t, d: cwt[:, h, 2 * t + d:2 * t + d + 1]
        bst = sm[:, 264:270]
        h_mv = v3(sm[:, 270:294], NT * H)
        h_rs = sm[:, 294:306]
        acs_end = sm[0:64, 306:307]

        arena = sb("arena", ARENA)
        at = [0]

        def region(cols, start=None):
            if start is not None:
                at[0] = start
            a = at[0]
            at[0] += cols
            assert at[0] <= ARENA, at[0]
            return arena[:, a:a + cols], a

        a_xc, _ = region(KE * T, 0)
        a_xc = v3(a_xc, KE)
        xu_r, xu_at = region(KE * W_PAD)
        a_xu = v3(xu_r, KE)
        q_r, _ = region(KE * T)
        a_qT = v3(q_r, KE)
        a_sz = v3(q_r, KE)
        k_r, _ = region(KE * T)
        a_kT = v3(k_r, KE)
        v_r, _ = region(NT * E2)
        a_v = v3(v_r, NT)
        scan_at = at[0]
        e_r, _ = region(2 * 2 * 5 * P)
        a_E = v4(e_r, 2, 2)
        a_pT, _ = region(5 * P)
        a_tmp = v3(region(2 * 512)[0], 2)
        a_kw = v3(region(2 * 512)[0], 2)
        a_cst = v3(region(2 * 512)[0], 2)
        a_cbuf = v3(region(2 * (W_PAD - 2 * PAD), scan_at)[0], 2)
        a_vb = v3(region(2 * T)[0], 2)
        a_bd = region(2 * 3 * P)[0].rearrange("p (s q b c) -> p s q b c", s=2, q=3, c=4)
        a_wq = region(3 * KE * 4)[0].rearrange("p (q k c) -> p q k c", q=3, k=KE)
        blockmask, _ = region(P)
        zeros = a_cst[:, 1, 0:256]
        ada_rows = v3(a_cst[:, 0, :], 2)
        nrow = e_r[0:32, 0:P]
        a_h = v3(region(NT * E2, xu_at)[0], NT)
        a_rowG = v3(region(4 * T, xu_at)[0][0:H, :], 4)
        a_u = v3(region(2 * T)[0][0:H, :], 2)
        a_lf = v3(region(2 * T)[0][0:H, :], 2)
        a_b = v3(region(2 * T)[0][0:H, :], 2)
        a_nM = v3(region(2 * T)[0][0:H, :], 2)
        a_wi = v3(region(2 * T)[0][0:H, :], 2)
        a_fl = v3(region(2 * T)[0][0:H, :], 2)
        a_a = v3(gates_w[0:H, :], 2)
        a_gtok = v3(sm[:, 0:48], NT)
        a_col = sm[:, 48:48 + 80]
        prow = v3(region(5 * P, scan_at)[0], 5)
        x_tok = v3(region(NT * D, 0)[0], NT)

        b_xs = v3(region(KE * T, 0)[0], KE)
        b_bc = v3(region(2 * G * T)[0], 2 * G)
        bx_r, _ = region(NT * E2)
        b_x = v3(bx_r, NT)
        b_sq = v3(bx_r, KE)
        y_r, y_at = region(NT * E2)
        b_y = v3(y_r, NT)
        b_h0 = v3(region(2 * E2)[0], 2)
        z_r, z_at = region(KE * T)
        b_z = v3(z_r, KE)
        b_acs = region(T)[0][0:64, :]
        b_col = region(9 * 64)[0]
        b_E = v4(region(4 * 512)[0], 2, 2)
        b_cb = v3(region(2 * 5 * P)[0], 2)
        b_t = v3(region(2 * 512)[0], 2)
        b_t2 = b_E[:, 0]
        acs_parts = v3(gates_w[0:64, 0:3 * T // 2].bitcast(mybir.dt.bfloat16), 3)
        ident_b = gates_w[0:64, 3 * T // 2:3 * T // 2 + 32].bitcast(mybir.dt.bfloat16)
        b_pre = v3(region(4 * W_PAD, y_at)[0], 4)
        b_cbuf = v3(region(2 * (W_PAD - 2 * PAD))[0], 2)
        b_dt, b_u, b_l, b_eq, b_es = (region(T)[0][0:64, :] for _ in range(5))
        b_Bt = v3(region(G * P)[0], G)
        b_wx = v3(region(2 * E2 // G, y_at)[0], 2)
        b_st = v3(region(2 * 512)[0], 2)

        m_h = v3(region(NT * D, 0)[0], NT)
        m_w = v3(region(6 * KD * FF)[0], 6)
        m_xc = v3(region(2 * D)[0][0:CH, :], 2)
        m_hg = region(2 * KD * CH)[0].rearrange("p (u c) -> p u c", u=2)
        m_sg = v3(region(2 * 2 * CH)[0], 2)
        m_a = region(4 * CH)[0].rearrange("p (u f c) -> p u f c", u=2, f=2)
        m_o = v3(region(2 * D)[0][0:CH, :], 2)
        m_y = region(2 * NT * D)[0].rearrange("p (i t c) -> p i t c", i=2, t=NT)
        m_L = v3(region(NT * 20)[0], NT)
        m_F = region(2 * NT * 16)[0].rearrange("p (i t e) -> p i t e", i=2, t=NT)
        m_A = v3(region(NT * 16)[0], NT)
        m_sl = v3(region(NT * 16)[0], NT)
        m_cnt, m_n, m_end, m_base = (region(16)[0] for _ in range(4))
        m_cmp = v3(region(2 * MAXP * 16)[0][0:1, :], 2 * MAXP)
        m_eq = region(2 * MAXP)[0][0:1, :]
        m_sf = v3(region(2 * NT)[0], 2)
        r_mx, r_mp, r_m1, r_m2, r_gs, r_w1, r_w2, r_e2 = (region(NT)[0] for _ in range(8))
        r_eg, r_ohg, r_t4, r_sel, r_oh1, r_oh2 = (v3(region(NT * 4)[0], NT) for _ in range(6))
        r_t16 = v4(region(NT * 16)[0], NT, NG)
        m_mark = region(1)[0]
        l_t = v3(region(2 * T, 30000)[0], 2)
        l_v = region(T)[0]
        l_rs = region(T)[0]
        y_out = v3(region(2 * 512)[0], 2)

        ada_b = lambda l, j: par[:, 0, 48 * l + j:48 * l + j + 1]
        a_cw = lambda j, c: par[:, 1, 16 * j + c:16 * j + c + 1]
        a_cb = lambda c: par[:, 1, 80 + c:81 + c]
        a_nw = lambda c: par[:, 1, 96 + c:97 + c]
        a_sk = lambda c: par[:, 1, 112 + c:113 + c]
        ln_w = lambda l, i, k: par[:, 2, 16 * l + 8 * i + k:16 * l + 8 * i + k + 1]
        ln_b = lambda l, i, k: par[:, 2, 32 + 16 * l + 8 * i + k:33 + 16 * l + 8 * i + k]
        b_cbias = lambda c: par[:, 2, 64 + c:65 + c]
        b_nw = lambda c: par[:, 2, 88 + c:89 + c]
        b_cw = lambda j, c: par[:, 3, 24 * j + c:24 * j + c + 1]
        n0T = par[:, 4, 0:32]
        PROWS = (112, 128, 104, 120, 32)

        slabs = []
        ada_w, a_in, a_dn, b_in, b_dn = i_["ada_w"], i_["a_w_in"], i_["a_w_down"], i_["b_w_in"], i_["b_w_out"]

        def add(kind, w, c0, quarters=(0, 1)):
            for q in quarters:
                slabs.append((kind, w[4 * q * P:4 * (q + 1) * P, c0:c0 + 256].rearrange("(k p) c -> p k c", p=P)))

        ada_at = [0]

        def add_ada(n):
            for _ in range(n):
                l, s = divmod(ada_at[0], 24)
                add("ada", ada_w[l], 256 * s)
                ada_at[0] += 1

        add_ada(8)
        for s in range(8):
            for q in range(2):
                add("xu", a_in[0], 256 * s, (q,))
                add_ada(1)
        for h in range(H):
            for d in range(2):
                C0 = i_["state_mlstm_C"][0, 0, d, h].rearrange("(k p) c -> p k c", p=P)
                slabs.append(("C0", C0[:, 0:2]))
                slabs.append(("C0", C0[:, 2:4]))
        for s in range(8):
            for q in range(2):
                add("z", a_in[0], E2 + 256 * s, (q,))
                add_ada(1)
        for s in range(4):
            for q in range(2):
                add("down", a_dn[0], 256 * s, (2 * q, 2 * q + 1))
                add_ada(1)
        moe_at = [len(slabs)]
        slabs.append(("dt", b_in[0][:, 5120:5184].rearrange("(k p) c -> p k c", p=P)))
        for s in list(range(8, 12)):
            add("bc", b_in[0], E2 + 256 * s)
        for s in range(8):
            add("x", b_in[0], E2 + 256 * s)
        for d in range(2):
            h0 = i_["state_ssd"][0, 0, d].rearrange("(k j) p n -> (j p) k n", j=2)
            slabs.append(("h0", h0[:, 0:8]))
            slabs.append(("h0", h0[:, 8:16]))
        for s in range(8):
            add("zb", b_in[0], 256 * s)
        for s in range(4):
            add("out", b_dn[0], 256 * s, range(4))
        moe_at.append(len(slabs))

        def slot(n):
            return ring[:, (n % RING) * SLAB:(n % RING + 1) * SLAB]

        slab_in = [sem(f"slab_in{s}") for s in range(RING)]
        landed = [16 * (n // RING + 1) for n in range(len(slabs))]
        slab_free = {}

        filled = sem("filled")
        n_filled = [0]
        group = {}
        stage_n = {}
        occupant = [None] * 8
        next_bank = [0]
        ring_banks = [5]

        def read(stage):
            return sem(stage + "_read")

        def claim(pe, stage, bank=None, reads=1):
            k = stage_n.get(stage, 0)
            stage_n[stage] = k + 1
            if bank is None:
                bank = next_bank[0] % ring_banks[0]
                next_bank[0] += 1
            if occupant[bank]:
                pe.wait_ge(*occupant[bank])
            occupant[bank] = (read(stage), reads * (k + 1))
            return (stage, k, bank), banks[bank]

        def finish(ins, key=None):
            n_filled[0] += 1
            ins.then_inc(filled, 1)
            if key:
                group[key[:2]] = (key[2], n_filled[0])

        def await_bank(eng, stage, k):
            b, n = group[stage, k]
            eng.wait_ge(filled, n)
            return banks[b]

        block = ctx.enter_context(nc.Block())
        mm = nc.tensor.matmul

        @block.tensor
        def _(pe):
            n_slab = [0]

            def slab(kind):
                n = n_slab[0]
                assert slabs[n][0] == kind, (n, slabs[n][0], kind)
                n_slab[0] = n + 1
                pe.wait_ge(slab_in[n % RING], landed[n])
                return n, slot(n)

            def used(n):
                slab_free[n] = n_filled[0]

            ada_n = [0]
            mod_key = [None]

            def ada_turn():
                s = ada_n[0] - 1
                if s in (0, 8, 24):
                    mod_key[0] = claim(pe, "mod", bank=5)[0]
                pe.wait_ge(read("ada"), s + 1)
                for j in (0, 1):
                    c = 2 * (2 * (s % 24) + j)
                    last = mm(banks[5][:, c:c + 2], ada_rows[:, s % 2, P * j:P * j + P], pick[:, :], start=True, stop=True)
                finish(last, mod_key[0] if s in (7, 23, 47) else None)
                group["turned", s] = n_filled[0]

            def ada_slab():
                if ada_n[0] not in (0, 8, 24):
                    ada_turn()
                ada_n[0] += 1
                key, ps = claim(pe, "ada", bank=7)
                for half in (0, 1):
                    n, w = slab("ada")
                    w = v3(w, 4)
                    for j in range(4):
                        k = 4 * half + j
                        last = mm(ps[32 * j:32 * j + 32, 0:256], csil[:, 2 * k:2 * k + 32], w[:, j, :],
                                  start=half == 0, stop=half == 1)
                    finish(last, key if half else None)
                    used(n)

            def project(stage, kind, ready, with_ada=False):
                keys = [claim(pe, stage) for _ in range(2)]
                for half in (0, 1):
                    n, w = slab(kind)
                    w = v3(w, 4)
                    for j in (0, 1):
                        for k in range(4):
                            ready(4 * half + k)
                            last = mm(keys[j][1][:, 0:T], w[:, k, P * j:P * j + P], hT[:, 4 * half + k, :],
                                      start=half == 0 and k == 0, stop=half == 1 and k == 3, skip_group_check=True)
                        if half or j:
                            finish(last, keys[j][0] if half else None)
                    used(n)
                    if with_ada:
                        ada_slab()

            def project_back(stage, kind, src, ready):
                for s in range(4):
                    keys = [claim(pe, stage) for _ in range(2)]
                    for q in range(4):
                        n, w = slab(kind)
                        w = v3(w, 4)
                        for j in (0, 1):
                            for k in range(4):
                                ready(4 * q + k)
                                last = mm(keys[j][1][:, 0:T], w[:, k, P * j:P * j + P], src[:, 4 * q + k, :],
                                          start=q == 0 and k == 0, stop=q == 3 and k == 3, skip_group_check=True)
                            if q == 3 or j:
                                finish(last, keys[j][0] if q == 3 else None)
                        used(n)
                        if kind == "down" and q % 2:
                            ada_slab()

            def layer_norm(n):
                key, ps = claim(pe, "mean", reads=KD)
                for k in range(KD):
                    pe.wait_ge(sem("r_ready"), KD * n + k + 1)
                    last = mm(ps[:, 0:T], ones_d[:, :], xT[:, k, :], start=k == 0, stop=k == KD - 1)
                finish(last, key)
                key, ps = claim(pe, "var")
                for k in range(KD):
                    pe.wait_ge(sem("sq_ready"), KD * n + k + 1)
                    last = mm(ps[:, 0:T], ones_d[:, :], hT[:, k, :], start=k == 0, stop=k == KD - 1)
                finish(last, key)

            def moe(l):
                L = f"_{l}"
                key, ps = claim(pe, "route")
                for t in range(NT):
                    for k in range(KD):
                        if t == 0:
                            pe.wait_ge(sem("h_ready"), 8 * (2 * l + 1) + k + 1)
                        mm(ps[:, 20 * t:20 * t + 20], hT[:, k, P * t:P * t + P], route_w[:, l, k, :],
                           start=k == 0, stop=False)
                    last = mm(ps[:, 20 * t:20 * t + 20], ones[0:1, :], route_b[0:1, 20 * l:20 * l + 20],
                              start=False, stop=True)
                finish(last, key)
                for t in range(NT):
                    for m in range(2):
                        key, ps = claim(pe, "ht")
                        for i in range(4):
                            last = nc.tensor.transpose(ps[:, P * i:P * i + P], hT[:, 4 * m + i, P * t:P * t + P],
                                                       ident[:, :])
                        finish(last, key)
                pe.wait_ge(sem("chosen"), l + 1)
                key, ps = claim(pe, "count")
                for t in range(NT):
                    for r in range(t):
                        mm(ps[:, 16 * t:16 * t + 16], ones[:, :], m_A[:, r, :], start=r == 0, stop=False)
                    mm(ps[:, 16 * t:16 * t + 16], before[:, :], m_A[:, t, :], start=t == 0, stop=True)
                for r in range(NT):
                    last = mm(ps[:, 48:64], ones[:, :], m_A[:, r, :], start=r == 0, stop=r == NT - 1)
                finish(last, key)
                for b in range(8):
                    if occupant[b]:
                        pe.wait_ge(*occupant[b])
                        occupant[b] = None
                fill = sem("mfill" + L)

                def pair(p, first):
                    for u in (0, 1):
                        pe.wait_ge(sem(f"mx_in{u}" + L), p * 16 + 16)
                        if u and not first:
                            pe.wait_ge(sem("mdn_read" + L), p * 4)
                        mm(banks[2 * u][:, 0:CH], m_xc[:, u, 0:P], ident[0:CH, 0:CH])
                        for k in range(1, KD):
                            last = nc.tensor.transpose(banks[2 * u + k // 4][:, CH * (k % 4):CH * (k % 4) + CH],
                                                       m_xc[:, u, P * k:P * k + P], ident[0:CH, 0:CH])
                        last.then_inc(fill, 1)
                    for u in (0, 1):
                        pe.wait_ge(sem("mT_read" + L), p * 2 + (u + 1))
                        for s in (0, 1):
                            pe.wait_ge(sem(f"mw_in{3 * u + s}" + L), p * 16 + 16)
                            for j in (0, 1):
                                o = CH * (2 * s + j)
                                for k in range(KD):
                                    last = mm(banks[4 + u][:, o:o + CH],
                                              v3(m_w[:, 3 * u + s, :], KD)[:, k, P * j:P * j + P],
                                              m_hg[:, u, CH * k:CH * k + CH], start=k == 0, stop=k == KD - 1)
                            last.then_inc(fill, 1)
                    for u in (0, 1):
                        pe.wait_ge(sem(f"mw_in{3 * u + 2}" + L), p * 16 + 16)
                        pe.wait_ge(sem("mup_read" + L), p * 2 + (u + 1))
                        for m in (0, 1):
                            for f in (0, 1):
                                last = mm(banks[(6, 2)[u] + m][0:CH, :], m_a[:, u, f, :],
                                          v3(m_w[:, 3 * u + 2, :], 2)[:, f, 512 * m:512 * m + 512],
                                          start=f == 0, stop=f == 1)
                            last.then_inc(fill, 1)

                pe.wait_ge(sem("planned"), l + 1)
                pairs = pe.value_load(plan[0:1, 2 * MAXP:2 * MAXP + 1], min_val=MINP, max_val=MAXP)
                pair(0, True)
                with pe.Fori(1, pairs) as p:
                    pair(p, False)
                pe.wait_ge(sem("mT_read" + L), pairs * 2)
                pe.wait_ge(sem("mgate_read" + L), pairs * 2)
                pe.wait_ge(sem("mup_read" + L), pairs * 2)
                pe.wait_ge(sem("mdn_read" + L), pairs * 4)
                pe.wait_ge(sem("moe_sum"), NT * l + NT)
                for m in range(KD):
                    key, ps = claim(pe, "yt")
                    for t in range(NT):
                        last = nc.tensor.transpose(ps[:, P * t:P * t + P], m_y[:, 0, t, P * m:P * m + P], ident[:, :])
                    finish(last, key)

            pe.wait_ge(sem("consts"), 1)
            pe.wait_ge(sem("prow_in"), 16 * 13)
            for i in range(5):
                key, ps = claim(pe, "par")
                finish(nc.tensor.transpose(ps[:, 0:PROWS[i]], prow[0:PROWS[i], i, :],
                                           ident[0:PROWS[i], 0:PROWS[i]]), key)
            pe.wait_ge(sem("x_in"), 32)
            for k in range(KD):
                key, ps = claim(pe, "xT")
                for t in range(NT):
                    last = nc.tensor.transpose(ps[:, P * t:P * t + P], x_tok[:, t, P * k:P * k + P], ident[:, :])
                finish(last, key)

            pe.wait_ge(sem("csil_ready"), 1)
            for _ in range(8):
                ada_slab()
            ada_turn()
            for s in range(8):
                project("xu", "xu", lambda k: pe.wait_ge(sem("h_ready"), k + 1) if s == 0 else None, True)
            ada_turn()
            ring_banks[0] = 6

            gkey, gps = claim(pe, "gates", bank=6)

            def gates(c):
                pe.wait_ge(read("qT"), c + 1)
                pe.wait_ge(read("kT"), c + 1)
                pe.wait_ge(read("vT"), c + 1)
                if c == 0:
                    pe.wait_ge(sem("small_in"), SMALL)
                for t in range(NT):
                    for i, src in enumerate((a_qT[:, c, :], a_kT[:, c, :], a_vb[:, c % 2, :])):
                        last = mm(gps[:, 16 * t:16 * t + 16], src[:, P * t:P * t + P],
                                  gates_w[:, (KE * i + c) * 16:(KE * i + c + 1) * 16],
                                  start=c == 0 and i == 0 and t == 0, stop=c == KE - 1 and i == 2,
                                  skip_group_check=True)
                if c == KE - 1:
                    finish(last, gkey)
                key, ps = claim(pe, "v")
                for t in range(NT):
                    last = nc.tensor.transpose(ps[:, P * t:P * t + P], a_vb[:, c % 2, P * t:P * t + P], ident[:, :])
                finish(last, key)

            for c in range(KE):
                pe.wait_ge(sem("bd_ready"), c + 1)
                pe.wait_ge(sem("xc_ready"), c + 1)
                for i, st in enumerate(("qT", "kT", "vT")):
                    key, ps = claim(pe, st)
                    if i < 2:
                        rhs = a_xc[:, c, :]
                        last = mm(ps[:, 0:T], a_bd[:, c % 2, i].rearrange("p b c -> p (b c)"), rhs,
                                  start=True, stop=True)
                    else:
                        for (t0, t1), o in zip(STREAMS, (PAD, TP + 3 * PAD)):
                            last = mm(ps[:, t0:t1], a_bd[:, c % 2, i].rearrange("p b c -> p (b c)"),
                                      a_xu[:, c, o:o + t1 - t0], start=True, stop=True)
                    finish(last, key)
                if c:
                    gates(c - 1)
            gates(KE - 1)

            pe.wait_ge(read("gates"), 1)
            for kind in range(4):
                key, ps = claim(pe, "grow")
                for t in range(NT):
                    last = nc.tensor.transpose(ps[0:H, P * t:P * t + P], a_gtok[:, t, 4 * kind:4 * kind + 4],
                                               ident[:, :])
                finish(last, key)
            pe.wait_ge(sem("rows_ready"), 1)
            key, ps = claim(pe, "col")
            for q, src in enumerate((a_nM, a_wi, a_fl)):
                for t in range(NT):
                    for d in range(2):
                        o = ((q * NT + t) * 2 + d) * 4
                        nc.tensor.transpose(ps[:, o:o + 4], src[:, d, P * t:P * t + P], ident[0:H, 0:H])
            for d in range(2):
                last = nc.tensor.transpose(ps[:, 72 + 4 * d:76 + 4 * d], a_u[:, d, 0:P], ident[0:H, 0:H])
            finish(last, key)

            def scores(h):
                for d in range(2):
                    key, ps = claim(pe, "abc")
                    finish(mm(ps[:, 0:T], ident[0:H, h:h + 1].to_broadcast([H, P]), a_a[:, d, :],
                              start=True, stop=True), key)
                key, ps = claim(pe, "scP")
                for j in range(KH):
                    last = mm(ps[:, 0:TP], a_qT[:, KH * h + j, 0:TP], a_kT[:, KH * h + j, 0:TP],
                              start=j == 0, stop=j == KH - 1)
                finish(last, key)
                key, ps = claim(pe, "scS")
                for t in (1, 2):
                    for j in range(KH):
                        last = mm(ps[:, TS * (t - 1):TS * t], a_qT[:, KH * h + j, P * t:P * t + P],
                                  a_kT[:, KH * h + j, TP:T], start=j == 0, stop=j == KH - 1)
                finish(last, key)
                key, ps = claim(pe, "qn")
                for t in (1, 2):
                    for j in range(KH):
                        last = mm(ps[:, 2 * t - 2:2 * t], a_qT[:, KH * h + j, P * t:P * t + P],
                                  n0T[:, KH * h + j:32:16], start=j == 0, stop=j == KH - 1)
                finish(last, key)

            scores(0)
            for h in range(H):
                if h + 1 < H:
                    scores(h + 1)
                for d in range(2):
                    keys = [claim(pe, f"qc{d}") for _ in range(2)]
                    for half in (0, 1):
                        n, w = slab("C0")
                        w = v3(w, 2)
                        for t in (1, 2):
                            for j in (0, 1):
                                last = mm(keys[t - 1][1][:, :], a_qT[:, KH * h + 2 * half + j, P * t:P * t + P], w[:, j, :],
                                          start=half == 0 and j == 0, stop=half == 1 and j == 1, skip_group_check=True)
                            if half or t == 2:
                                finish(last, keys[t - 1][0] if half else None)
                        used(n)
                pe.wait_ge(sem("p_ready"), h + 1)
                key, ps = claim(pe, "pTS")
                for t in range(2):
                    for r in range(2):
                        o = P * (2 * t + r)
                        last = nc.tensor.transpose(ps[:, o:o + P], a_E[:, h % 2, 0, P + TS * t + P * r:2 * P + TS * t + P * r],
                                                   ident[:, :])
                finish(last, key)
                key, ps = claim(pe, "pTP")
                finish(nc.tensor.transpose(ps[:, 0:P], a_E[:, h % 2, 0, 0:P], ident[:, :]), key)
                key, ps = claim(pe, "kt", reads=2)
                for j in range(KH):
                    last = nc.tensor.transpose(ps[:, P * j:P * j + P], a_kT[:, KH * h + j, 0:TP], ident[:, :])
                finish(last, key)
                pe.wait_ge(read("pTS"), h + 1)
                pe.wait_ge(read("pTP"), h + 1)
                for t in range(NT):
                    key, ps = claim(pe, "pv")
                    rs = (0,) if t == 0 else (0, 1)
                    for r in rs:
                        lhs = a_pT[:, 4 * P:5 * P] if t == 0 else a_pT[:, P * (2 * t - 2 + r):P * (2 * t - 1 + r)]
                        last = mm(ps[:, :], lhs, a_v[:, 0 if t == 0 else 1 + r, DH * h:DH * h + DH],
                                  start=r == 0, stop=r == rs[-1])
                    finish(last, key)
                pe.wait_ge(read("kt"), 2 * h + 2)
                for d in range(2):
                    for j in range(KH):
                        key, ps = claim(pe, "cn")
                        finish(mm(ps[:, :], a_kw[:, d, P * j:P * j + P], a_v[:, 0, DH * h:DH * h + DH],
                                  start=True, stop=True), key)
                key, ps = claim(pe, "nn")
                for d in range(2):
                    for j in range(KH):
                        last = mm(ps[:, KH * d + j:KH * d + j + 1], a_kw[:, d, P * j:P * j + P], ones[:, 0:1],
                                  start=True, stop=True)
                finish(last, key)
            pe.wait_ge(read("nn"), H)
            key, ps = claim(pe, "nrow")
            finish(nc.tensor.transpose(ps[0:32, 0:P], sm[:, 128:160], ident[:, :]), key)

            ring_banks[0] = 5
            for s in range(8):
                project("z", "z", lambda k: None, True)
            for c in range(KE):
                key, ps = claim(pe, "hn")
                pe.wait_ge(sem("hn_ready"), NT * (c // KH + 1))
                for t in range(NT):
                    last = nc.tensor.transpose(ps[:, P * t:P * t + P], a_h[:, t, P * c:P * c + P], ident[:, :])
                finish(last, key)
            project_back("yA", "down", a_xc, lambda k: pe.wait_ge(sem("gA_ready"), k + 1))
            ada_turn()
            ring_banks[0] = 6
            layer_norm(0)
            moe(0)
            layer_norm(1)

            n, w = slab("dt")
            w = v3(w[:, 0:KD * 64], KD)
            key, ps = claim(pe, "dt")
            for k in range(KD):
                pe.wait_ge(sem("h_ready"), 16 + k + 1)
                last = mm(ps[0:64, 0:T], w[:, k, :], hT[:, k, :], start=k == 0, stop=k == KD - 1)
            finish(last, key)
            used(n)
            for s in range(4):
                project("xbc", "bc", lambda k: None)
            for s in range(8):
                project("xbc", "x", lambda k: None)
            pe.wait_ge(sem("brows_ready"), 1)
            key, ps = claim(pe, "bcol0")
            for t in range(NT):
                nc.tensor.transpose(ps[:, 64 * t:64 * t + 64], b_acs[:, P * t:P * t + P], ident[0:64, 0:64])
                last = nc.tensor.transpose(ps[:, 192 + 64 * t:256 + 64 * t], b_dt[:, P * t:P * t + P],
                                           ident[0:64, 0:64])
            finish(last, key)
            key, ps = claim(pe, "bcol1")
            for t in range(NT):
                last = nc.tensor.transpose(ps[:, 64 * t:64 * t + 64], b_es[:, P * t:P * t + P], ident[0:64, 0:64])
            finish(last, key)
            for d in range(2):
                for half in (0, 1):
                    n, w = slab("h0")
                    for c2 in range(2):
                        key, ps = claim(pe, "h0")
                        for i in range(4):
                            c = 4 * c2 + i
                            last = nc.tensor.transpose(ps[:, P * i:P * i + P], w[:, P * c:P * c + P], ident[:, :])
                        finish(last, key)
                    used(n)
            pe.wait_ge(sem("xs_ready"), 8)
            key, ps = claim(pe, "Bt")
            for g in range(G):
                last = nc.tensor.transpose(ps[:, P * g:P * g + P], b_bc[:, g, 0:TP], ident[:, :])
            finish(last, key)
            for c in range(KE):
                pe.wait_ge(sem("xs_ready"), 8 + c + 1)
                key, ps = claim(pe, "xt")
                for t in range(NT):
                    last = nc.tensor.transpose(ps[:, P * t:P * t + P], b_xs[:, c, P * t:P * t + P], ident[:, :])
                finish(last, key)
            pe.wait_ge(read("Bt"), 1)
            for g in range(G):
                for d in range(2):
                    pe.wait_ge(sem("wx_ready"), 2 * g + d + 1)
                    key, ps = claim(pe, "sn")
                    for i in range(4):
                        last = mm(ps[:, P * i:P * i + P], b_wx[:, d, P * i:P * i + P], b_Bt[:, g, :],
                                  start=True, stop=True)
                    finish(last, key)
            z_at_work = {}

            def z_part(n):
                c, part = divmod(n, 4)
                half = part // 2
                if part == 0:
                    z_at_work["key"] = claim(pe, "zb", bank=4)
                if c % 2 == 0 and part % 2 == 0:
                    z_at_work[half] = slab("zb")
                key, ps = z_at_work["key"]
                n_slab_z, w = z_at_work[half]
                for k in range(2 * part, 2 * part + 2):
                    last = mm(ps[:, 0:T], v3(w, 4)[:, k % 4, P * (c % 2):P * (c % 2) + P], hT[:, k, :],
                              start=k == 0, stop=k == KD - 1, skip_group_check=True)
                finish(last, key if part == 3 else None)
                if c % 2 and part % 2:
                    used(n_slab_z)

            for g in range(G):
                key, ps = claim(pe, "cbP", bank=4)
                finish(mm(ps[:, 0:TP], b_bc[:, g, 0:TP], b_bc[:, G + g, 0:TP], start=True, stop=True), key)
                key, ps = claim(pe, "cbS", bank=3)
                for r in range(2):
                    last = mm(ps[:, TS * r:TS * r + TS], b_bc[:, g, TP + P * r:TP + P * r + P], b_bc[:, G + g, TP:T],
                              start=True, stop=True)
                finish(last, key)
                ykeys = [claim(pe, f"y{t}", bank=5 + t) for t in range(NT)]

                def broadcast(u):
                    hh, d = divmod(u, 2)
                    key, ps = claim(pe, "acsb", bank=u % 4)
                    row = 32 * d + HG * g + hh
                    for i in range(3):
                        last = mm(ps[:, 0:T], ident_b[:, row:row + 1].to_broadcast([64, P]), acs_parts[:, i, :],
                                  start=i == 0, stop=i == 2)
                    finish(last, key)

                for u in range(3):
                    broadcast(u)
                for u in range(2 * HG):
                    if u + 3 < 2 * HG:
                        broadcast(u + 3)
                    hh, d = divmod(u, 2)
                    pe.wait_ge(sem("w_ready"), 2 * HG * g + u + 1)
                    E = b_E[:, hh % 2, d, :]
                    parts = (((0, 0, 0), (1, 128, 1), (2, 256, 1), (2, 384, 2)),
                             ((0, 0, 0), (1, 128, 1), (1, 256, 2), (2, 384, 2)))[d]
                    for n_part, (t, o, r) in enumerate(parts):
                        last = mm(ykeys[t][1][:, PH * hh:PH * hh + PH], E[:, o:o + P],
                                  b_x[:, r, 512 * g + PH * hh:512 * g + PH * hh + PH],
                                  start=d == 0 and n_part != 3, stop=d == 1 and n_part != 1,
                                  skip_group_check=True)
                    finish(last, ykeys[2][0] if u == 2 * HG - 1 else None)
                    group["w_used", 2 * HG * g + u] = n_filled[0]
                    z_part(2 * HG * g + u)
                for t in range(2):
                    group[f"y{t}", g] = (5 + t, group["y2", g][1])
                for d in range(2):
                    for t in (1, 2):
                        key, ps = claim(pe, "inter", bank=2 * (d) + (t - 1))
                        finish(mm(ps[:, :], b_bc[:, G + g, P * t:P * t + P], b_h0[:, d, 512 * g:512 * g + 512],
                                  start=True, stop=True), key)
            for c in range(KE):
                key, ps = claim(pe, "yT")
                pe.wait_ge(read("y2"), c // 4 + 1)
                for t in range(NT):
                    last = nc.tensor.transpose(ps[:, P * t:P * t + P], b_y[:, t, P * c:P * c + P], ident[:, :])
                finish(last, key)
            key, ps = claim(pe, "msq")
            for c in range(KE):
                pe.wait_ge(sem("gsq_ready"), c + 1)
                last = mm(ps[:, 0:T], ones_d[:, :], b_sq[:, c, :], start=c == 0, stop=c == KE - 1)
            finish(last, key)
            project_back("yB", "out", b_xs, lambda k: pe.wait_ge(sem("gB_ready"), k + 1))
            layer_norm(2)
            moe(1)
            layer_norm(3)
            for t in range(NT):
                for m in range(2):
                    pe.wait_ge(sem("x_final"), KD)
                    key, ps = claim(pe, "out")
                    for i in range(4):
                        last = nc.tensor.transpose(ps[:, P * i:P * i + P], xT[:, 4 * m + i, P * t:P * t + P],
                                                   ident[:, :])
                    finish(last, key)



        @block.sync
        def _(sp):
            sp.dma_start(x_tok[:, 0, :], i_["x_prompt"][0]).then_inc(sem("x_in"), 16)
            sp.dma_start(x_tok[:, 1:3, :], i_["x_sample"][0].rearrange("(t p) c -> p t c", p=P)).then_inc(sem("x_in"), 16)

            def moe(l):
                L = f"_{l}"
                wg = i_["moe_w_gate"][l].rearrange("g e k f -> (g e) k f")
                wu = i_["moe_w_up"][l].rearrange("g e k f -> (g e) k f")
                wd = i_["moe_w_down"][l].rearrange("g e f k -> (g e) f k")
                sp.wait_ge(sem("planned"), l + 1)
                pairs = sp.value_load(plan[0:1, 2 * MAXP:2 * MAXP + 1], min_val=MINP, max_val=MAXP)

                def pair(p, first):
                    experts = []
                    for u in (0, 1):
                        q = p * 2 + u
                        at = plan[0:1, q:q + 1] if first else plan[0:1, bass.ds(q, 1)]
                        experts.append(sp.value_load(at, min_val=0, max_val=NEXP - 1))
                        if not first:
                            sp.wait_ge(sem("mfill" + L), p * 10 + (u - 9))
                        elif u == 0:
                            sp.wait_ge(sem("scattered"), 16 * 2 * NT * (l + 1))
                        x = xg[CH * q:CH * q + CH, :] if first else xg[bass.ds(q * CH, CH), :]
                        sp.dma_start(m_xc[:, u, :], x).then_inc(sem(f"mx_in{u}" + L), 16)
                    for u, s, w, n in ((0, 0, wg, 3), (0, 1, wu, 4), (1, 0, wg, 5), (1, 1, wu, 6), (0, 2, wd, 8), (1, 2, wd, 10)):
                        if not first:
                            sp.wait_ge(sem("mfill" + L), p * 10 + (n - 10))
                        src = w[bass.ds(experts[u], 1)].rearrange("o (k p) f -> p (o k) f", p=P)
                        sp.dma_start(v3(m_w[:, 3 * u + s, :], KD if s < 2 else 2), src).then_inc(
                            sem(f"mw_in{3 * u + s}" + L), 16)

                pair(0, True)
                with sp.Fori(1, pairs) as p:
                    pair(p, False)

            for n, (kind, src) in enumerate(slabs):
                for l in range(DEPTH):
                    if n == min(moe_at[l] + RING, len(slabs)):
                        moe(l)
                if n >= RING:
                    sp.wait_ge(filled, slab_free[n - RING])
                k, c = src.shape[1], src.shape[2]
                sp.dma_start(v3(slot(n)[:, 0:k * c], k), src).then_inc(slab_in[n % RING], 16)
            moe(1)

        @block.gpsimd
        def _(pool):
            pl = nc.gpsimd
            n_link = [0]

            def link(ins):
                n_link[0] += 1
                ins.then_inc(sem("pool_step"), 1)
                pool.wait_ge(sem("pool_step"), n_link[0])

            pl.memset(ones[:, :], 1.0)
            pl.memset(csil[:, 2 * KD:], 0.0)
            pl.memset(ones_d[:, :], 1.0 / D)
            pl.memset(zeros[:, :], 0.0)
            pl.memset(before[:, :], 1.0)
            pl.iota(chunk_no[:, :], pattern=[[1, 2 * MAXP]], base=0, channel_multiplier=0,
                    allow_small_or_imprecise_dtypes=True)
            for j in range(4):
                pl.memset(rank[:, j:j + 1], float(4 - j))
            pl.memset(blockmask[:, :], 1.0)
            pl.memset(strip_f[:, :], 0.0)
            pl.memset(strip_b[:, :], 0.0)
            link(pl.memset(ident[:, :], 0.0))
            link(pl.affine_select(out=ident[:, :], in_=ident[:, :], compare_op=ALU.not_equal, fill=1.0, base=0,
                                  pattern=[[-1, P]], channel_multiplier=1))
            pl.affine_select(out=before[:, :], in_=before[:, :], compare_op=ALU.is_gt, fill=0.0, base=0,
                             pattern=[[1, P]], channel_multiplier=-1)
            pl.affine_select(out=strip_f[:, :], in_=strip_f[:, :], compare_op=ALU.is_ge, fill=-BIG, base=P,
                             pattern=[[-1, 3 * P]], channel_multiplier=1)
            pl.affine_select(out=strip_b[:, :], in_=strip_b[:, :], compare_op=ALU.is_ge, fill=-BIG, base=-P,
                             pattern=[[1, 3 * P]], channel_multiplier=-1)
            link(pl.tensor_tensor(out=pick[:, :], in0=ident[:, 0:2], in1=ident[:, 32:34], op=ALU.add))
            link(pl.tensor_tensor(out=pick[:, :], in0=pick[:, :], in1=ident[:, 64:66], op=ALU.add))
            pl.tensor_tensor(out=pick[:, :], in0=pick[:, :], in1=ident[:, 96:98], op=ALU.add)
            bm = blockmask[:, :].rearrange("p (b c) -> p b c", c=4)
            link(pl.affine_select(out=bm, in_=bm, compare_op=ALU.is_ge, fill=0.0, base=0,
                                  pattern=[[-4, 32], [0, 4]], channel_multiplier=1))
            link(pl.affine_select(out=bm, in_=bm, compare_op=ALU.is_ge, fill=0.0, base=3,
                                  pattern=[[4, 32], [0, 4]], channel_multiplier=-1))
            pl.memset(ones[:, 0:1], 1.0).then_inc(sem("consts"), 1)
            pl.memset(xu_r, 0.0).then_inc(sem("pads"), 1)

            small = []
            for q, name in enumerate(("a_w_q", "a_w_k", "a_w_v")):
                small.append((a_wq[:, q], i_[name][0].rearrange("(k b) c d -> (b c) k d", b=32)))
            small.append((gates_w[:, :].rearrange("p (k c) -> p k c", c=16),
                          i_["a_w_gates"][0].rearrange("(k p) c -> p k c", p=P)))
            small.append((b_gates[:, :], i_["a_b_gates"][0].rearrange("(k h) -> h k", h=H)))
            small.append((m0[:, :], i_["state_mlstm_m"][0, 0].rearrange("d h -> h d")))
            for l in range(DEPTH):
                small.append((route_w[:, l, :, 0:4], i_["moe_w_rg"][l].rearrange("(k p) c -> p k c", p=P)))
                for g in range(NG):
                    small.append((route_w[:, l, :, 4 + 4 * g:8 + 4 * g],
                                  i_["moe_w_re"][l, g].rearrange("(k p) c -> p k c", p=P)))
                small.append((route_b[:, 20 * l:20 * l + 4], i_["moe_b_rg"][l:l + 1]))
                small.append((route_b[:, 20 * l + 4:20 * l + 20],
                              i_["moe_b_re"][l:l + 1].rearrange("l g e -> l (g e)")))
            small.append((dt_bias[:, :], i_["b_dt_bias"][0].rearrange("d (h o) -> (d h) o", o=1)))
            small.append((a_log[:, :], i_["b_a_log"][0].rearrange("d (h o) -> (d h) o", o=1)))
            for j in range(2):
                small.append((d_skip[64 * j:64 * j + 64, :],
                              i_["b_d_skip"][0:1, j::2].to_broadcast([64, KE])))
            assert 16 * len(small) == SMALL
            for dst, src in small:
                pool.dma_start(dst, src, allow_slow_non_contiguous=True).then_inc(sem("small_in"), 16)

            pool.wait_ge(sem("small_in"), SMALL)
            for c in range(KE):
                if c >= 2:
                    pool.wait_ge(filled, group["vT", c - 2][1])
                for q in range(3):
                    ins = pl.tensor_tensor(out=a_bd[:, c % 2, q], in0=a_wq[:, q, c, :].unsqueeze(1).to_broadcast([P, 32, 4]),
                                           in1=bm, op=ALU.mult)
                ins.then_inc(sem("bd_ready"), 1)

            def moe(l):
                L = f"_{l}"
                pool.wait_ge(sem("slots_ready"), l + 1)
                pool.wait_ge(sem("cleared"), 32)
                for t in range(NT):
                    pool.wait_ge(read("ht"), 2 * NT * l + 2 * t + 2)
                    for i in range(2):
                        pool.indirect_dma_start(
                            out=xg[:, :], out_offset=bass.IndirectOffsetOnAxis(slots[:, NT * i + t:NT * i + t + 1], 0),
                            in_=m_h[:, t, :], in_offset=None).then_inc(sem("scattered"), 16)
                pool.wait_ge(sem("results_out"), l + 1)
                for t in range(NT):
                    for i in range(2):
                        pool.indirect_dma_start(
                            out=m_y[:, i, t, :], out_offset=None, in_=yg[:, :],
                            in_offset=bass.IndirectOffsetOnAxis(slots[:, NT * i + t:NT * i + t + 1], 0),
                        ).then_inc(sem(f"gathered{t}"), 16)

            pool.wait_ge(sem("h_ready"), 8)
            for rows in (xg, yg[2 * MINP * CH:, :]):
                pool.dma_start(rows.rearrange("(p a) (b c) -> p (a b) c", p=P, c=256),
                               zeros[:, :].unsqueeze(1).to_broadcast([P, rows.shape[0] // P * 4, 256])
                               ).then_inc(sem("cleared"), 16)
            moe(0)
            pool.wait_ge(sem("h_ready"), 17)
            pl.memset(b_pre.rearrange("p k t -> p (k t)"), 0.0).then_inc(sem("pads"), 1)
            pool.wait_ge(read("bcol1"), 1)
            for g in range(G):
                pool.wait_ge(read("xt"), 4 * g + 4)
                for d in range(2):
                    if g:
                        pool.wait_ge(filled, group["sn", 2 * (g - 1) + d][1])
                    pl.tensor_tensor(out=b_wx[:, d, :].rearrange("p (h c) -> p h c", h=HG),
                                     in0=b_x[:, 0, 512 * g:512 * g + 512].rearrange("p (h c) -> p h c", h=HG),
                                     in1=b_col[:, 512 + 32 * d + HG * g:512 + 32 * d + HG * g + HG]
                                     .unsqueeze(2).to_broadcast([P, HG, PH]), op=ALU.mult).then_inc(sem("wx_ready"), 1)
            moe(1)

        @block.scalar
        def _(act):
            ac = nc.scalar.activation
            n_link = [0]

            def link(ins):
                n_link[0] += 1
                ins.then_inc(sem("act_step"), 1)
                act.wait_ge(sem("act_step"), n_link[0])

            prows = (
                (0, 0, 96, i_["ada_b"].rearrange("l (j p) -> (l j) p", p=P)),
                (0, 96, 8, i_["c_ctx"].rearrange("(j p) -> j p", p=P)),
                (0, 104, 8, i_["c"].rearrange("o (j p) -> (o j) p", p=P)),
                (1, 0, 80, i_["a_conv_w"][0].rearrange("w (j p) -> (w j) p", p=P)),
                (1, 80, 16, i_["a_conv_b"].rearrange("o (j p) -> (o j) p", p=P)),
                (1, 96, 16, i_["a_norm_w"].rearrange("o (j p) -> (o j) p", p=P)),
                (1, 112, 16, i_["a_skip"].rearrange("o (j p) -> (o j) p", p=P)),
                (2, 0, 32, i_["ln_w"].rearrange("l i (j p) -> (l i j) p", p=P)),
                (2, 32, 32, i_["ln_b"].rearrange("l i (j p) -> (l i j) p", p=P)),
                (2, 64, 24, i_["b_conv_b"].rearrange("o (j p) -> (o j) p", p=P)),
                (2, 88, 16, i_["b_norm_w"].rearrange("o (j p) -> (o j) p", p=P)),
                (3, 0, 120, i_["b_conv_w"][0].rearrange("w (j p) -> (w j) p", p=P)),
                (4, 0, 32, i_["state_mlstm_n"][0, 0].rearrange("d h (j p) -> (d h j) p", p=P)),
            )
            for tile, r0, n, src in prows:
                act.dma_start(prow[r0:r0 + n, tile, :], src).then_inc(sem("prow_in"), 16)

            act.wait_ge(read("par"), 1)
            ac(csil[:, 0:2 * KD].rearrange("p (k v) -> p v k", v=2), par[:, 0, 96:112].rearrange("p (v k) -> p v k", v=2),
               ACT.Silu).then_inc(sem("csil_ready"), 1)
            for k in range(KD):
                ps = await_bank(act, "xT", k)
                ac(xT[:, k, :], ps[:, 0:T], ACT.Copy).then_inc(read("xT"), 1)

            def modulate(l, shift, permuted, k):
                for v, (t0, t1) in enumerate(STREAMS):
                    out, src = hT[:, k, t0:t1], xT[:, k, t0:t1]
                    if permuted and v:
                        out = out.rearrange("p (w r) -> p r w", r=ROWS)
                        src = src.rearrange("p (r w) -> p r w", r=ROWS)
                    last = ac(out, src, ACT.Identity, bias=mod[:, l, shift + k, v:v + 1],
                              scale=mod[:, l, shift + 8 + k, v:v + 1])
                last.then_inc(sem("h_ready"), 1)

            def ada_row(s):
                ps = await_bank(act, "ada", s)
                if s >= 2:
                    act.wait_ge(filled, group["turned", s - 2])
                ac(ada_rows[:, s % 2, :], ps[:, 0:256], ACT.Copy).then_inc(read("ada"), 1)

            for s in range(8):
                ada_row(s)
            act.wait_ge(sem("mod_ready"), 1)
            act.wait_ge(read("xT"), KD)
            for k in range(KD):
                modulate(0, 0, False, k)

            act.wait_ge(sem("pads"), 1)

            def conv_silu(c, cbuf, bias, out, ready):
                act.wait_ge(sem("conv_ready"), c + 1)
                ac(out[:, 0:TP], cbuf[:, 0:TP], ACT.Silu, bias=bias)
                ac(out[:, TP:T], cbuf[:, TP + 2 * PAD:], ACT.Silu, bias=bias).then_inc(sem(ready), 1)

            def padded(dst, ps, stage):
                ac(dst[:, PAD:PAD + TP], ps[:, 0:TP], ACT.Copy)
                ac(dst[:, TP + 3 * PAD:T + 3 * PAD], ps[:, TP:T], ACT.Copy).then_inc(read(stage), 1)

            for c in range(KE):
                if c % 2 == 0:
                    ada_row(8 + c)
                padded(a_xu[:, c, :], await_bank(act, "xu", c), "xu")
                if c:
                    conv_silu(c - 1, a_cbuf[:, (c - 1) % 2, :], a_cb(c - 1), a_xc[:, c - 1, :], "xc_ready")
                if c % 2:
                    ada_row(8 + c)
            conv_silu(KE - 1, a_cbuf[:, (KE - 1) % 2, :], a_cb(KE - 1), a_xc[:, KE - 1, :], "xc_ready")

            for c in range(KE):
                ps = await_bank(act, "qT", c)
                ac(a_qT[:, c, :], ps[:, 0:T], ACT.Copy).then_inc(read("qT"), 1)
                ps = await_bank(act, "vT", c)
                if c >= 2:
                    act.wait_ge(filled, group["v", c - 2][1])
                ac(a_vb[:, c % 2, :], ps[:, 0:T], ACT.Copy).then_inc(read("vT"), 1)

            act.wait_ge(sem("gate_x"), 1)
            link(ac(a_u, a_u, ACT.Exp))
            ac(a_u, a_u, ACT.Ln, bias=1.0).then_inc(sem("gate_ln"), 1)
            for c in range(KE):
                ac(a_xc[:, c, :], a_xc[:, c, :], ACT.Copy, scale=a_sk(c)).then_inc(sem("skip_ready"), 1)
            act.wait_ge(sem("gate_m"), 1)
            for d in range(2):
                ac(a_wi[:, d, TP:T], a_nM[:, d, TP:T], ACT.Exp, bias=m0[:, d:d + 1])
                end = TP - 1 if d == 0 else 0
                ac(a_u[:, d, 0:TP], a_a[:, d, 0:TP], ACT.Exp, bias=a_nM[:, d, end:end + 1])
            ac(a_fl, a_fl, ACT.Exp).then_inc(sem("rows_ready"), 1)
            act.dma_start(o_["m"][0, 0].rearrange("d h -> h d"), m_new[:, :], allow_slow_non_contiguous=True).then_inc(sem("out_m"), 16)

            def weights_exp(h):
                for d in range(2):
                    act.wait_ge(read("abc"), 2 * h + d + 1)
                    ac(a_E[:, h % 2, d, :], a_E[:, h % 2, d, :], ACT.Exp).then_inc(sem("e_ready"), 1)

            weights_exp(0)
            for h in range(H):
                if h + 1 < H:
                    weights_exp(h + 1)
                act.wait_ge(sem("cw_ready"), h + 1)
                if h:
                    act.wait_ge(read("pv"), NT * h)
                for t in range(2):
                    ps = await_bank(act, "qc0", 2 * h + t)
                    ac(a_tmp[:, t, :], ps[:, :], ACT.Copy, scale=cw(h, t, 0)).then_inc(read("qc0"), 1)
                if h:
                    act.wait_ge(filled, group["pv", NT * h - 1][1])
                ps = await_bank(act, "pTS", h)
                ac(a_pT[:, 0:4 * P], ps[:, :], ACT.Copy).then_inc(read("pTS"), 1)
                ps = await_bank(act, "pTP", h)
                ac(a_pT[:, 4 * P:5 * P], ps[:, 0:P], ACT.Copy).then_inc(read("pTP"), 1)
                for d in range(2):
                    for j in range(KH):
                        n = (2 * h + d) * KH + j
                        ps = await_bank(act, "cn", n)
                        if n == 1:
                            act.wait_ge(sem("cleared"), 32)
                        if n >= 2:
                            act.wait_ge(sem(f"out{n % 2}"), 16 * (n // 2))
                        ac(a_cst[:, n % 2, :], ps[:, :], ACT.Copy).then_inc(read("cn"), 1)
                        act.wait_ge(read("cn"), n + 1)
                        act.dma_start(o_["C"][0, 0, d, h, P * j:P * j + P, :], a_cst[:, n % 2, :]).then_inc(sem(f"out{n % 2}"), 16)
            act.wait_ge(sem("hvar_ready"), 1)
            ac(h_rs, h_rs, ACT.Sqrt).then_inc(sem("hsqrt"), 1)
            act.wait_ge(read("nrow"), 1)
            act.dma_start(o_["n"][0, 0].rearrange("d h (j p) -> (d h j) p", p=P), nrow[:, :]).then_inc(sem("out_n"), 16)
            act.wait_ge(sem("out0"), 16 * OUT_C)
            for c in range(KE):
                if c % 2 == 0:
                    ada_row(24 + c)
                ps = await_bank(act, "z", c)
                ac(a_sz[:, c, :], ps[:, 0:T], ACT.Silu).then_inc(read("z"), 1)
                if c % 2:
                    ada_row(24 + c)
            for s in range(40, 48):
                ada_row(s)

            def layer_norm(n, l, i, after):
                for k in range(KD):
                    act.wait_ge(read("mean"), KD * n + k + 1)
                    ac(hT[:, k, :], xT[:, k, :], ACT.Square).then_inc(sem("sq_ready"), 1)
                act.wait_ge(read("var"), n + 1)
                ac(l_rs, l_v, ACT.Sqrt).then_inc(sem("ln_sqrt"), 1)
                for k in range(KD):
                    act.wait_ge(sem("xn_ready"), KD * n + k + 1)
                    ins = ac(xT[:, k, :], xT[:, k, :], ACT.Identity, bias=ln_b(l, i, k))
                    if after is None:
                        ins.then_inc(sem("x_final"), 1)
                    else:
                        link(ins)
                        modulate(*after, k)

            def moe(l):
                L = f"_{l}"
                act.wait_ge(sem("route_a"), 2 * l + 1)
                ac(r_eg, r_eg, ACT.Exp).then_inc(sem("route_b"), 1)
                act.wait_ge(sem("route_a"), 2 * l + 2)
                ac(r_e2, r_e2, ACT.Exp).then_inc(sem("route_b"), 1)
                for n in range(2 * NT):
                    ps = await_bank(act, "ht", 2 * NT * l + n)
                    ac(m_h[:, n // 2, 512 * (n % 2):512 * (n % 2) + 512], ps[:, :], ACT.Copy).then_inc(read("ht"), 1)
                fill = sem("mfill" + L)

                def pair(p, first):
                    for u in (0, 1):
                        act.wait_ge(fill, p * 10 + (u + 1))
                        ac(m_hg[:, u, 0:512], banks[2 * u][:, :], ACT.Copy)
                        ac(m_hg[:, u, 512:1024], banks[2 * u + 1][:, :], ACT.Copy).then_inc(sem("mT_read" + L), 1)
                    for u in (0, 1):
                        act.wait_ge(fill, p * 10 + (4 + 2 * u))
                        ac(m_sg[:, u, :], banks[4 + u][:, 0:2 * CH], ACT.Silu).then_inc(sem("mgate_read" + L), 1)
                    for u in (0, 1):
                        if not first:
                            act.wait_ge(sem(f"mout{u}" + L), p * 16)
                        for m in (0, 1):
                            act.wait_ge(fill, p * 10 + (7 + 2 * u + m))
                            ac(m_o[:, u, 512 * m:512 * m + 512], banks[(6, 2)[u] + m][0:CH, :],
                               ACT.Copy).then_inc(sem("mdn_read" + L), 1)
                        act.wait_ge(sem("mdn_read" + L), p * 4 + (2 * u + 2))
                        q = p * 2 + u
                        out = yg[CH * q:CH * q + CH, :] if first else yg[bass.ds(q * CH, CH), :]
                        act.dma_start(out, m_o[:, u, :]).then_inc(sem(f"mout{u}" + L), 16)

                act.wait_ge(sem("cleared"), 32)
                act.wait_ge(sem("planned"), l + 1)
                pairs = act.value_load(plan[0:1, 2 * MAXP:2 * MAXP + 1], min_val=MINP, max_val=MAXP)
                pair(0, True)
                with act.Fori(1, pairs) as p:
                    pair(p, False)
                for u in range(2):
                    act.wait_ge(sem(f"mout{u}" + L), pairs * 16)
                ac(m_mark, ident[:, 0:1], ACT.Copy).then_inc(sem("results_out"), 1)

            act.wait_ge(sem("mod_ready"), 2)
            layer_norm(0, 0, 0, (0, 24, False))
            moe(0)
            act.wait_ge(sem("mod_ready"), 3)
            layer_norm(1, 0, 1, (1, 0, True))

            ac(a_neg[:, :], a_log[:, :], ACT.Exp).then_inc(sem("dt_a"), 1)
            act.wait_ge(sem("dt_x"), 1)
            link(ac(b_u, b_u, ACT.Exp))
            ac(b_l, b_u, ACT.Ln, bias=1.0).then_inc(sem("dt_ln"), 1)
            act.wait_ge(sem("pads"), 2)

            def b_silu(c):
                out, w = (b_bc[:, c, :], 16 + c) if c < 8 else (b_xs[:, c - 8, :], c - 8)
                act.wait_ge(sem("bconv_ready"), c + 1)
                cb = b_cbuf[:, c % 2, :]
                ac(out[:, 0:TP], cb[:, 0:TP], ACT.Silu, bias=b_cbias(w))
                ac(out[:, TP:T], cb[:, TP + 2 * PAD:], ACT.Silu, bias=b_cbias(w)).then_inc(sem("xs_ready"), 1)

            for c in range(24):
                ps = await_bank(act, "xbc", c)
                if c >= 4:
                    act.wait_ge(sem("bconv_ready"), c - 3)
                padded(b_pre[:, c % 4, :], ps, "xbc")
                if c:
                    b_silu(c - 1)
            b_silu(23)
            act.wait_ge(sem("acs_ready"), 1)
            ac(b_u[:, 0:TP], b_acs[:, 0:TP], ACT.Exp, bias=acs_end, scale=-1.0).then_inc(sem("wr_exp"), 1)
            ac(b_es[:, TP:T], b_acs[:, TP:T], ACT.Exp).then_inc(sem("es_exp"), 1)
            for c in range(8):
                ps = await_bank(act, "h0", c)
                ac(b_h0[:, c // 4, 512 * (c % 4):512 * (c % 4) + 512], ps[:, :], ACT.Copy).then_inc(read("h0"), 1)
            ps = await_bank(act, "Bt", 0)
            ac(b_Bt.rearrange("p g n -> p (g n)"), ps[:, :], ACT.Copy).then_inc(read("Bt"), 1)
            for c in range(KE):
                ps = await_bank(act, "xt", c)
                ac(b_x[:, :, P * c:P * c + P], v3(ps[:, 0:T], NT), ACT.Copy).then_inc(read("xt"), 1)
            for g in range(G):
                for d in range(2):
                    n = 2 * g + d
                    ps = await_bank(act, "sn", n)
                    if n >= 2:
                        act.wait_ge(sem(f"out{n % 2}"), 16 * (OUT_C + n // 2))
                    ac(b_st[:, n % 2, :], ps[:, :], ACT.Copy).then_inc(read("sn"), 1)
                    act.wait_ge(read("sn"), n + 1)
                    act.dma_start(o_["s"][0, 0, d, HG * g:HG * g + HG].rearrange("(k j) p n -> (j p) k n", j=2),
                                  v3(b_st[:, n % 2, :], 4)).then_inc(sem(f"out{n % 2}"), 16)
            for g in range(G):
                if g >= 2:
                    act.wait_ge(sem("w_ready"), 2 * HG * (g - 1))
                ps = await_bank(act, "cbP", g)
                ac(b_cb[:, g % 2, 0:P], ps[:, 0:P], ACT.Copy).then_inc(read("cbP"), 1)
                ps = await_bank(act, "cbS", g)
                ac(b_cb[:, g % 2, P:5 * P], ps[:, :], ACT.Copy).then_inc(read("cbS"), 1)
                for u in range(2 * HG):
                    act.wait_ge(read("acsb"), 2 * HG * g + u + 1)
                    e = b_E[:, (u // 2) % 2, u % 2, :]
                    ac(e, e, ACT.Exp).then_inc(sem("be_ready"), 1)
                    for c in ([u // 4 - 1] if u % 4 == 1 and u > 4 else [3] if u == 2 * HG - 1 else []):
                        z_tile = 4 * g + c
                        ps = await_bank(act, "zb", z_tile)
                        ac(b_z[:, z_tile, :], ps[:, 0:T], ACT.Silu).then_inc(read("zb"), 1)
            for c in range(KE):
                act.wait_ge(sem("g_ready"), c + 1)
                ac(b_sq[:, c, :], b_xs[:, c, :], ACT.Square).then_inc(sem("gsq_ready"), 1)
                ac(b_xs[:, c, :], b_xs[:, c, :], ACT.Copy, scale=b_nw(c)).then_inc(sem("gB_ready"), 1)
            act.wait_ge(read("msq"), 1)
            ac(l_rs, l_v, ACT.Sqrt).then_inc(sem("rms_sqrt"), 1)
            layer_norm(2, 1, 0, (1, 24, False))
            moe(1)
            layer_norm(3, 1, 1, None)
            for t in range(NT):
                for m in range(2):
                    n = 2 * t + m
                    ps = await_bank(act, "out", n)
                    if n >= 2:
                        act.wait_ge(sem(f"out{n % 2}"), 16 * (OUT_C + OUT_S + n // 2))
                    ac(y_out[:, n % 2, :], ps[:, :], ACT.Copy).then_inc(read("out"), 1)
                    act.wait_ge(read("out"), n + 1)
                    dst = o_["yp"][0] if t == 0 else o_["ys"][0, P * t - P:P * t]
                    act.dma_start(dst[:, 512 * m:512 * m + 512], y_out[:, n % 2, :]).then_inc(sem(f"out{n % 2}"), 16)
            act.wait_ge(sem("out_m"), 16)
            act.wait_ge(sem("out_n"), 16)
            for s in range(2):
                act.wait_ge(sem(f"out{s}"), 16 * (OUT_C + OUT_S + NT))

        @block.vector
        def _(dve):
            ve = nc.vector
            n_link = [0]

            def step(ins):
                n_link[0] += 1
                ins.then_inc(sem("dve_step"), 1)

            def settle():
                dve.wait_ge(sem("dve_step"), n_link[0])

            def link(ins):
                step(ins)
                settle()

            for i in range(5):
                ps = await_bank(dve, "par", i)
                ve.tensor_copy(par[:, i, 0:PROWS[i]], ps[:, 0:PROWS[i]]).then_inc(read("par"), 1)

            def ada(part, l, j0, j1):
                ps = await_bank(dve, "mod", part)
                bias = par[:, 0, 48 * l + j0:48 * l + j1].unsqueeze(2).to_broadcast([P, j1 - j0, 2])
                ve.tensor_tensor(out=mod[:, l, j0:j1, :], in0=ps[:, 2 * j0:2 * j1].rearrange("p (j v) -> p j v", v=2),
                                 in1=bias, op=ALU.add).then_inc(read("mod"), 1)
                dve.wait_ge(read("mod"), part + 1)
                for s in (8, 32):
                    if j0 <= s < j1:
                        last = ve.tensor_scalar(mod[:, l, s:s + 8, :], mod[:, l, s:s + 8, :], 1.0, None, ALU.add)
                last.then_inc(sem("mod_ready"), 1)

            dve.wait_ge(read("par"), 5)
            ada(0, 0, 0, 16)

            def conv(c, src, dst, w, ready):
                last = ve.tensor_scalar(dst, src[:, 0:W_PAD - 2 * PAD], w(0), None, ALU.mult)
                for j in range(1, TAPS):
                    link(last)
                    last = ve.scalar_tensor_tensor(out=dst, in0=src[:, j:j + W_PAD - 2 * PAD], scalar=w(j), in1=dst,
                                                   op0=ALU.mult, op1=ALU.add)
                last.then_inc(sem(ready), 1)

            for c in range(KE):
                dve.wait_ge(read("xu"), c + 1)
                if c >= 2:
                    dve.wait_ge(sem("xc_ready"), c - 1)
                conv(c, a_xu[:, c, :], a_cbuf[:, c % 2, :], lambda j: a_cw(j, c), "conv_ready")
            ada(1, 0, 16, 48)
            for c in range(KE):
                ps = await_bank(dve, "kT", c)
                ve.tensor_copy(a_kT[:, c, :], ps[:, 0:T]).then_inc(read("kT"), 1)
                ps = await_bank(dve, "v", c)
                ve.tensor_copy(a_v[:, :, P * c:P * c + P], v3(ps[:, 0:T], NT)).then_inc(read("v"), 1)
            ps = await_bank(dve, "gates", 0)
            ve.tensor_copy(sm[:, 0:48], ps[:, 0:48]).then_inc(read("gates"), 1)
            for kind in range(4):
                ps = await_bank(dve, "grow", kind)
                ve.tensor_scalar(a_rowG[:, kind, :], ps[0:H, 0:T], b_gates[:, kind:kind + 1], None,
                                 ALU.add).then_inc(read("grow"), 1)
            dve.wait_ge(read("grow"), 4)
            ig, fg = a_rowG[:, 0:4:2, :], a_rowG[:, 1:4:2, :]
            ve.scalar_tensor_tensor(out=a_u, in0=fg, scalar=-1.0, in1=fg, op0=ALU.mult,
                                    op1=ALU.min).then_inc(sem("gate_x"), 1)
            dve.wait_ge(sem("gate_ln"), 1)
            link(ve.scalar_tensor_tensor(out=a_lf, in0=fg, scalar=0.0, in1=a_u, op0=ALU.min, op1=ALU.subtract))

            def both_ways(f):
                for d in range(2):
                    for v, (t0, t1) in enumerate(STREAMS):
                        view = (lambda ap, t0=t0, t1=t1: ap[:, t0:t1]) if d == 0 else \
                            (lambda ap, t0=t0, t1=t1: ap[:, t0:t1][:, ::-1])
                        step(f(d, v, view, t1 - t0))
                settle()

            both_ways(lambda d, v, view, n: ve.tensor_tensor_scan(
                out=view(a_b[:, d]), data0=ones[0:H, 0:1].to_broadcast([H, n]), data1=view(a_lf[:, d]), initial=0.0,
                op0=ALU.mult, op1=ALU.add))
            link(ve.tensor_tensor(out=a_a, in0=ig, in1=a_b, op=ALU.subtract))
            both_ways(lambda d, v, view, n: ve.tensor_tensor_scan(
                out=view(a_nM[:, d]), data0=view(a_a[:, d]), data1=view(a_a[:, d]),
                initial=m0[:, d:d + 1] if v else 0.0, op0=ALU.max, op1=ALU.max))
            step(ve.memset(a_wi[:, :, 0:TP], 0.0))
            for d in range(2):
                end = TP - 1 if d == 0 else 0
                step(ve.tensor_tensor(out=m_new[:, d:d + 1], in0=a_b[:, d, end:end + 1], in1=a_nM[:, d, end:end + 1],
                                      op=ALU.add))
            link(ve.scalar_tensor_tensor(out=a_fl, in0=a_nM, scalar=-1.0, in1=a_b, op0=ALU.mult, op1=ALU.subtract))
            ve.tensor_scalar(a_nM, a_nM, -1.0, None, ALU.mult).then_inc(sem("gate_m"), 1)

            ps = await_bank(dve, "col", 0)
            link(ve.tensor_scalar(c_wi.rearrange("p t d h -> p (t d h)"), ps[:, 32:48], DH ** -0.5, None, ALU.mult))
            step(ve.tensor_copy(c_nM.rearrange("p t d h -> p (t d h)"), ps[:, 0:24]))
            step(ve.tensor_copy(c_wk, ps[:, 72:80]))
            ve.tensor_copy(c_fl.rearrange("p t d h -> p (t d h)"), ps[:, 48:72]).then_inc(read("col"), 1)
            dve.wait_ge(read("col"), 1)
            settle()

            TILES = ((0, 0, P), (1, P, TS), (2, P + TS, TS))

            def strip(d, t):
                s = (strip_f, strip_b)[d]
                return s[:, P:2 * P] if t == 0 else s[:, P:3 * P] if t == 1 else s[:, 0:2 * P]

            def weights(h):
                E = a_E[:, h % 2]
                if h >= 2:
                    dve.wait_ge(filled, group["pTP", h - 2][1])
                for d in range(2):
                    ps = await_bank(dve, "abc", 2 * h + d)
                    for t, o, n in TILES:
                        src = ps[:, 0:TP] if t == 0 else ps[:, TP:T]
                        ins = ve.scalar_tensor_tensor(out=E[:, d, o:o + n], in0=src, scalar=c_nM[:, t, d, h:h + 1],
                                                      in1=strip(d, t), op0=ALU.add, op1=ALU.min)
                    ins.then_inc(read("abc"), 1)
                for t, o, n in TILES:
                    b = await_bank(dve, "scP" if t == 0 else "scS", h)
                    src = b[:, 0:TP] if t == 0 else b[:, TS * (t - 1):TS * t]
                    for d in range(2):
                        if t == 0:
                            dve.wait_ge(sem("e_ready"), 2 * h + d + 1)
                        ins = ve.scalar_tensor_tensor(out=E[:, d, o:o + n], in0=src, scalar=DH ** -0.5,
                                                      in1=E[:, d, o:o + n], op0=ALU.mult, op1=ALU.mult,
                                                      accum_out=den[:, 2 * t + d:2 * t + d + 1])
                        if d and t == 0:
                            ins.then_inc(read("scP"), 1)
                        elif d and t == 2:
                            ins.then_inc(read("scS"), 1)
                dve.wait_ge(read("scS"), h + 1)
                dve.wait_ge(read("scP"), h + 1)
                ps = await_bank(dve, "qn", h)
                wi = c_wi[:, :, :, h]
                ve.tensor_tensor(out=qn.rearrange("p (t d) -> p t d", d=2), in0=ps[:, 0:4].rearrange("p (t d) -> p t d", d=2),
                                 in1=wi, op=ALU.mult).then_inc(read("qn"), 1)
                dve.wait_ge(read("qn"), h + 1)
                settle()
                link(ve.tensor_tensor(out=den[:, 2:6], in0=den[:, 2:6], in1=qn, op=ALU.add))
                link(ve.scalar_tensor_tensor(out=den[:, :], in0=den[:, :], scalar=-1.0, in1=den[:, :], op0=ALU.mult,
                                             op1=ALU.max))
                link(ve.tensor_tensor(out=den.rearrange("p (t d) -> p t d", d=2),
                                      in0=den.rearrange("p (t d) -> p t d", d=2), in1=c_fl[:, :, :, h], op=ALU.max))
                link(ve.reciprocal(rden, den))
                ve.tensor_tensor(out=cwt[:, h, :].rearrange("p (t d) -> p t d", d=2),
                                 in0=rden[:, 2:6].rearrange("p (t d) -> p t d", d=2), in1=wi,
                                 op=ALU.mult).then_inc(sem("cw_ready"), 1)
                for t, o, n in TILES:
                    ins = ve.tensor_scalar(E[:, 0, o:o + n], E[:, 0, o:o + n], rden[:, 2 * t:2 * t + 1], None, ALU.mult)
                link(ins)
                for t, o, n in TILES:
                    ins = ve.scalar_tensor_tensor(out=E[:, 0, o:o + n], in0=E[:, 1, o:o + n],
                                                  scalar=rden[:, 2 * t + 1:2 * t + 2], in1=E[:, 0, o:o + n],
                                                  op0=ALU.mult, op1=ALU.add)
                ins.then_inc(sem("p_ready"), 1)

            weights(0)
            for h in range(H):
                if h + 1 < H:
                    weights(h + 1)
                dve.wait_ge(sem("cw_ready"), h + 1)
                for t in range(2):
                    dve.wait_ge(read("qc0"), 2 * h + t + 1)
                    ps = await_bank(dve, "qc1", 2 * h + t)
                    ve.scalar_tensor_tensor(out=a_tmp[:, t, :], in0=ps[:, :], scalar=cw(h, t, 1), in1=a_tmp[:, t, :],
                                            op0=ALU.mult, op1=ALU.add).then_inc(read("qc1"), 1)
                ps = await_bank(dve, "kt", h)
                if h:
                    dve.wait_ge(filled, group["nn", h - 1][1])
                for d in range(2):
                    ve.tensor_scalar(a_kw[:, d, :], ps[:, :], c_wk[:, 4 * d + h:4 * d + h + 1], None,
                                     ALU.mult).then_inc(read("kt"), 1)
                for t in range(NT):
                    ps = await_bank(dve, "pv", NT * h + t)
                    out = a_h[:, t, DH * h:DH * h + DH]
                    if t == 0:
                        ve.tensor_copy(out, ps[:, :]).then_inc(read("pv"), 1)
                    else:
                        dve.wait_ge(read("qc1"), 2 * h + t)
                        ve.tensor_tensor(out=out, in0=ps[:, :], in1=a_tmp[:, t - 1, :], op=ALU.add).then_inc(read("pv"), 1)
                for t in range(NT):
                    dve.wait_ge(read("pv"), NT * h + t + 1)
                    link(ve.bn_stats(bst[:, 0:6], a_h[:, t, DH * h:DH * h + DH]))
                    link(ve.bn_aggr(h_mv[:, NT * h + t, :], bst[:, 0:6]))
                ps = await_bank(dve, "nn", h)
                ve.tensor_copy(nT[:, :, h, :], ps[:, 0:8].rearrange("p (d j) -> p d j", d=2)).then_inc(read("nn"), 1)
            ve.tensor_scalar(h_rs, h_mv[:, :, 1], EPS, None, ALU.add).then_inc(sem("hvar_ready"), 1)
            ps = await_bank(dve, "nrow", 0)
            ve.tensor_copy(nrow[:, :], ps[0:32, 0:P]).then_inc(read("nrow"), 1)
            dve.wait_ge(sem("hsqrt"), 1)
            link(ve.reciprocal(h_rs, h_rs))
            for h in range(H):
                for t in range(NT):
                    n = NT * h + t
                    hh = a_h[:, t, DH * h:DH * h + DH]
                    ve.tensor_scalar(hh, hh, h_mv[:, n, 0:1], h_rs[:, n:n + 1], ALU.subtract,
                                     ALU.mult).then_inc(sem("hn_ready"), 1)
            dve.wait_ge(sem("skip_ready"), KE)
            for c in range(KE):
                ps = await_bank(dve, "hn", c)
                xc = a_xc[:, c, :]
                ve.scalar_tensor_tensor(out=xc, in0=ps[:, 0:T], scalar=a_nw(c), in1=xc, op0=ALU.mult,
                                        op1=ALU.add).then_inc(read("hn"), 1)
                dve.wait_ge(read("hn"), c + 1)
                dve.wait_ge(read("z"), c + 1)
                ve.tensor_tensor(out=xc, in0=xc, in1=a_sz[:, c, :], op=ALU.mult).then_inc(sem("gA_ready"), 1)

            def residual(l, gate, m, src, stage, buf, permuted=False):
                for v, (t0, t1) in enumerate(STREAMS):
                    out, s = buf[:, t0:t1], src[:, t0:t1]
                    if permuted and v:
                        out = out.rearrange("p (r w) -> p r w", r=ROWS)
                        s = s.rearrange("p (w r) -> p r w", r=ROWS)
                    ins = ve.tensor_scalar(out, s, mod[:, l, gate + m, v:v + 1], None, ALU.mult)
                if stage is None:
                    link(ins)
                else:
                    ins.then_inc(read(stage), 1)
                    dve.wait_ge(read(stage), (KD * l if stage == "yt" else 0) + m + 1)
                ve.scalar_tensor_tensor(out=xT[:, m, :], in0=xT[:, m, :], scalar=ALPHA, in1=buf, op0=ALU.mult,
                                        op1=ALU.add).then_inc(sem("r_ready"), 1)

            def layer_norm(n, l, i):
                ps = await_bank(dve, "mean", n)
                dve.wait_ge(sem("r_ready"), KD * n + KD)
                for k in range(KD):
                    ve.tensor_tensor(out=xT[:, k, :], in0=xT[:, k, :], in1=ps[:, 0:T],
                                     op=ALU.subtract).then_inc(read("mean"), 1)
                ps = await_bank(dve, "var", n)
                ve.tensor_scalar(l_v, ps[:, 0:T], EPS, None, ALU.add).then_inc(read("var"), 1)
                dve.wait_ge(sem("ln_sqrt"), n + 1)
                dve.wait_ge(read("mean"), KD * n + KD)
                dve.wait_ge(sem("sq_ready"), KD * n + KD)
                link(ve.reciprocal(l_rs, l_rs))
                for k in range(KD):
                    ve.scalar_tensor_tensor(out=xT[:, k, :], in0=xT[:, k, :], scalar=ln_w(l, i, k), in1=l_rs,
                                            op0=ALU.mult, op1=ALU.mult).then_inc(sem("xn_ready"), 1)

            def bc(ap, n):
                return ap.unsqueeze(len(ap.shape)).to_broadcast(list(ap.shape) + [n])

            rk = rank[:, :].unsqueeze(1).to_broadcast([P, NT, 4])

            def first_max(src, mx, out, tmp):
                link(ve.tensor_reduce(mx, src, X, ALU.max))
                link(ve.tensor_tensor(out=tmp, in0=src, in1=bc(mx, 4), op=ALU.is_equal))
                link(ve.tensor_tensor(out=tmp, in0=tmp, in1=rk, op=ALU.mult))
                link(ve.tensor_reduce(r_mp, tmp, X, ALU.max))
                link(ve.tensor_tensor(out=out, in0=tmp, in1=bc(r_mp, 4), op=ALU.is_equal))

            def moe(l):
                L = f"_{l}"
                ps = await_bank(dve, "route", l)
                ve.tensor_copy(m_L.rearrange("p t c -> p (t c)"), ps[:, 0:60]).then_inc(read("route"), 1)
                dve.wait_ge(read("route"), l + 1)
                lg, le = m_L[:, :, 0:4], m_L[:, :, 4:20].rearrange("p t (g e) -> p t g e", g=NG)
                first_max(lg, r_mx, r_ohg, r_t4)
                ve.tensor_tensor(out=r_eg, in0=lg, in1=bc(r_mx, 4), op=ALU.subtract).then_inc(sem("route_a"), 1)
                for t in range(NT):
                    ins = (ve.tensor_tensor(out=r_t16[:, t], in0=le[:, t], in1=bc(r_ohg[:, t], 4), op=ALU.mult))
                link(ins)
                link(ve.tensor_reduce(r_sel, r_t16.rearrange("p t g e -> p t e g"), X, ALU.add))
                first_max(r_sel, r_m1, r_oh1, r_t4)
                link(ve.scalar_tensor_tensor(out=r_sel, in0=r_oh1, scalar=-BIG, in1=r_sel, op0=ALU.mult, op1=ALU.add))
                first_max(r_sel, r_m2, r_oh2, r_t4)
                ve.tensor_tensor(out=r_e2, in0=r_m2, in1=r_m1, op=ALU.subtract).then_inc(sem("route_a"), 1)
                for i, oh in enumerate((r_oh1, r_oh2)):
                    for t in range(NT):
                        ins = ve.tensor_tensor(out=m_F[:, i, t, :].rearrange("p (g e) -> p g e", g=NG),
                                               in0=bc(r_ohg[:, t], 4), in1=oh[:, t].unsqueeze(1).to_broadcast([P, NG, NE]),
                                               op=ALU.mult)
                link(ins)
                ve.tensor_tensor(out=m_A, in0=m_F[:, 0], in1=m_F[:, 1], op=ALU.add).then_inc(sem("chosen"), 1)
                ps = await_bank(dve, "count", l)
                ve.tensor_copy(m_sl.rearrange("p t e -> p (t e)"), ps[:, 0:48])
                ve.tensor_copy(m_cnt, ps[:, 48:64]).then_inc(read("count"), 1)
                dve.wait_ge(read("count"), l + 1)
                link(ve.tensor_scalar(m_n, m_cnt, 0.0, None, ALU.is_gt))
                for j in range(1, T // CH):
                    link(ve.scalar_tensor_tensor(out=m_n, in0=m_cnt, scalar=float(CH * j), in1=m_n, op0=ALU.is_gt,
                                                 op1=ALU.add))
                link(ve.tensor_tensor_scan(out=m_end, data0=ones[:, 0:1].to_broadcast([P, NEXP]), data1=m_n,
                                           initial=0.0, op0=ALU.mult, op1=ALU.add))
                link(ve.tensor_tensor(out=m_base, in0=m_end, in1=m_n, op=ALU.subtract))
                for t in range(NT):
                    ins = ve.scalar_tensor_tensor(out=m_sl[:, t, :], in0=m_base, scalar=float(CH), in1=m_sl[:, t, :],
                                                  op0=ALU.mult, op1=ALU.add)
                link(ins)
                for i in range(2):
                    ins = ve.tensor_tensor(out=m_F[:, i], in0=m_F[:, i], in1=m_sl, op=ALU.mult)
                link(ins)
                for i in range(2):
                    ins = ve.tensor_reduce(m_sf[:, i, :], m_F[:, i], X, ALU.add)
                link(ins)
                ve.tensor_copy(slots[:, :], m_sf.rearrange("p i t -> p (i t)")).then_inc(sem("slots_ready"), 1)
                link(ve.tensor_tensor(out=m_cmp, in0=m_end[0:1, :].unsqueeze(1).to_broadcast([1, 2 * MAXP, NEXP]),
                                      in1=bc(chunk_no[:, :], NEXP), op=ALU.is_le))
                link(ve.tensor_reduce(m_eq, m_cmp, X, ALU.add))
                link(ve.tensor_scalar(m_eq, m_eq, float(NEXP - 1), None, ALU.min))
                ve.tensor_copy(plan[0:1, 0:2 * MAXP], m_eq)
                even = chunk_no[:, :].rearrange("o (p u) -> o p u", u=2)[:, :, 0]
                link(ve.tensor_tensor(out=m_cmp[:, 0, 0:MAXP] if MAXP <= NEXP else None, in0=even,
                                      in1=m_end[0:1, NEXP - 1:NEXP].to_broadcast([1, MAXP]), op=ALU.is_lt))
                link(ve.tensor_reduce(m_eq[:, 0:1], m_cmp[:, 0, 0:MAXP], X, ALU.add))
                ve.tensor_copy(plan[0:1, 2 * MAXP:2 * MAXP + 1], m_eq[:, 0:1]).then_inc(sem("planned"), 1)

                dve.wait_ge(sem("route_b"), 2 * l + 2)
                link(ve.tensor_reduce(r_gs, r_eg, X, ALU.add))
                link(ve.scalar_tensor_tensor(out=r_w1, in0=r_e2, scalar=1.0, in1=r_gs, op0=ALU.add, op1=ALU.mult))
                link(ve.reciprocal(r_w1, r_w1))
                link(ve.tensor_tensor(out=r_w2, in0=r_w1, in1=r_e2, op=ALU.mult))

                def pair(p, first):
                    for u in (0, 1):
                        dve.wait_ge(sem("mgate_read" + L), p * 2 + (u + 1))
                        dve.wait_ge(sem("mfill" + L), p * 10 + (4 + 2 * u))
                        ve.tensor_tensor(out=m_a[:, u].rearrange("p f c -> p (f c)"), in0=m_sg[:, u, :],
                                         in1=banks[4 + u][:, 2 * CH:4 * CH], op=ALU.mult).then_inc(sem("mup_read" + L), 1)

                pairs = dve.value_load(plan[0:1, 2 * MAXP:2 * MAXP + 1], min_val=MINP, max_val=MAXP)
                pair(0, True)
                with dve.Fori(1, pairs) as p:
                    pair(p, False)
                for t in range(NT):
                    dve.wait_ge(sem(f"gathered{t}"), 32 * (l + 1))
                    link(ve.tensor_scalar(m_y[:, 0, t, :], m_y[:, 0, t, :], r_w1[:, t:t + 1], None, ALU.mult))
                    ve.scalar_tensor_tensor(out=m_y[:, 0, t, :], in0=m_y[:, 1, t, :], scalar=r_w2[:, t:t + 1],
                                            in1=m_y[:, 0, t, :], op0=ALU.mult, op1=ALU.add).then_inc(sem("moe_sum"), 1)
                for m in range(KD):
                    if m >= 2:
                        dve.wait_ge(sem("r_ready"), (2 * l + 1) * KD + m - 1)
                    residual(l, 40, m, await_bank(dve, "yt", KD * l + m)[:, 0:T], "yt", l_t[:, m % 2, :])

            dve.wait_ge(sem("out_n"), 16)
            for m in range(KD):
                if m >= 2:
                    dve.wait_ge(sem("r_ready"), m - 1)
                residual(0, 16, m, await_bank(dve, "yA", m)[:, 0:T], "yA", l_t[:, m % 2, :])
            ada(2, 1, 0, 48)
            layer_norm(0, 0, 0)
            moe(0)
            layer_norm(1, 0, 1)

            ps = await_bank(dve, "dt", 0)
            ve.tensor_scalar(b_dt, ps[0:64, 0:T], dt_bias[:, :], None, ALU.add).then_inc(read("dt"), 1)
            dve.wait_ge(read("dt"), 1)
            ve.scalar_tensor_tensor(out=b_u, in0=b_dt, scalar=-1.0, in1=b_dt, op0=ALU.mult,
                                    op1=ALU.min).then_inc(sem("dt_x"), 1)
            dve.wait_ge(sem("dt_ln"), 1)
            link(ve.tensor_scalar(b_es, b_u, 1.0, None, ALU.add))
            link(ve.tensor_scalar(b_eq, b_es, 1.0, None, ALU.is_equal))
            step(ve.scalar_tensor_tensor(out=b_es, in0=b_es, scalar=-1.0, in1=b_eq, op0=ALU.add, op1=ALU.add))
            link(ve.tensor_tensor(out=b_l, in0=b_l, in1=b_eq, op=ALU.add))
            link(ve.reciprocal(b_es, b_es))
            link(ve.tensor_tensor(out=b_l, in0=b_l, in1=b_es, op=ALU.mult))
            link(ve.tensor_tensor(out=b_l, in0=b_l, in1=b_u, op=ALU.mult))
            link(ve.scalar_tensor_tensor(out=b_dt, in0=b_dt, scalar=0.0, in1=b_l, op0=ALU.max, op1=ALU.add))
            dve.wait_ge(sem("dt_a"), 1)
            link(ve.tensor_scalar(b_l, b_dt, a_neg[:, :], -1.0, ALU.mult, ALU.mult))
            for d in range(2):
                q = slice(32 * d, 32 * d + 32)
                for t0, t1 in STREAMS:
                    view = (lambda ap: ap[q, t0:t1]) if d == 0 else (lambda ap: ap[q, t0:t1][:, ::-1])
                    step(ve.tensor_tensor_scan(out=view(b_acs), data0=ones[q, 0:1].to_broadcast([32, t1 - t0]),
                                               data1=view(b_l), initial=0.0, op0=ALU.mult, op1=ALU.add))
            settle()
            for d in range(2):
                q = slice(32 * d, 32 * d + 32)
                end = TP - 1 if d == 0 else 0
                ins = ve.tensor_copy(acs_end[q, :], b_acs[q, end:end + 1])
            ins.then_inc(sem("acs_ready"), 1)
            link(ve.tensor_copy(ident_b, ident[0:64, 0:64]))
            link(ve.tensor_copy(b_l, b_acs))
            for i in range(3):
                link(ve.tensor_copy(acs_parts[:, i, :], b_l))
                if i < 2:
                    link(ve.tensor_tensor(out=b_l, in0=b_l, in1=acs_parts[:, i, :], op=ALU.subtract))

            def rows_done():
                dve.wait_ge(sem("wr_exp"), 1)
                dve.wait_ge(sem("es_exp"), 1)
                ve.tensor_tensor(out=b_es[:, 0:TP], in0=b_u[:, 0:TP], in1=b_dt[:, 0:TP],
                                 op=ALU.mult).then_inc(sem("brows_ready"), 1)

            for c in range(24):
                w = 16 + c if c < 8 else c - 8
                dve.wait_ge(read("xbc"), c + 1)
                if c >= 2:
                    dve.wait_ge(sem("xs_ready"), c - 1)
                conv(c, b_pre[:, c % 4, :], b_cbuf[:, c % 2, :], lambda j: b_cw(j, w), "bconv_ready")
            rows_done()
            ps = await_bank(dve, "bcol0", 0)
            step(ve.tensor_scalar(b_col[:, 0:192], ps[:, 0:192], -1.0, None, ALU.mult))
            ve.tensor_copy(b_col[:, 192:384], ps[:, 192:384]).then_inc(read("bcol0"), 1)
            ps = await_bank(dve, "bcol1", 0)
            step(ve.tensor_copy(b_col[:, 512:576], ps[:, 0:64]))
            ve.tensor_copy(b_col[:, 384:512], ps[:, 64:192]).then_inc(read("bcol1"), 1)
            dve.wait_ge(read("bcol0"), 1)
            dve.wait_ge(read("bcol1"), 1)
            settle()
            nacs = lambda t, r: b_col[:, 64 * t + r:64 * t + r + 1]
            dtc = lambda t, r: b_col[:, 192 + 64 * t + r:193 + 64 * t + r]

            for g in range(G):
                dve.wait_ge(read("cbP"), g + 1)
                dve.wait_ge(read("cbS"), g + 1)

                def segments(d):
                    cb = b_cb[:, g % 2, :]
                    if d == 0:
                        return ((0, 0, P, 0, strip_b[:, P:2 * P], cb[:, 0:P]),
                                (1, P, 2 * P, TP, strip_b[:, P:3 * P], cb[:, P:3 * P]),
                                (2, 3 * P, P, 2 * P, strip_b[:, P:2 * P], cb[:, 4 * P:5 * P]))
                    return ((0, 0, P, 0, strip_f[:, P:2 * P], cb[:, 0:P]),
                            (1, P, P, TP, strip_f[:, P:2 * P], cb[:, P:2 * P]),
                            (2, 2 * P, 2 * P, TP, strip_f[:, 0:2 * P], cb[:, 3 * P:5 * P]))

                def args(u):
                    hh, d = divmod(u, 2)
                    n = 2 * HG * g + u
                    if n >= 4:
                        dve.wait_ge(filled, group["w_used", n - 4])
                    r = 32 * d + HG * g + hh
                    ps = await_bank(dve, "acsb", n)
                    for t, o, w, s0, mask, _ in segments(d):
                        ins = ve.scalar_tensor_tensor(out=b_E[:, hh % 2, d, o:o + w], in0=ps[:, s0:s0 + w],
                                                      scalar=nacs(t, r), in1=mask, op0=ALU.add, op1=ALU.min)
                    ins.then_inc(read("acsb"), 1)

                args(0)
                args(1)
                for u in range(2 * HG):
                    if u + 2 < 2 * HG:
                        args(u + 2)
                    hh, d = divmod(u, 2)
                    r = 32 * d + HG * g + hh
                    dve.wait_ge(sem("be_ready"), 2 * HG * g + u + 1)
                    for t, o, w, _, _, cbs in segments(d):
                        e = b_E[:, hh % 2, d, o:o + w]
                        ins = ve.scalar_tensor_tensor(out=e, in0=e, scalar=dtc(t, r), in1=cbs, op0=ALU.mult,
                                                      op1=ALU.mult)
                    ins.then_inc(sem("w_ready"), 1)
                ps = await_bank(dve, "y0", g)
                if g == 0:
                    for s in range(2):
                        dve.wait_ge(sem(f"out{s}"), 16 * (OUT_C + OUT_S))
                ve.tensor_copy(b_y[:, 0, 512 * g:512 * g + 512], ps[:, :]).then_inc(read("y0"), 1)
                for d in range(2):
                    for t in (1, 2):
                        n = 4 * g + 2 * d + t - 1
                        ps = await_bank(dve, "inter", n)
                        c0 = 384 + 64 * (t - 1) + 32 * d + HG * g
                        out = b_t[:, t - 1, :] if d == 0 else b_t2[:, t - 1, :]
                        ve.tensor_tensor(out=out.rearrange("p (h c) -> p h c", h=HG),
                                         in0=ps[:, :].rearrange("p (h c) -> p h c", h=HG),
                                         in1=bc(b_col[:, c0:c0 + HG], PH), op=ALU.mult).then_inc(read("inter"), 1)
                dve.wait_ge(read("inter"), 4 * g + 4)
                for t in (1, 2):
                    step(ve.tensor_tensor(out=b_t[:, t - 1, :], in0=b_t[:, t - 1, :], in1=b_t2[:, t - 1, :], op=ALU.add))
                settle()
                for t in (1, 2):
                    ps = await_bank(dve, f"y{t}", g)
                    ve.tensor_tensor(out=b_y[:, t, 512 * g:512 * g + 512], in0=ps[:, :], in1=b_t[:, t - 1, :],
                                     op=ALU.add).then_inc(read(f"y{t}"), 1)
            for c in range(KE):
                ps = await_bank(dve, "yT", c)
                xs = b_xs[:, c, :]
                ve.scalar_tensor_tensor(out=xs, in0=xs, scalar=d_skip[:, c:c + 1], in1=ps[:, 0:T], op0=ALU.mult,
                                        op1=ALU.add).then_inc(read("yT"), 1)
                dve.wait_ge(read("yT"), c + 1)
                dve.wait_ge(read("zb"), c + 1)
                ve.tensor_tensor(out=xs, in0=xs, in1=b_z[:, c, :], op=ALU.mult).then_inc(sem("g_ready"), 1)
            ps = await_bank(dve, "msq", 0)
            ve.tensor_scalar(l_v, ps[:, 0:T], float(D) / E2, EPS, ALU.mult, ALU.add).then_inc(read("msq"), 1)
            dve.wait_ge(sem("rms_sqrt"), 1)
            link(ve.reciprocal(l_rs, l_rs))
            for m in range(KD):
                ps = await_bank(dve, "yB", m)
                if m >= 2:
                    dve.wait_ge(sem("r_ready"), 2 * KD + m - 1)
                ve.tensor_tensor(out=b_t[:, m % 2, 0:T], in0=ps[:, 0:T], in1=l_rs, op=ALU.mult).then_inc(read("yB"), 1)
                dve.wait_ge(read("yB"), m + 1)
                residual(1, 16, m, b_t[:, m % 2, 0:T], None, l_t[:, m % 2, :], permuted=True)
            layer_norm(2, 1, 0)
            moe(1)
            layer_norm(3, 1, 1)


_INS = ["x_prompt", "x_sample", "state_mlstm_C", "state_mlstm_n", "state_mlstm_m", "state_ssd", "c", "c_ctx",
        "ada_w", "ada_b", "ln_w", "ln_b", "a_w_in", "a_conv_w", "a_conv_b", "a_w_q", "a_w_k", "a_w_v", "a_w_gates",
        "a_b_gates", "a_norm_w", "a_skip", "a_w_down", "b_w_in", "b_conv_w", "b_conv_b", "b_dt_bias", "b_a_log",
        "b_d_skip", "b_norm_w", "b_w_out", "moe_w_rg", "moe_b_rg", "moe_w_re", "moe_b_re", "moe_w_gate",
        "moe_w_up", "moe_w_down"]
_OUTS = {"yp": (1, TP, D), "ys": (1, TS, D), "C": (1, 1, 2, H, DH, DH), "n": (1, 1, 2, H, DH), "m": (1, 1, 2, H),
         "s": (1, 1, 2, G * HG, PH, P)}


def kernel(**inputs):
    import numpy as np
    import concourse.bacc as bacc
    from concourse.bass_utils import run_bass_kernel_spmd

    nc = bacc.Bacc("TRN2", target_bir_lowering=False, num_devices=1)
    arrays, ins, outs = {}, {}, {}
    for name in _INS:
        a = np.ascontiguousarray(inputs[name])
        arrays["in_" + name] = a
        ins[name] = nc.dram_tensor("in_" + name, a.shape, mybir.dt.from_np(a.dtype), kind="ExternalInput").ap()
    for name, shape in _OUTS.items():
        outs[name] = nc.dram_tensor("out_" + name, shape, F32, kind="ExternalOutput").ap()
    program(nc, ins, outs)
    r = run_bass_kernel_spmd(nc, [arrays], core_ids=[0]).results[0]
    return tuple(r["out_" + name] for name in _OUTS)
```

```python
from contextlib import ExitStack

import concourse.bass as bass
from concourse import mybir

F32 = mybir.dt.float32
ALU = mybir.AluOpType
ACT = mybir.ActivationFunctionType
X = mybir.AxisListType.X

P = 128
TP, TS = 128, 256
T = TP + TS
NT = T // P
STREAMS = ((0, TP), (TP, T))
D = 1024
KD = D // P
E2 = 2048
KE = E2 // P
DEPTH = 2
ALPHA = (2.0 * DEPTH) ** 0.25
EPS = 1e-5
TAPS = 5
PAD = TAPS // 2
W_PAD = T + 4 * PAD
H = 4
DH = E2 // H
KH = DH // P
G = 4
HG = 8
PH = 64
GRID = 64
ROWS = TS // GRID
NG = 4
NE = 4
NEXP = NG * NE
BIG = 1e30
FF = 256
CH = 128
MAXQ = (2 * T + NG * NE * (CH - 1)) // CH
MAXP = (MAXQ + 1) // 2
MINP = T // CH
RING = 6
ARENA = 37120
SLAB = 1024


def program(nc, i_, o_):
    ctx = ExitStack()
    with ctx:
        def sb(name, cols, parts=P):
            return ctx.enter_context(nc.sbuf_tensor(name, [parts, cols], F32))

        sems = {}

        def sem(name):
            if name not in sems:
                sems[name] = ctx.enter_context(nc.semaphore(name))
            return sems[name]

        banks = [ctx.enter_context(nc.psum_tensor(f"bank{b}", [P, 512], F32)) for b in range(8)]

        OUT_C, OUT_S = H * KH, G
        SMALL = 16 * 24

        def v3(ap, n):
            return ap.rearrange("p (n c) -> p n c", n=n)

        def v4(ap, a, b):
            return ap.rearrange("p (a b c) -> p a b c", a=a, b=b)

        xT = v3(sb("xT", KD * T)[:, :], KD)
        hT = v3(sb("hT", KD * T)[:, :], KD)
        ring = sb("ring", RING * SLAB)
        par = v3(sb("par", 5 * P)[:, :], 5)
        mod = sb("mod", DEPTH * 48 * 2)[:, :].rearrange("p (l j v) -> p l j v", l=DEPTH, v=2)
        csil = sb("csil", 2 * KD + 30)
        pick = sb("pick", 32)
        ident = sb("ident", P)
        ones = sb("ones", P)
        ones_d = sb("ones_d", P)
        strip_f = sb("strip_f", 3 * P)
        strip_b = sb("strip_b", 3 * P)
        gates_w = sb("gates_w", (3 * KE + 1) * 16)
        route_all = sb("route_w", DEPTH * KD * 20 + 12)
        route_w = route_all[:, 0:DEPTH * KD * 20].rearrange("p (l k c) -> p l k c", l=DEPTH, k=KD)
        route_b = sb("route_b", DEPTH * 20, 1)
        b_gates = sb("b_gates", 4, H)
        m0 = sb("m0", 2, H)
        m_new = sb("m_new", 2, H)
        dt_bias = sb("dt_bias", 1, 64)
        a_log = sb("a_log", 1, 64)
        a_neg = sb("a_neg", 1, 64)
        d_skip = sb("d_skip", KE)
        rank = sb("rank", 4)
        before = sb("before", P)
        chunk_no = sb("chunk_no", 2 * MAXP, 1)
        slots = ctx.enter_context(nc.sbuf_tensor("slots", [P, 2 * NT], mybir.dt.uint32))
        plan = ctx.enter_context(nc.sbuf_tensor("plan", [1, 2 * MAXP + 1], mybir.dt.int32))
        xg = nc.dram_tensor("xg", [2 * MAXP * CH, D], F32, kind="Internal").ap()
        yg = nc.dram_tensor("yg", [2 * MAXP * CH, D], F32, kind="Internal").ap()
        sm = sb("sm", 308)
        nT = sm[:, 128:160].rearrange("p (d h j) -> p d h j", d=2, h=H)
        c_wi = sm[:, 160:176].rearrange("p (t d h) -> p t d h", t=2, d=2)
        c_nM = sm[:, 176:200].rearrange("p (t d h) -> p t d h", t=NT, d=2)
        c_fl = sm[:, 200:224].rearrange("p (t d h) -> p t d h", t=NT, d=2)
        c_wk = sm[:, 224:232]
        h_bias = sm[:, 0:2 * KD].rearrange("p (k v) -> p k v", v=2)
        ln_ab = sm[:, 2 * KD:3 * KD]
        eps = sm[:, 3 * KD:3 * KD + 1]
        den, rden, qn = sm[:, 232:238], sm[:, 238:244], sm[:, 244:248]
        cwt = v3(sm[:, 248:264], H)
        cw = lambda h, t, d: cwt[:, h, 2 * t + d:2 * t + d + 1]
        bst = sm[:, 264:270]
        h_mv = v3(sm[:, 270:294], NT * H)
        h_rs = sm[:, 294:306]
        acs_end = sm[0:64, 306:307]

        arena = sb("arena", ARENA)
        at = [0]

        def region(cols, start=None):
            if start is not None:
                at[0] = start
            a = at[0]
            at[0] += cols
            assert at[0] <= ARENA, at[0]
            return arena[:, a:a + cols], a

        a_xc, _ = region(KE * T, 0)
        a_xc = v3(a_xc, KE)
        xu_r, xu_at = region(KE * W_PAD)
        a_xu = v3(xu_r, KE)
        q_r, _ = region(KE * T)
        a_qT = v3(q_r, KE)
        a_sz = v3(q_r, KE)
        k_r, _ = region(KE * T)
        a_kT = v3(k_r, KE)
        v_r, _ = region(NT * E2)
        a_v = v3(v_r, NT)
        scan_at = at[0]
        e_r, _ = region(2 * 2 * 5 * P)
        a_E = v4(e_r, 2, 2)
        a_pT, _ = region(5 * P)
        a_tmp = v3(region(2 * 512)[0], 2)
        a_kw = v3(region(2 * 512)[0], 2)
        a_cst = v3(region(2 * 512)[0], 2)
        a_cbuf = v3(region(2 * (W_PAD - 2 * PAD), scan_at)[0], 2)
        a_vb = v3(region(2 * T)[0], 2)
        a_bd = region(2 * 3 * P)[0].rearrange("p (s q b c) -> p s q b c", s=2, q=3, c=4)
        a_wq = region(3 * KE * 4)[0].rearrange("p (q k c) -> p q k c", q=3, k=KE)
        blockmask, _ = region(P)
        zeros = a_cst[:, 1, 0:256]
        ada_rows = v3(a_cst[:, 0, :], 2)
        nrow = e_r[0:32, 0:P]
        a_h = v3(region(NT * E2, xu_at)[0], NT)
        a_rowG = v3(region(4 * T, xu_at)[0][0:H, :], 4)
        a_u = v3(region(2 * T)[0][0:H, :], 2)
        a_lf = v3(region(2 * T)[0][0:H, :], 2)
        a_b = v3(region(2 * T)[0][0:H, :], 2)
        a_nM = v3(region(2 * T)[0][0:H, :], 2)
        a_wi = v3(region(2 * T)[0][0:H, :], 2)
        a_fl = v3(region(2 * T)[0][0:H, :], 2)
        a_a = v3(gates_w[0:H, 0:2 * T], 2)
        a_grow = a_cbuf[0:96, 0, 0:T]
        prow = v3(region(5 * P, scan_at)[0], 5)
        x_tok = v3(region(NT * D, 0)[0], NT)

        b_xs = v3(region(KE * T, 0)[0], KE)
        b_bc = v3(region(2 * G * T)[0], 2 * G)
        bx_r, _ = region(NT * E2)
        b_x = v3(bx_r, NT)
        b_sq = v3(bx_r, KE)
        _, y_at = region(NT * E2)
        b_h0 = v3(region(2 * E2)[0], 2)
        z_r, z_at = region(KE * T)
        b_z = v3(z_r, KE)
        b_acs = region(T)[0][0:64, :]
        b_col = region(9 * 64)[0]
        b_E = v4(region(4 * 512)[0], 2, 2)
        b_cb = v3(region(2 * 5 * P)[0], 2)
        b_t = v3(region(2 * 512)[0], 2)
        b_inter = region(2 * 2 * 512, y_at + 2 * P * KD)[0].rearrange("p (g t c) -> p g t c", g=2, t=2)
        acs_parts = v3(gates_w[0:64, 0:3 * T // 2].bitcast(mybir.dt.bfloat16), 3)
        ident_b = gates_w[0:64, 3 * T // 2:3 * T // 2 + 32].bitcast(mybir.dt.bfloat16)
        b_pre = v3(region(4 * W_PAD, y_at)[0], 4)
        b_cbuf = v3(region(2 * (W_PAD - 2 * PAD))[0], 2)
        b_dt, b_u, b_l, b_eq, b_es = (region(T)[0][0:64, :] for _ in range(5))
        b_Bt = v3(region(G * P)[0], G)
        b_part = region(512)[0]
        b_wx = v3(region(2 * E2 // G, y_at)[0], 2)
        b_st = v3(region(2 * 512)[0], 2)

        m_h = v3(region(NT * D, 0)[0], NT)
        m_w = v3(region(6 * KD * FF)[0], 6)
        m_xc = v3(region(2 * D)[0][0:CH, :], 2)
        m_hg = region(2 * KD * CH)[0].rearrange("p (u c) -> p u c", u=2)
        m_sg = v3(region(2 * 2 * CH)[0], 2)
        m_a = region(4 * CH)[0].rearrange("p (u f c) -> p u f c", u=2, f=2)
        m_o = v3(region(2 * D)[0][0:CH, :], 2)
        m_y = region(2 * NT * D)[0].rearrange("p (i t c) -> p i t c", i=2, t=NT)
        m_rows = m_y[:, 0, 0, 0:T]
        m_L = v3(region(NT * 20)[0], NT)
        m_F = region(2 * NT * 16)[0].rearrange("p (i t e) -> p i t e", i=2, t=NT)
        m_A = v3(region(NT * 16)[0], NT)
        m_sl = v3(region(NT * 16)[0], NT)
        m_cnt, m_n, m_end, m_base = (region(16)[0] for _ in range(4))
        m_cmp = v3(region(2 * MAXP * 16)[0][0:1, :], 2 * MAXP)
        m_eq = region(2 * MAXP)[0][0:1, :]
        m_even = region(MAXP)[0][0:1, :]
        m_sf = v3(region(2 * NT)[0], 2)
        r_mx, r_mp, r_m1, r_m2, r_gs, r_w1, r_w2, r_e2 = (region(NT)[0] for _ in range(8))
        r_eg, r_ohg, r_t4, r_sel, r_oh1, r_oh2 = (v3(region(NT * 4)[0], NT) for _ in range(6))
        r_t16 = v4(region(NT * 16)[0], NT, NG)
        m_mark = region(1)[0]
        l_v = region(T, 30000)[0]
        l_rs = region(T)[0]
        y_out = v3(region(2 * 512)[0], 2)

        ada_b = lambda l, j: par[:, 0, 48 * l + j:48 * l + j + 1]
        a_cw = lambda j, c: par[:, 1, 16 * j + c:16 * j + c + 1]
        a_cb = lambda c: par[:, 1, 80 + c:81 + c]
        a_nw = lambda c: par[:, 1, 96 + c:97 + c]
        a_sk = lambda c: par[:, 1, 112 + c:113 + c]
        ln_w = lambda l, i, k: par[:, 2, 16 * l + 8 * i + k:16 * l + 8 * i + k + 1]
        ln_b = lambda l, i, k: par[:, 2, 32 + 16 * l + 8 * i + k:33 + 16 * l + 8 * i + k]
        b_cbias = lambda c: par[:, 2, 64 + c:65 + c]
        b_nw = lambda c: par[:, 2, 88 + c:89 + c]
        b_cw = lambda j, c: par[:, 3, 24 * j + c:24 * j + c + 1]
        n0T = par[:, 4, 0:32]
        PROWS = (112, 128, 104, 120, 32)

        slabs = []
        ada_w, a_in, a_dn, b_in, b_dn = i_["ada_w"], i_["a_w_in"], i_["a_w_down"], i_["b_w_in"], i_["b_w_out"]

        def add(kind, w, c0, quarters=(0, 1)):
            for q in quarters:
                slabs.append((kind, w[4 * q * P:4 * (q + 1) * P, c0:c0 + 256].rearrange("(k p) c -> p k c", p=P)))

        ada_at = [0]

        def add_ada(n):
            for _ in range(n):
                l, s = divmod(ada_at[0], 24)
                add("ada", ada_w[l], 256 * s)
                ada_at[0] += 1

        add_ada(8)
        for s in range(8):
            for q in range(2):
                add("xu", a_in[0], 256 * s, (q,))
                add_ada(1)
        for h in range(H):
            for d in range(2):
                C0 = i_["state_mlstm_C"][0, 0, d, h].rearrange("(k p) c -> p k c", p=P)
                slabs.append(("C0", C0[:, 0:2]))
                slabs.append(("C0", C0[:, 2:4]))
        for s in range(8):
            for q in range(2):
                add("z", a_in[0], E2 + 256 * s, (q,))
                add_ada(1)
        for s in range(4):
            for q in range(2):
                add("down", a_dn[0], 256 * s, (2 * q, 2 * q + 1))
                add_ada(1)
        moe_at = [len(slabs)]
        slabs.append(("dt", b_in[0][:, 5120:5184].rearrange("(k p) c -> p k c", p=P)))
        for s in range(8, 12):
            add("bc", b_in[0], E2 + 256 * s)
        for s in range(8):
            add("x", b_in[0], E2 + 256 * s)
        for d in range(2):
            h0 = i_["state_ssd"][0, 0, d].rearrange("(k j) p n -> (j p) k n", j=2)
            slabs.append(("h0", h0[:, 0:8]))
            slabs.append(("h0", h0[:, 8:16]))
        for s in range(8):
            add("zb", b_in[0], 256 * s)
        for s in range(4):
            add("out", b_dn[0], 256 * s, range(4))
        moe_at.append(len(slabs))

        def slot(n):
            return ring[:, (n % RING) * SLAB:(n % RING + 1) * SLAB]

        slab_in = [sem(f"slab_in{s}") for s in range(RING)]
        landed = [16 * (n // RING + 1) for n in range(len(slabs))]
        slab_free = {}

        filled = sem("filled")
        n_filled = [0]
        group = {}
        stage_n = {}
        occupant = [None] * 8
        next_bank = [0]
        ring_banks = [5]

        def read(stage):
            return sem(stage + "_read")

        def claim(pe, stage, bank=None, evictions=1, freed_at=None):
            k = stage_n.get(stage, 0)
            stage_n[stage] = k + 1
            if bank is None:
                bank = next_bank[0] % ring_banks[0]
                next_bank[0] += 1
            if occupant[bank]:
                pe.wait_ge(*occupant[bank])
            occupant[bank] = freed_at or (read(stage), evictions * (k + 1))
            return (stage, k, bank), banks[bank]

        def finish(ins, key=None):
            n_filled[0] += 1
            ins.then_inc(filled, 1)
            if key:
                group[key[:2]] = (key[2], n_filled[0])

        def await_bank(eng, stage, k):
            b, n = group[stage, k]
            eng.wait_ge(filled, n)
            return banks[b]

        block = ctx.enter_context(nc.Block())
        mm = nc.tensor.matmul

        @block.tensor
        def _(pe):
            n_slab = [0]

            def slab(kind):
                n = n_slab[0]
                assert slabs[n][0] == kind, (n, slabs[n][0], kind)
                n_slab[0] = n + 1
                pe.wait_ge(slab_in[n % RING], landed[n])
                return n, slot(n)

            def used(n):
                slab_free[n] = n_filled[0]

            ada_n = [0]
            mod_key = [None]

            def ada_turn():
                s = ada_n[0] - 1
                if s in (0, 8, 24):
                    mod_key[0] = claim(pe, "mod", bank=5)[0]
                pe.wait_ge(read("ada"), s + 1)
                for j in (0, 1):
                    c = 2 * (2 * (s % 24) + j)
                    last = mm(banks[5][:, c:c + 2], ada_rows[:, s % 2, P * j:P * j + P], pick[:, 0:2], start=True, stop=True)
                finish(last, mod_key[0] if s in (7, 23, 47) else None)
                group["turned", s] = n_filled[0]

            def ada_slab():
                if ada_n[0] not in (0, 8, 24):
                    ada_turn()
                ada_n[0] += 1
                key, ps = claim(pe, "ada", bank=7)
                for half in (0, 1):
                    n, w = slab("ada")
                    w = v3(w, 4)
                    for j in range(4):
                        k = 4 * half + j
                        last = mm(ps[32 * j:32 * j + 32, 0:256], csil[:, 2 * k:2 * k + 32], w[:, j, :],
                                  start=half == 0, stop=half == 1)
                    finish(last, key if half else None)
                    used(n)

            def project(stage, kind, ready, with_ada=False):
                keys = [claim(pe, stage) for _ in range(2)]
                for half in (0, 1):
                    n, w = slab(kind)
                    w = v3(w, 4)
                    for j in (0, 1):
                        for k in range(4):
                            ready(4 * half + k)
                            last = mm(keys[j][1][:, 0:T], w[:, k, P * j:P * j + P], hT[:, 4 * half + k, :],
                                      start=half == 0 and k == 0, stop=half == 1 and k == 3, skip_group_check=True)
                        if half or j:
                            finish(last, keys[j][0] if half else None)
                    used(n)
                    if with_ada:
                        ada_slab()

            def project_back(stage, kind, src, ready):
                for s in range(4):
                    keys = [claim(pe, stage, freed_at=(sem("r_ready"), 2 * s + j + 1) if stage == "yA" else None)
                            for j in range(2)]
                    for q in range(4):
                        n, w = slab(kind)
                        w = v3(w, 4)
                        for j in (0, 1):
                            for k in range(4):
                                ready(4 * q + k)
                                last = mm(keys[j][1][:, 0:T], w[:, k, P * j:P * j + P], src[:, 4 * q + k, :],
                                          start=q == 0 and k == 0, stop=q == 3 and k == 3, skip_group_check=True)
                            if q == 3 or j:
                                finish(last, keys[j][0] if q == 3 else None)
                        used(n)
                        if kind == "down" and q % 2:
                            ada_slab()

            def layer_norm(n):
                key, ps = claim(pe, "mean", evictions=KD)
                for k in range(KD):
                    pe.wait_ge(sem("r_ready"), KD * n + k + 1)
                    last = mm(ps[:, 0:T], ones_d[:, :], xT[:, k, :], start=k == 0, stop=k == KD - 1)
                finish(last, key)
                key, ps = claim(pe, "var")
                for k in range(KD):
                    pe.wait_ge(sem("sq_ready"), KD * n + k + 1)
                    last = mm(ps[:, 0:T], ones_d[:, :], hT[:, k, :], start=k == 0, stop=k == KD - 1)
                finish(last, key)

            def moe(l):
                L = f"_{l}"
                key, ps = claim(pe, "rows")
                for k in range(KD):
                    pe.wait_ge(sem("h_ready"), 8 * (2 * l + 1) + k + 1)
                    o, j = (KD * l + k) * 20, k % 4
                    last = mm(ps[32 * j:32 * j + 32, 0:T], route_all[:, o:o + 32], hT[:, k, :],
                              start=k < 4, stop=k >= 4)
                finish(last, key)
                pe.wait_ge(read("rows"), l + 1)
                key, ps = claim(pe, "route")
                for t in range(NT):
                    mm(ps[:, 20 * t:20 * t + 20], m_rows[:, P * t:P * t + P], pick[:, 0:20], start=True, stop=False)
                    last = mm(ps[:, 20 * t:20 * t + 20], ones[0:1, :], route_b[0:1, 20 * l:20 * l + 20],
                              start=False, stop=True)
                finish(last, key)
                for t in range(NT):
                    for m in range(2):
                        key, ps = claim(pe, "ht")
                        for i in range(4):
                            last = nc.tensor.transpose(ps[:, P * i:P * i + P], hT[:, 4 * m + i, P * t:P * t + P],
                                                       ident[:, :])
                        finish(last, key)
                pe.wait_ge(sem("chosen"), l + 1)
                key, ps = claim(pe, "count")
                for t in range(NT):
                    for r in range(t):
                        mm(ps[:, 16 * t:16 * t + 16], ones[:, :], m_A[:, r, :], start=r == 0, stop=False)
                    mm(ps[:, 16 * t:16 * t + 16], before[:, :], m_A[:, t, :], start=t == 0, stop=True)
                for r in range(NT):
                    last = mm(ps[:, 48:64], ones[:, :], m_A[:, r, :], start=r == 0, stop=r == NT - 1)
                finish(last, key)
                for b in range(8):
                    if occupant[b]:
                        pe.wait_ge(*occupant[b])
                        occupant[b] = None
                fill = sem("mfill" + L)

                def pair(p, first):
                    for u in (0, 1):
                        pe.wait_ge(sem(f"mx_in{u}" + L), p * 16 + 16)
                        if u and not first:
                            pe.wait_ge(sem("mdn_read" + L), p * 4)
                        mm(banks[2 * u][:, 0:CH], m_xc[:, u, 0:P], ident[0:CH, 0:CH])
                        for k in range(1, KD):
                            last = nc.tensor.transpose(banks[2 * u + k // 4][:, CH * (k % 4):CH * (k % 4) + CH],
                                                       m_xc[:, u, P * k:P * k + P], ident[0:CH, 0:CH])
                        last.then_inc(fill, 1)
                    for u in (0, 1):
                        pe.wait_ge(sem("mT_read" + L), p * 2 + (u + 1))
                        for s in (0, 1):
                            pe.wait_ge(sem(f"mw_in{3 * u + s}" + L), p * 16 + 16)
                            for j in (0, 1):
                                o = CH * (2 * s + j)
                                for k in range(KD):
                                    last = mm(banks[4 + u][:, o:o + CH],
                                              v3(m_w[:, 3 * u + s, :], KD)[:, k, P * j:P * j + P],
                                              m_hg[:, u, CH * k:CH * k + CH], start=k == 0, stop=k == KD - 1)
                            last.then_inc(fill, 1)
                    for u in (0, 1):
                        pe.wait_ge(sem(f"mw_in{3 * u + 2}" + L), p * 16 + 16)
                        pe.wait_ge(sem("mup_read" + L), p * 2 + (u + 1))
                        for m in (0, 1):
                            for f in (0, 1):
                                last = mm(banks[(6, 2)[u] + m][0:CH, :], m_a[:, u, f, :],
                                          v3(m_w[:, 3 * u + 2, :], 2)[:, f, 512 * m:512 * m + 512],
                                          start=f == 0, stop=f == 1)
                            last.then_inc(fill, 1)

                pe.wait_ge(sem("planned"), l + 1)
                pairs = pe.value_load(plan[0:1, 2 * MAXP:2 * MAXP + 1], min_val=MINP, max_val=MAXP)
                pair(0, True)
                with pe.Fori(1, pairs) as p:
                    pair(p, False)
                pe.wait_ge(sem("mT_read" + L), pairs * 2)
                pe.wait_ge(sem("mgate_read" + L), pairs * 2)
                pe.wait_ge(sem("mup_read" + L), pairs * 2)
                pe.wait_ge(sem("mdn_read" + L), pairs * 4)
                pe.wait_ge(sem("moe_sum"), NT * l + NT)
                for m in range(KD):
                    key, ps = claim(pe, "yt", freed_at=(sem("r_ready"), (2 * l + 1) * KD + m + 1))
                    for t in range(NT):
                        last = nc.tensor.transpose(ps[:, P * t:P * t + P], m_y[:, 0, t, P * m:P * m + P], ident[:, :])
                    finish(last, key)

            pe.wait_ge(sem("consts"), 1)
            pe.wait_ge(sem("prow_in"), 16 * 13)
            for i in range(5):
                key, ps = claim(pe, "par")
                finish(nc.tensor.transpose(ps[:, 0:PROWS[i]], prow[0:PROWS[i], i, :],
                                           ident[0:PROWS[i], 0:PROWS[i]]), key)
            pe.wait_ge(sem("x_in"), 32)
            for k in range(KD):
                key, ps = claim(pe, "xT")
                for t in range(NT):
                    last = nc.tensor.transpose(ps[:, P * t:P * t + P], x_tok[:, t, P * k:P * k + P], ident[:, :])
                finish(last, key)

            pe.wait_ge(sem("csil_ready"), 1)
            for _ in range(8):
                ada_slab()
            ada_turn()
            for s in range(8):
                project("xu", "xu", lambda k: pe.wait_ge(sem("h_ready"), k + 1) if s == 0 else None, True)
            ada_turn()
            ring_banks[0] = 6

            gkey, gps = claim(pe, "gates", bank=6)

            def gates(c):
                pe.wait_ge(read("qT"), c + 1)
                pe.wait_ge(read("kT"), c + 1)
                pe.wait_ge(read("vT"), c + 1)
                if c == 0:
                    pe.wait_ge(sem("small_in"), SMALL)
                for i, src in enumerate((a_qT[:, c, :], a_kT[:, c, :], a_vb[:, c % 2, :])):
                    last = mm(gps[32 * i:32 * i + 32, 0:T], gates_w[:, (KE * i + c) * 16:(KE * i + c + 2) * 16], src,
                              start=c == 0, stop=c == KE - 1)
                if c == KE - 1:
                    finish(last, gkey)
                key, ps = claim(pe, "v")
                for t in range(NT):
                    last = nc.tensor.transpose(ps[:, P * t:P * t + P], a_vb[:, c % 2, P * t:P * t + P], ident[:, :])
                finish(last, key)

            for c in range(KE):
                pe.wait_ge(sem("bd_ready"), c + 1)
                pe.wait_ge(sem("xc_ready"), c + 1)
                for i, st in enumerate(("qT", "kT", "vT")):
                    key, ps = claim(pe, st)
                    if i < 2:
                        rhs = a_xc[:, c, :]
                        last = mm(ps[:, 0:T], a_bd[:, c % 2, i].rearrange("p b c -> p (b c)"), rhs,
                                  start=True, stop=True)
                    else:
                        for (t0, t1), o in zip(STREAMS, (PAD, TP + 3 * PAD)):
                            last = mm(ps[:, t0:t1], a_bd[:, c % 2, i].rearrange("p b c -> p (b c)"),
                                      a_xu[:, c, o:o + t1 - t0], start=True, stop=True)
                    finish(last, key)
                if c:
                    gates(c - 1)
            gates(KE - 1)

            pe.wait_ge(read("gates"), 1)
            for kind in range(4):
                key, ps = claim(pe, "grow")
                finish(mm(ps[0:H, 0:T], pick[0:96, 4 * kind:4 * kind + 4], a_grow, start=True, stop=True), key)
            def decays(h):
                for d in range(2):
                    key, ps = claim(pe, "abc")
                    finish(mm(ps[:, 0:T], ident[0:H, h:h + 1].to_broadcast([H, P]), a_a[:, d, :],
                              start=True, stop=True), key)

            def scores(h):
                key, ps = claim(pe, "scP")
                for j in range(KH):
                    last = mm(ps[:, 0:TP], a_qT[:, KH * h + j, 0:TP], a_kT[:, KH * h + j, 0:TP],
                              start=j == 0, stop=j == KH - 1)
                finish(last, key)
                key, ps = claim(pe, "scS")
                for t in (1, 2):
                    for j in range(KH):
                        last = mm(ps[:, TS * (t - 1):TS * t], a_qT[:, KH * h + j, P * t:P * t + P],
                                  a_kT[:, KH * h + j, TP:T], start=j == 0, stop=j == KH - 1)
                finish(last, key)
                key, ps = claim(pe, "qn")
                for t in (1, 2):
                    for j in range(KH):
                        last = mm(ps[:, 2 * t - 2:2 * t], a_qT[:, KH * h + j, P * t:P * t + P],
                                  n0T[:, KH * h + j:32:16], start=j == 0, stop=j == KH - 1)
                finish(last, key)

            scores(0)
            pe.wait_ge(sem("rows_ready"), 1)
            key, ps = claim(pe, "col")
            for q, src in enumerate((a_nM, a_wi, a_fl)):
                for t in range(NT):
                    for d in range(2):
                        o = ((q * NT + t) * 2 + d) * 4
                        nc.tensor.transpose(ps[:, o:o + 4], src[:, d, P * t:P * t + P], ident[0:H, 0:H])
            for d in range(2):
                last = nc.tensor.transpose(ps[:, 72 + 4 * d:76 + 4 * d], a_u[:, d, 0:P], ident[0:H, 0:H])
            finish(last, key)
            decays(0)
            for h in range(H):
                if h + 1 < H:
                    decays(h + 1)
                    scores(h + 1)
                for d in range(2):
                    keys = [claim(pe, f"qc{d}") for _ in range(2)]
                    for half in (0, 1):
                        n, w = slab("C0")
                        w = v3(w, 2)
                        for t in (1, 2):
                            for j in (0, 1):
                                last = mm(keys[t - 1][1][:, :], a_qT[:, KH * h + 2 * half + j, P * t:P * t + P], w[:, j, :],
                                          start=half == 0 and j == 0, stop=half == 1 and j == 1, skip_group_check=True)
                            if half or t == 2:
                                finish(last, keys[t - 1][0] if half else None)
                        used(n)
                pe.wait_ge(sem("p_ready"), h + 1)
                key, ps = claim(pe, "pTS")
                for t in range(2):
                    for r in range(2):
                        o = P * (2 * t + r)
                        e = P + TS * t + P * r
                        last = nc.tensor.transpose(ps[:, o:o + P], a_E[:, h % 2, 0, e:e + P],
                                                   ident[:, :])
                finish(last, key)
                key, ps = claim(pe, "pTP")
                finish(nc.tensor.transpose(ps[:, 0:P], a_E[:, h % 2, 0, 0:P], ident[:, :]), key)
                key, ps = claim(pe, "kt", evictions=2)
                for j in range(KH):
                    last = nc.tensor.transpose(ps[:, P * j:P * j + P], a_kT[:, KH * h + j, 0:TP], ident[:, :])
                finish(last, key)
                pe.wait_ge(read("pTS"), h + 1)
                pe.wait_ge(read("pTP"), h + 1)
                for t in range(NT):
                    key, ps = claim(pe, "pv")
                    rs = (0,) if t == 0 else (0, 1)
                    for r in rs:
                        lhs = a_pT[:, 4 * P:5 * P] if t == 0 else a_pT[:, P * (2 * t - 2 + r):P * (2 * t - 1 + r)]
                        last = mm(ps[:, :], lhs, a_v[:, 0 if t == 0 else 1 + r, DH * h:DH * h + DH],
                                  start=r == 0, stop=r == rs[-1])
                    finish(last, key)
                pe.wait_ge(read("kt"), 2 * h + 2)
                for d in range(2):
                    for j in range(KH):
                        key, ps = claim(pe, "cn")
                        finish(mm(ps[:, :], a_kw[:, d, P * j:P * j + P], a_v[:, 0, DH * h:DH * h + DH],
                                  start=True, stop=True), key)
                key, ps = claim(pe, "nn")
                for d in range(2):
                    for j in range(KH):
                        last = mm(ps[:, KH * d + j:KH * d + j + 1], a_kw[:, d, P * j:P * j + P], ones[:, 0:1],
                                  start=True, stop=True)
                finish(last, key)
            pe.wait_ge(read("nn"), H)
            key, ps = claim(pe, "nrow")
            finish(nc.tensor.transpose(ps[0:32, 0:P], sm[:, 128:160], ident[:, :]), key)

            ring_banks[0] = 5
            def head_back(c):
                key, ps = claim(pe, "hn")
                pe.wait_ge(sem("hn_ready"), NT * (c // KH + 1))
                for t in range(NT):
                    last = nc.tensor.transpose(ps[:, P * t:P * t + P], a_h[:, t, P * c:P * c + P], ident[:, :])
                finish(last, key)

            for s in range(8):
                project("z", "z", lambda k: None, True)
                if s:
                    head_back(2 * s - 2)
                    head_back(2 * s - 1)
            head_back(KE - 2)
            head_back(KE - 1)
            project_back("yA", "down", a_xc, lambda k: pe.wait_ge(sem("gA_ready"), k + 1))
            ada_turn()
            ring_banks[0] = 6
            layer_norm(0)
            moe(0)
            layer_norm(1)

            n, w = slab("dt")
            w = v3(w[:, 0:KD * 64], KD)
            key, ps = claim(pe, "dt")
            for k in range(KD):
                pe.wait_ge(sem("h_ready"), 16 + k + 1)
                last = mm(ps[0:64, 0:T], w[:, k, :], hT[:, k, :], start=k == 0, stop=k == KD - 1)
            finish(last, key)
            used(n)
            for s in range(4):
                project("xbc", "bc", lambda k: None)
            for s in range(8):
                project("xbc", "x", lambda k: None)
            for d in range(2):
                for half in (0, 1):
                    n, w = slab("h0")
                    for c2 in range(2):
                        key, ps = claim(pe, "h0")
                        for i in range(4):
                            c = 4 * c2 + i
                            last = nc.tensor.transpose(ps[:, P * i:P * i + P], w[:, P * c:P * c + P], ident[:, :])
                        finish(last, key)
                    used(n)
            pe.wait_ge(sem("brows_ready"), 1)
            key, ps = claim(pe, "bcol0")
            for t in range(NT):
                nc.tensor.transpose(ps[:, 64 * t:64 * t + 64], b_acs[:, P * t:P * t + P], ident[0:64, 0:64])
                last = nc.tensor.transpose(ps[:, 192 + 64 * t:256 + 64 * t], b_dt[:, P * t:P * t + P],
                                           ident[0:64, 0:64])
            finish(last, key)
            key, ps = claim(pe, "bcol1")
            for t in range(NT):
                last = nc.tensor.transpose(ps[:, 64 * t:64 * t + 64], b_es[:, P * t:P * t + P], ident[0:64, 0:64])
            finish(last, key)
            pe.wait_ge(sem("xs_ready"), 8)
            key, ps = claim(pe, "Bt")
            for g in range(G):
                last = nc.tensor.transpose(ps[:, P * g:P * g + P], b_bc[:, g, 0:TP], ident[:, :])
            finish(last, key)
            for c in range(KE):
                pe.wait_ge(sem("xs_ready"), 8 + c + 1)
                key, ps = claim(pe, "xt")
                for t in range(NT):
                    last = nc.tensor.transpose(ps[:, P * t:P * t + P], b_xs[:, c, P * t:P * t + P], ident[:, :])
                finish(last, key)
            pe.wait_ge(read("Bt"), 1)

            def new_state(n):
                g, d = divmod(n, 2)
                pe.wait_ge(sem("wx_ready"), n + 1)
                key, ps = claim(pe, "sn", bank=7)
                for i in range(4):
                    last = mm(ps[:, P * i:P * i + P], b_wx[:, d, P * i:P * i + P], b_Bt[:, g, :],
                              start=True, stop=True)
                finish(last, key)

            z_at_work = {}

            def z_part(n):
                c, part = divmod(n, 4)
                half = part // 2
                if part == 0:
                    z_at_work["key"] = claim(pe, "zb", bank=4)
                if c % 2 == 0 and part % 2 == 0:
                    z_at_work[half] = slab("zb")
                key, ps = z_at_work["key"]
                n_slab_z, w = z_at_work[half]
                for k in range(2 * part, 2 * part + 2):
                    last = mm(ps[:, 0:T], v3(w, 4)[:, k % 4, P * (c % 2):P * (c % 2) + P], hT[:, k, :],
                              start=k == 0, stop=k == KD - 1, skip_group_check=True)
                finish(last, key if part == 3 else None)
                if c % 2 and part % 2:
                    used(n_slab_z)

            def products(g, which, bank):
                key, ps = claim(pe, which, bank=bank)
                if which == "cbP":
                    last = mm(ps[:, 0:TP], b_bc[:, g, 0:TP], b_bc[:, G + g, 0:TP], start=True, stop=True)
                else:
                    for r in range(2):
                        last = mm(ps[:, TS * r:TS * r + TS], b_bc[:, g, TP + P * r:TP + P * r + P],
                                  b_bc[:, G + g, TP:T], start=True, stop=True)
                finish(last, key)

            def cached(g, i, bank):
                d, t = i // 2, i % 2 + 1
                key, ps = claim(pe, "inter", bank=bank)
                finish(mm(ps[:, :], b_bc[:, G + g, P * t:P * t + P], b_h0[:, d, 512 * g:512 * g + 512],
                          start=True, stop=True), key)

            def broadcast(n):
                head, d = divmod(n, 2)
                key, ps = claim(pe, "acsb", bank=n % 4)
                row = 32 * d + head
                for i in range(3):
                    last = mm(ps[:, 0:T], ident_b[:, row:row + 1].to_broadcast([64, P]), acs_parts[:, i, :],
                              start=i == 0, stop=i == 2)
                finish(last, key)

            products(0, "cbP", 7)
            products(0, "cbS", 6)
            for i in range(4):
                cached(0, i, 4 + i % 2)
            for n in range(3):
                broadcast(n)
            y_key = None
            for n in range(2 * G * HG):
                head, d = divmod(n, 2)
                g, hh = divmod(head, HG)
                if n + 3 < 2 * G * HG:
                    broadcast(n + 3)
                if n % 4 == 0:
                    y_key, y_ps = claim(pe, "y", bank=5 + n // 4 % 2)
                    pe.wait_ge(sem("inter_ready"), 2 * g + 2)
                    for t in (1, 2):
                        mm(y_ps[:, P * t:P * t + P], b_inter[:, g % 2, t - 1, PH * hh:PH * hh + P], ident[:, :],
                           start=t == 1, stop=False, skip_group_check=True)
                pe.wait_ge(sem("w_ready"), n + 1)
                rows = slice(PH * (head % 2), PH * (head % 2) + PH)
                for i, (q0, w, o, r) in enumerate((((0, P, 0, 0), (TP, 2 * P, P, 1), (TP + P, P, 3 * P, 2)),
                                                   ((0, P, 0, 0), (TP, P, P, 1), (TP, 2 * P, 2 * P, 2)))[d]):
                    last = mm(y_ps[rows, q0:q0 + w], b_x[:, r, PH * head:PH * head + PH],
                              b_E[:, hh % 2, d, o:o + w], start=False, stop=d == 1 and i != 1,
                              skip_group_check=True)
                finish(last, y_key if n % 4 == 3 else None)
                group["w_used", n] = n_filled[0]
                z_part(n)
                u = n % (2 * HG)
                if g + 1 < G:
                    if u in (1, 3, 5, 7):
                        cached(g + 1, u // 2, 7)
                    elif u == 9:
                        products(g + 1, "cbP", 7)
                    elif u == 12:
                        products(g + 1, "cbS", 7)
                elif u % 2:
                    new_state(u // 2)
            key, ps = claim(pe, "msq")
            for c in range(KE):
                pe.wait_ge(sem("gsq_ready"), c + 1)
                last = mm(ps[:, 0:T], ones_d[:, :], b_sq[:, c, :], start=c == 0, stop=c == KE - 1)
            finish(last, key)
            project_back("yB", "out", b_xs, lambda k: pe.wait_ge(sem("gB_ready"), k + 1))
            layer_norm(2)
            moe(1)
            layer_norm(3)
            for t in range(NT):
                for m in range(2):
                    pe.wait_ge(sem("x_final"), KD)
                    key, ps = claim(pe, "out")
                    for i in range(4):
                        last = nc.tensor.transpose(ps[:, P * i:P * i + P], xT[:, 4 * m + i, P * t:P * t + P],
                                                   ident[:, :])
                    finish(last, key)



        @block.sync
        def _(sp):
            sp.dma_start(x_tok[:, 0, :], i_["x_prompt"][0]).then_inc(sem("x_in"), 16)
            sp.dma_start(x_tok[:, 1:3, :], i_["x_sample"][0].rearrange("(t p) c -> p t c", p=P)).then_inc(sem("x_in"), 16)

            def moe(l):
                L = f"_{l}"
                wg = i_["moe_w_gate"][l].rearrange("g e k f -> (g e) k f")
                wu = i_["moe_w_up"][l].rearrange("g e k f -> (g e) k f")
                wd = i_["moe_w_down"][l].rearrange("g e f k -> (g e) f k")
                sp.wait_ge(sem("planned"), l + 1)
                pairs = sp.value_load(plan[0:1, 2 * MAXP:2 * MAXP + 1], min_val=MINP, max_val=MAXP)

                def pair(p, first):
                    def weights(u, s, w, n):
                        if not first:
                            sp.wait_ge(sem("mfill" + L), p * 10 + (n - 10))
                        src = w[bass.ds(experts[u], 1)].rearrange("o (k p) f -> p (o k) f", p=P)
                        sp.dma_start(v3(m_w[:, 3 * u + s, :], KD if s < 2 else 2), src).then_inc(
                            sem(f"mw_in{3 * u + s}" + L), 16)

                    order = ((0, 0, wg, 3), (0, 1, wu, 4), (1, 0, wg, 5), (1, 1, wu, 6), (0, 2, wd, 8), (1, 2, wd, 10))
                    experts = []
                    for u in (0, 1):
                        q = p * 2 + u
                        at = plan[0:1, q:q + 1] if first else plan[0:1, bass.ds(q, 1)]
                        experts.append(sp.value_load(at, min_val=0, max_val=NEXP - 1))
                    if first:
                        weights(*order[0])
                        weights(*order[1])
                    for u in (0, 1):
                        q = p * 2 + u
                        if not first:
                            sp.wait_ge(sem("mfill" + L), p * 10 + (u - 9))
                        elif u == 0:
                            sp.wait_ge(sem("scattered"), 16 * 2 * NT * (l + 1))
                        x = xg[CH * q:CH * q + CH, :] if first else xg[bass.ds(q * CH, CH), :]
                        sp.dma_start(m_xc[:, u, :], x).then_inc(sem(f"mx_in{u}" + L), 16)
                    for which in order[2 if first else 0:]:
                        weights(*which)

                pair(0, True)
                with sp.Fori(1, pairs) as p:
                    pair(p, False)

            sp.wait_ge(sem("prow_in"), 16 * 13)
            for n, (kind, src) in enumerate(slabs):
                for l in range(DEPTH):
                    if n == min(moe_at[l] + RING, len(slabs)):
                        moe(l)
                if n >= RING:
                    sp.wait_ge(filled, slab_free[n - RING])
                k, c = src.shape[1], src.shape[2]
                sp.dma_start(v3(slot(n)[:, 0:k * c], k), src).then_inc(slab_in[n % RING], 16)
            moe(1)

        @block.gpsimd
        def _(pool):
            pl = nc.gpsimd
            n_link = [0]

            def link(ins):
                n_link[0] += 1
                ins.then_inc(sem("pool_step"), 1)
                pool.wait_ge(sem("pool_step"), n_link[0])

            pl.memset(ones[:, :], 1.0)
            pl.memset(csil[:, 2 * KD:], 0.0)
            pl.memset(gates_w[:, 3 * KE * 16:], 0.0)
            pl.memset(route_all[:, DEPTH * KD * 20:], 0.0)
            pl.memset(ones_d[:, :], 1.0 / D)
            pl.memset(zeros[:, :], 0.0)
            pl.memset(before[:, :], 1.0)
            pl.memset(eps, EPS)
            pl.iota(chunk_no[:, :], pattern=[[1, 2 * MAXP]], base=0, channel_multiplier=0,
                    allow_small_or_imprecise_dtypes=True)
            for j in range(4):
                pl.memset(rank[:, j:j + 1], float(4 - j))
            pl.memset(blockmask[:, :], 1.0)
            pl.memset(strip_f[:, :], 0.0)
            pl.memset(strip_b[:, :], 0.0)
            link(pl.memset(ident[:, :], 0.0))
            link(pl.affine_select(out=ident[:, :], in_=ident[:, :], compare_op=ALU.not_equal, fill=1.0, base=0,
                                  pattern=[[-1, P]], channel_multiplier=1))
            pl.affine_select(out=before[:, :], in_=before[:, :], compare_op=ALU.is_gt, fill=0.0, base=0,
                             pattern=[[1, P]], channel_multiplier=-1)
            pl.affine_select(out=strip_f[:, :], in_=strip_f[:, :], compare_op=ALU.is_ge, fill=-BIG, base=P,
                             pattern=[[-1, 3 * P]], channel_multiplier=1)
            pl.affine_select(out=strip_b[:, :], in_=strip_b[:, :], compare_op=ALU.is_ge, fill=-BIG, base=-P,
                             pattern=[[1, 3 * P]], channel_multiplier=-1)
            link(pl.tensor_tensor(out=pick[:, :], in0=ident[:, 0:32], in1=ident[:, 32:64], op=ALU.add))
            link(pl.tensor_tensor(out=pick[:, :], in0=pick[:, :], in1=ident[:, 64:96], op=ALU.add))
            pl.tensor_tensor(out=pick[:, :], in0=pick[:, :], in1=ident[:, 96:128], op=ALU.add)
            bm = blockmask[:, :].rearrange("p (b c) -> p b c", c=4)
            link(pl.affine_select(out=bm, in_=bm, compare_op=ALU.is_ge, fill=0.0, base=0,
                                  pattern=[[-4, 32], [0, 4]], channel_multiplier=1))
            link(pl.affine_select(out=bm, in_=bm, compare_op=ALU.is_ge, fill=0.0, base=3,
                                  pattern=[[4, 32], [0, 4]], channel_multiplier=-1))
            pl.memset(ones[:, 0:1], 1.0).then_inc(sem("consts"), 1)
            pl.memset(xu_r, 0.0).then_inc(sem("pads"), 1)

            small = []
            for q, name in enumerate(("a_w_q", "a_w_k", "a_w_v")):
                small.append((a_wq[:, q], i_[name][0].rearrange("(k b) c d -> (b c) k d", b=32)))
            small.append((gates_w[:, 0:3 * KE * 16].rearrange("p (k c) -> p k c", c=16),
                          i_["a_w_gates"][0].rearrange("(k p) c -> p k c", p=P)))
            small.append((b_gates[:, :], i_["a_b_gates"][0].rearrange("(k h) -> h k", h=H)))
            small.append((m0[:, :], i_["state_mlstm_m"][0, 0].rearrange("d h -> h d")))
            for l in range(DEPTH):
                small.append((route_w[:, l, :, 0:4], i_["moe_w_rg"][l].rearrange("(k p) c -> p k c", p=P)))
                for g in range(NG):
                    small.append((route_w[:, l, :, 4 + 4 * g:8 + 4 * g],
                                  i_["moe_w_re"][l, g].rearrange("(k p) c -> p k c", p=P)))
                small.append((route_b[:, 20 * l:20 * l + 4], i_["moe_b_rg"][l:l + 1]))
                small.append((route_b[:, 20 * l + 4:20 * l + 20],
                              i_["moe_b_re"][l:l + 1].rearrange("l g e -> l (g e)")))
            small.append((dt_bias[:, :], i_["b_dt_bias"][0].rearrange("d (h o) -> (d h) o", o=1)))
            small.append((a_log[:, :], i_["b_a_log"][0].rearrange("d (h o) -> (d h) o", o=1)))
            for j in range(2):
                small.append((d_skip[64 * j:64 * j + 64, :],
                              i_["b_d_skip"][0:1, j::2].to_broadcast([64, KE])))
            assert 16 * len(small) == SMALL
            pool.wait_ge(sem("mod_ready"), 1)
            for dst, src in small:
                pool.dma_start(dst, src, allow_slow_non_contiguous=True).then_inc(sem("small_in"), 16)

            pool.wait_ge(sem("small_in"), SMALL)
            for c in range(KE):
                if c >= 2:
                    pool.wait_ge(filled, group["vT", c - 2][1])
                for q in range(3):
                    ins = pl.tensor_tensor(out=a_bd[:, c % 2, q], in0=a_wq[:, q, c, :].unsqueeze(1).to_broadcast([P, 32, 4]),
                                           in1=bm, op=ALU.mult)
                ins.then_inc(sem("bd_ready"), 1)

            def moe(l):
                L = f"_{l}"
                pool.wait_ge(sem("slots_ready"), l + 1)
                pool.wait_ge(sem("cleared"), 32)
                for t in range(NT):
                    pool.wait_ge(read("ht"), 2 * NT * l + 2 * t + 2)
                    for i in range(2):
                        pool.indirect_dma_start(
                            out=xg[:, :], out_offset=bass.IndirectOffsetOnAxis(slots[:, NT * i + t:NT * i + t + 1], 0),
                            in_=m_h[:, t, :], in_offset=None).then_inc(sem("scattered"), 16)
                pool.wait_ge(sem("results_out"), l + 1)
                for t in range(NT):
                    for i in range(2):
                        pool.indirect_dma_start(
                            out=m_y[:, i, t, :], out_offset=None, in_=yg[:, :],
                            in_offset=bass.IndirectOffsetOnAxis(slots[:, NT * i + t:NT * i + t + 1], 0),
                        ).then_inc(sem(f"gathered{t}"), 16)

            pool.wait_ge(sem("h_ready"), 8)
            for rows in (xg, yg[2 * MINP * CH:, :]):
                pool.dma_start(rows.rearrange("(p a) (b c) -> p (a b) c", p=P, c=256),
                               zeros[:, :].unsqueeze(1).to_broadcast([P, rows.shape[0] // P * 4, 256])
                               ).then_inc(sem("cleared"), 16)
            moe(0)
            pool.wait_ge(sem("h_ready"), 17)
            pl.memset(b_pre.rearrange("p k t -> p (k t)"), 0.0).then_inc(sem("pads"), 1)
            pool.wait_ge(read("bcol1"), 1)
            for g in range(G):
                pool.wait_ge(read("xt"), 4 * g + 4)
                for d in range(2):
                    if g:
                        pool.wait_ge(filled, group["sn", 2 * (g - 1) + d][1])
                    pl.tensor_tensor(out=b_wx[:, d, :].rearrange("p (h c) -> p h c", h=HG),
                                     in0=b_x[:, 0, 512 * g:512 * g + 512].rearrange("p (h c) -> p h c", h=HG),
                                     in1=b_col[:, 512 + 32 * d + HG * g:512 + 32 * d + HG * g + HG]
                                     .unsqueeze(2).to_broadcast([P, HG, PH]), op=ALU.mult).then_inc(sem("wx_ready"), 1)
            moe(1)

        @block.scalar
        def _(act):
            ac = nc.scalar.activation
            n_link = [0]

            def link(ins):
                n_link[0] += 1
                ins.then_inc(sem("act_step"), 1)
                act.wait_ge(sem("act_step"), n_link[0])

            prows = (
                (0, 0, 96, i_["ada_b"].rearrange("l (j p) -> (l j) p", p=P)),
                (0, 96, 8, i_["c_ctx"].rearrange("(j p) -> j p", p=P)),
                (0, 104, 8, i_["c"].rearrange("o (j p) -> (o j) p", p=P)),
                (1, 0, 80, i_["a_conv_w"][0].rearrange("w (j p) -> (w j) p", p=P)),
                (1, 80, 16, i_["a_conv_b"].rearrange("o (j p) -> (o j) p", p=P)),
                (1, 96, 16, i_["a_norm_w"].rearrange("o (j p) -> (o j) p", p=P)),
                (1, 112, 16, i_["a_skip"].rearrange("o (j p) -> (o j) p", p=P)),
                (2, 0, 32, i_["ln_w"].rearrange("l i (j p) -> (l i j) p", p=P)),
                (2, 32, 32, i_["ln_b"].rearrange("l i (j p) -> (l i j) p", p=P)),
                (2, 64, 24, i_["b_conv_b"].rearrange("o (j p) -> (o j) p", p=P)),
                (2, 88, 16, i_["b_norm_w"].rearrange("o (j p) -> (o j) p", p=P)),
                (3, 0, 120, i_["b_conv_w"][0].rearrange("w (j p) -> (w j) p", p=P)),
                (4, 0, 32, i_["state_mlstm_n"][0, 0].rearrange("d h (j p) -> (d h j) p", p=P)),
            )
            for tile, r0, n, src in prows:
                act.dma_start(prow[r0:r0 + n, tile, :], src).then_inc(sem("prow_in"), 16)

            act.wait_ge(read("par"), 1)
            ac(csil[:, 0:2 * KD].rearrange("p (k v) -> p v k", v=2), par[:, 0, 96:112].rearrange("p (v k) -> p v k", v=2),
               ACT.Silu).then_inc(sem("csil_ready"), 1)
            for k in range(KD):
                ps = await_bank(act, "xT", k)
                ac(xT[:, k, :], ps[:, 0:T], ACT.Copy).then_inc(read("xT"), 1)

            def modulate(l, shift, permuted, k, bias):
                for v, (t0, t1) in enumerate(STREAMS):
                    out, src = hT[:, k, t0:t1], xT[:, k, t0:t1]
                    if permuted and v:
                        out = out.rearrange("p (w r) -> p r w", r=ROWS)
                        src = src.rearrange("p (r w) -> p r w", r=ROWS)
                    last = ac(out, src, ACT.Identity, bias=bias(k, v),
                              scale=mod[:, l, shift + 8 + k, v:v + 1])
                last.then_inc(sem("h_ready"), 1)

            def ada_row(s):
                ps = await_bank(act, "ada", s)
                if s >= 2:
                    act.wait_ge(filled, group["turned", s - 2])
                ac(ada_rows[:, s % 2, :], ps[:, 0:256], ACT.Copy).then_inc(read("ada"), 1)

            for s in range(8):
                ada_row(s)
            act.wait_ge(sem("mod_ready"), 1)
            act.wait_ge(read("xT"), KD)
            for k in range(KD):
                modulate(0, 0, False, k, lambda k, v: mod[:, 0, k, v:v + 1])
            for k in range(KD):
                act.wait_ge(sem("h_ready"), k + 1)
                ac(xT[:, k, :], xT[:, k, :], ACT.Copy, scale=ALPHA).then_inc(sem("x_scaled"), 1)

            act.wait_ge(sem("pads"), 1)

            def conv_silu(c, cbuf, bias, out, ready):
                act.wait_ge(sem("conv_ready"), c + 1)
                ac(out[:, 0:TP], cbuf[:, 0:TP], ACT.Silu, bias=bias)
                ac(out[:, TP:T], cbuf[:, TP + 2 * PAD:], ACT.Silu, bias=bias).then_inc(sem(ready), 1)

            def padded(dst, ps, stage):
                ac(dst[:, PAD:PAD + TP], ps[:, 0:TP], ACT.Copy)
                ac(dst[:, TP + 3 * PAD:T + 3 * PAD], ps[:, TP:T], ACT.Copy).then_inc(read(stage), 1)

            for c in range(KE):
                if c % 2 == 0:
                    ada_row(8 + c)
                padded(a_xu[:, c, :], await_bank(act, "xu", c), "xu")
                if c:
                    conv_silu(c - 1, a_cbuf[:, (c - 1) % 2, :], a_cb(c - 1), a_xc[:, c - 1, :], "xc_ready")
                if c % 2:
                    ada_row(8 + c)
            conv_silu(KE - 1, a_cbuf[:, (KE - 1) % 2, :], a_cb(KE - 1), a_xc[:, KE - 1, :], "xc_ready")

            for c in range(KE):
                ps = await_bank(act, "qT", c)
                ac(a_qT[:, c, :], ps[:, 0:T], ACT.Copy).then_inc(read("qT"), 1)
                ps = await_bank(act, "vT", c)
                if c >= 2:
                    act.wait_ge(filled, group["v", c - 2][1])
                ac(a_vb[:, c % 2, :], ps[:, 0:T], ACT.Copy).then_inc(read("vT"), 1)

            act.wait_ge(sem("gate_x"), 1)
            link(ac(a_u, a_u, ACT.Exp))
            ac(a_u, a_u, ACT.Ln, bias=1.0).then_inc(sem("gate_ln"), 1)
            for c in range(KE):
                ac(a_xc[:, c, :], a_xc[:, c, :], ACT.Copy, scale=a_sk(c)).then_inc(sem("skip_ready"), 1)
            act.wait_ge(sem("gate_m"), 1)
            for d in range(2):
                ac(a_wi[:, d, TP:T], a_nM[:, d, TP:T], ACT.Exp, bias=m0[:, d:d + 1])
                end = TP - 1 if d == 0 else 0
                ac(a_u[:, d, 0:TP], a_a[:, d, 0:TP], ACT.Exp, bias=a_nM[:, d, end:end + 1])
            ac(a_fl, a_fl, ACT.Exp).then_inc(sem("rows_ready"), 1)
            act.dma_start(o_["m"][0, 0].rearrange("d h -> h d"), m_new[:, :],
                          allow_slow_non_contiguous=True).then_inc(sem("out_m"), 16)

            def weights_exp(h):
                for d in range(2):
                    act.wait_ge(read("abc"), 2 * h + d + 1)
                    ac(a_E[:, h % 2, d, :], a_E[:, h % 2, d, :], ACT.Exp).then_inc(sem("e_ready"), 1)

            weights_exp(0)
            for h in range(H):
                if h + 1 < H:
                    weights_exp(h + 1)
                act.wait_ge(sem("cw_ready"), h + 1)
                if h:
                    act.wait_ge(read("pv"), NT * h)
                for t in range(2):
                    ps = await_bank(act, "qc0", 2 * h + t)
                    ac(a_tmp[:, t, :], ps[:, :], ACT.Copy, scale=cw(h, t, 0)).then_inc(read("qc0"), 1)
                if h:
                    act.wait_ge(filled, group["pv", NT * h - 1][1])
                ps = await_bank(act, "pTS", h)
                ac(a_pT[:, 0:4 * P], ps[:, :], ACT.Copy).then_inc(read("pTS"), 1)
                ps = await_bank(act, "pTP", h)
                ac(a_pT[:, 4 * P:5 * P], ps[:, 0:P], ACT.Copy).then_inc(read("pTP"), 1)
                for d in range(2):
                    for j in range(KH):
                        n = (2 * h + d) * KH + j
                        ps = await_bank(act, "cn", n)
                        if n == 1:
                            act.wait_ge(sem("cleared"), 32)
                        if n >= 2:
                            act.wait_ge(sem(f"out{n % 2}"), 16 * (n // 2))
                        ac(a_cst[:, n % 2, :], ps[:, :], ACT.Copy).then_inc(read("cn"), 1)
                        act.wait_ge(read("cn"), n + 1)
                        act.dma_start(o_["C"][0, 0, d, h, P * j:P * j + P, :],
                                      a_cst[:, n % 2, :]).then_inc(sem(f"out{n % 2}"), 16)
            act.wait_ge(sem("hvar_ready"), 1)
            ac(h_rs, h_rs, ACT.Sqrt).then_inc(sem("hsqrt"), 1)
            act.wait_ge(read("nrow"), 1)
            act.dma_start(o_["n"][0, 0].rearrange("d h (j p) -> (d h j) p", p=P), nrow[:, :]).then_inc(sem("out_n"), 16)
            act.wait_ge(sem("out0"), 16 * OUT_C)
            for c in range(KE):
                if c % 2 == 0:
                    ada_row(24 + c)
                ps = await_bank(act, "z", c)
                ac(a_sz[:, c, :], ps[:, 0:T], ACT.Silu).then_inc(read("z"), 1)
                if c % 2:
                    ada_row(24 + c)
            for s in range(40, 48):
                ada_row(s)

            def layer_norm(n, l, i, after):
                for k in range(KD):
                    act.wait_ge(read("mean"), KD * n + k + 1)
                    ac(hT[:, k, :], xT[:, k, :], ACT.Square).then_inc(sem("sq_ready"), 1)
                ps = await_bank(act, "var", n)
                ac(l_rs, ps[:, 0:T], ACT.Sqrt, bias=eps[:, :]).then_inc(read("var"), 1)
                for k in range(KD):
                    act.wait_ge(sem("xn_ready"), KD * n + k + 1)
                    if after:
                        modulate(*after, k, lambda k, v: h_bias[:, k, v:v + 1])
                    else:
                        ac(xT[:, k, :], xT[:, k, :], ACT.Identity, bias=ln_b(l, i, k)).then_inc(sem("x_final"), 1)
                if after:
                    for k in range(KD):
                        act.wait_ge(sem("h_ready"), KD * (n + 1) + k + 1)
                        ac(xT[:, k, :], xT[:, k, :], ACT.Identity, bias=ln_ab[:, k:k + 1],
                           scale=ALPHA).then_inc(sem("x_scaled"), 1)

            def moe(l):
                L = f"_{l}"
                act.wait_ge(sem("route_a"), 2 * l + 1)
                ac(r_eg, r_eg, ACT.Exp).then_inc(sem("route_b"), 1)
                act.wait_ge(sem("route_a"), 2 * l + 2)
                ac(r_e2, r_e2, ACT.Exp).then_inc(sem("route_b"), 1)
                for n in range(2 * NT):
                    ps = await_bank(act, "ht", 2 * NT * l + n)
                    ac(m_h[:, n // 2, 512 * (n % 2):512 * (n % 2) + 512], ps[:, :], ACT.Copy).then_inc(read("ht"), 1)
                fill = sem("mfill" + L)

                def pair(p, first):
                    for u in (0, 1):
                        act.wait_ge(fill, p * 10 + (u + 1))
                        ac(m_hg[:, u, 0:512], banks[2 * u][:, :], ACT.Copy)
                        ac(m_hg[:, u, 512:1024], banks[2 * u + 1][:, :], ACT.Copy).then_inc(sem("mT_read" + L), 1)
                    for u in (0, 1):
                        act.wait_ge(fill, p * 10 + (4 + 2 * u))
                        ac(m_sg[:, u, :], banks[4 + u][:, 0:2 * CH], ACT.Silu).then_inc(sem("mgate_read" + L), 1)
                    for u in (0, 1):
                        if not first:
                            act.wait_ge(sem(f"mout{u}" + L), p * 16)
                        for m in (0, 1):
                            act.wait_ge(fill, p * 10 + (7 + 2 * u + m))
                            ac(m_o[:, u, 512 * m:512 * m + 512], banks[(6, 2)[u] + m][0:CH, :],
                               ACT.Copy).then_inc(sem("mdn_read" + L), 1)
                        act.wait_ge(sem("mdn_read" + L), p * 4 + (2 * u + 2))
                        q = p * 2 + u
                        out = yg[CH * q:CH * q + CH, :] if first else yg[bass.ds(q * CH, CH), :]
                        act.dma_start(out, m_o[:, u, :]).then_inc(sem(f"mout{u}" + L), 16)

                act.wait_ge(sem("cleared"), 32)
                act.wait_ge(sem("planned"), l + 1)
                pairs = act.value_load(plan[0:1, 2 * MAXP:2 * MAXP + 1], min_val=MINP, max_val=MAXP)
                pair(0, True)
                with act.Fori(1, pairs) as p:
                    pair(p, False)
                for u in range(2):
                    act.wait_ge(sem(f"mout{u}" + L), pairs * 16)
                ac(m_mark, ident[:, 0:1], ACT.Copy).then_inc(sem("results_out"), 1)

            act.wait_ge(sem("mod_ready"), 2)
            layer_norm(0, 0, 0, (0, 24, False))
            moe(0)
            act.wait_ge(sem("mod_ready"), 3)
            layer_norm(1, 0, 1, (1, 0, True))

            ac(a_neg[:, :], a_log[:, :], ACT.Exp).then_inc(sem("dt_a"), 1)
            act.wait_ge(sem("dt_x"), 1)
            link(ac(b_u, b_u, ACT.Exp))
            ac(b_l, b_u, ACT.Ln, bias=1.0).then_inc(sem("dt_ln"), 1)
            act.wait_ge(sem("pads"), 2)

            def b_silu(c):
                out, w = (b_bc[:, c, :], 16 + c) if c < 8 else (b_xs[:, c - 8, :], c - 8)
                act.wait_ge(sem("bconv_ready"), c + 1)
                cb = b_cbuf[:, c % 2, :]
                ac(out[:, 0:TP], cb[:, 0:TP], ACT.Silu, bias=b_cbias(w))
                ac(out[:, TP:T], cb[:, TP + 2 * PAD:], ACT.Silu, bias=b_cbias(w)).then_inc(sem("xs_ready"), 1)

            for c in range(24):
                ps = await_bank(act, "xbc", c)
                if c >= 4:
                    act.wait_ge(sem("bconv_ready"), c - 3)
                padded(b_pre[:, c % 4, :], ps, "xbc")
                if c:
                    b_silu(c - 1)
            b_silu(23)
            act.wait_ge(sem("acs_ready"), 1)
            ac(b_u[:, 0:TP], b_acs[:, 0:TP], ACT.Exp, bias=acs_end, scale=-1.0).then_inc(sem("wr_exp"), 1)
            ac(b_es[:, TP:T], b_acs[:, TP:T], ACT.Exp).then_inc(sem("es_exp"), 1)
            for c in range(8):
                ps = await_bank(act, "h0", c)
                ac(b_h0[:, c // 4, 512 * (c % 4):512 * (c % 4) + 512], ps[:, :], ACT.Copy).then_inc(read("h0"), 1)
            ps = await_bank(act, "Bt", 0)
            ac(b_Bt.rearrange("p g n -> p (g n)"), ps[:, :], ACT.Copy).then_inc(read("Bt"), 1)
            for c in range(KE):
                ps = await_bank(act, "xt", c)
                ac(b_x[:, :, P * c:P * c + P], v3(ps[:, 0:T], NT), ACT.Copy).then_inc(read("xt"), 1)
            def new_state(n):
                g, d = divmod(n, 2)
                ps = await_bank(act, "sn", n)
                if n >= 2:
                    act.wait_ge(sem(f"out{n % 2}"), 16 * (OUT_C + n // 2))
                ac(b_st[:, n % 2, :], ps[:, :], ACT.Copy).then_inc(read("sn"), 1)
                act.wait_ge(read("sn"), n + 1)
                act.dma_start(o_["s"][0, 0, d, HG * g:HG * g + HG].rearrange("(k j) p n -> (j p) k n", j=2),
                              v3(b_st[:, n % 2, :], 4)).then_inc(sem(f"out{n % 2}"), 16)

            def products(g, which):
                if g >= 2:
                    act.wait_ge(sem("w_ready"), 2 * HG * (g - 1))
                ps = await_bank(act, which, g)
                if which == "cbP":
                    ac(b_cb[:, g % 2, 0:P], ps[:, 0:P], ACT.Copy).then_inc(read("cbP"), 1)
                else:
                    ac(b_cb[:, g % 2, P:5 * P], ps[:, :], ACT.Copy).then_inc(read("cbS"), 1)

            def z_tile(c):
                ps = await_bank(act, "zb", c)
                ac(b_z[:, c, :], ps[:, 0:T], ACT.Silu).then_inc(read("zb"), 1)

            products(0, "cbP")
            products(0, "cbS")
            for n in range(2 * G * HG):
                act.wait_ge(read("acsb"), n + 1)
                e = b_E[:, n // 2 % 2, n % 2, :]
                ac(e, e, ACT.Exp).then_inc(sem("be_ready"), 1)
                g, u = divmod(n, 2 * HG)
                if g + 1 < G and u in (12, 15):
                    products(g + 1, "cbP" if u == 12 else "cbS")
                if n % 4 == 1 and n > 4:
                    z_tile(n // 4 - 1)
                if g == G - 1 and u >= 4 and u % 2 == 0:
                    new_state(u // 2 - 2)
            new_state(6)
            z_tile(KE - 1)
            new_state(7)
            for c in range(KE):
                act.wait_ge(sem("g_ready"), c + 1)
                ac(b_sq[:, c, :], b_xs[:, c, :], ACT.Square).then_inc(sem("gsq_ready"), 1)
                ac(b_xs[:, c, :], b_xs[:, c, :], ACT.Copy, scale=b_nw(c)).then_inc(sem("gB_ready"), 1)
            act.wait_ge(read("msq"), 1)
            ac(l_rs, l_v, ACT.Sqrt).then_inc(sem("rms_sqrt"), 1)
            layer_norm(2, 1, 0, (1, 24, False))
            moe(1)
            layer_norm(3, 1, 1, None)
            for t in range(NT):
                for m in range(2):
                    n = 2 * t + m
                    ps = await_bank(act, "out", n)
                    if n >= 2:
                        act.wait_ge(sem(f"out{n % 2}"), 16 * (OUT_C + OUT_S + n // 2))
                    ac(y_out[:, n % 2, :], ps[:, :], ACT.Copy).then_inc(read("out"), 1)
                    act.wait_ge(read("out"), n + 1)
                    dst = o_["yp"][0] if t == 0 else o_["ys"][0, P * t - P:P * t]
                    act.dma_start(dst[:, 512 * m:512 * m + 512], y_out[:, n % 2, :]).then_inc(sem(f"out{n % 2}"), 16)
            act.wait_ge(sem("out_m"), 16)
            act.wait_ge(sem("out_n"), 16)
            for s in range(2):
                act.wait_ge(sem(f"out{s}"), 16 * (OUT_C + OUT_S + NT))

        @block.vector
        def _(dve):
            ve = nc.vector
            n_link = [0]

            def step(ins):
                n_link[0] += 1
                ins.then_inc(sem("dve_step"), 1)

            def settle():
                dve.wait_ge(sem("dve_step"), n_link[0])

            def link(ins):
                step(ins)
                settle()

            for i in range(5):
                ps = await_bank(dve, "par", i)
                ve.tensor_copy(par[:, i, 0:PROWS[i]], ps[:, 0:PROWS[i]]).then_inc(read("par"), 1)

            def ada(part, l, j0, j1):
                ps = await_bank(dve, "mod", part)
                bias = par[:, 0, 48 * l + j0:48 * l + j1].unsqueeze(2).to_broadcast([P, j1 - j0, 2])
                ve.tensor_tensor(out=mod[:, l, j0:j1, :], in0=ps[:, 2 * j0:2 * j1].rearrange("p (j v) -> p j v", v=2),
                                 in1=bias, op=ALU.add).then_inc(read("mod"), 1)
                dve.wait_ge(read("mod"), part + 1)
                for s in (8, 32):
                    if j0 <= s < j1:
                        last = ve.tensor_scalar(mod[:, l, s:s + 8, :], mod[:, l, s:s + 8, :], 1.0, None, ALU.add)
                last.then_inc(sem("mod_ready"), 1)

            dve.wait_ge(read("par"), 5)
            ada(0, 0, 0, 16)

            def conv(c, src, dst, w, ready):
                last = ve.tensor_scalar(dst, src[:, 0:W_PAD - 2 * PAD], w(0), None, ALU.mult)
                for j in range(1, TAPS):
                    link(last)
                    last = ve.scalar_tensor_tensor(out=dst, in0=src[:, j:j + W_PAD - 2 * PAD], scalar=w(j), in1=dst,
                                                   op0=ALU.mult, op1=ALU.add)
                last.then_inc(sem(ready), 1)

            for c in range(KE):
                dve.wait_ge(read("xu"), c + 1)
                if c >= 2:
                    dve.wait_ge(sem("xc_ready"), c - 1)
                conv(c, a_xu[:, c, :], a_cbuf[:, c % 2, :], lambda j: a_cw(j, c), "conv_ready")
            ada(1, 0, 16, 48)
            for c in range(KE):
                ps = await_bank(dve, "kT", c)
                ve.tensor_copy(a_kT[:, c, :], ps[:, 0:T]).then_inc(read("kT"), 1)
                ps = await_bank(dve, "v", c)
                ve.tensor_copy(a_v[:, :, P * c:P * c + P], v3(ps[:, 0:T], NT)).then_inc(read("v"), 1)
            ps = await_bank(dve, "gates", 0)
            ve.tensor_copy(a_grow, ps[0:96, 0:T]).then_inc(read("gates"), 1)
            for kind in range(4):
                ps = await_bank(dve, "grow", kind)
                ve.tensor_scalar(a_rowG[:, kind, :], ps[0:H, 0:T], b_gates[:, kind:kind + 1], None,
                                 ALU.add).then_inc(read("grow"), 1)
            dve.wait_ge(read("grow"), 4)
            ig, fg = a_rowG[:, 0:4:2, :], a_rowG[:, 1:4:2, :]
            ve.scalar_tensor_tensor(out=a_u, in0=fg, scalar=-1.0, in1=fg, op0=ALU.mult,
                                    op1=ALU.min).then_inc(sem("gate_x"), 1)
            dve.wait_ge(sem("gate_ln"), 1)
            link(ve.scalar_tensor_tensor(out=a_lf, in0=fg, scalar=0.0, in1=a_u, op0=ALU.min, op1=ALU.subtract))

            def both_ways(f):
                for d in range(2):
                    for v, (t0, t1) in enumerate(STREAMS):
                        view = (lambda ap, t0=t0, t1=t1: ap[:, t0:t1]) if d == 0 else \
                            (lambda ap, t0=t0, t1=t1: ap[:, t0:t1][:, ::-1])
                        step(f(d, v, view, t1 - t0))
                settle()

            both_ways(lambda d, v, view, n: ve.tensor_tensor_scan(
                out=view(a_b[:, d]), data0=ones[0:H, 0:1].to_broadcast([H, n]), data1=view(a_lf[:, d]), initial=0.0,
                op0=ALU.mult, op1=ALU.add))
            link(ve.tensor_tensor(out=a_a, in0=ig, in1=a_b, op=ALU.subtract))
            both_ways(lambda d, v, view, n: ve.tensor_tensor_scan(
                out=view(a_nM[:, d]), data0=view(a_a[:, d]), data1=view(a_a[:, d]),
                initial=m0[:, d:d + 1] if v else 0.0, op0=ALU.max, op1=ALU.max))
            step(ve.memset(a_wi[:, :, 0:TP], 0.0))
            for d in range(2):
                end = TP - 1 if d == 0 else 0
                step(ve.tensor_tensor(out=m_new[:, d:d + 1], in0=a_b[:, d, end:end + 1], in1=a_nM[:, d, end:end + 1],
                                      op=ALU.add))
            link(ve.scalar_tensor_tensor(out=a_fl, in0=a_nM, scalar=-1.0, in1=a_b, op0=ALU.mult, op1=ALU.subtract))
            ve.tensor_scalar(a_nM, a_nM, -1.0, None, ALU.mult).then_inc(sem("gate_m"), 1)

            ps = await_bank(dve, "col", 0)
            link(ve.tensor_scalar(c_wi.rearrange("p t d h -> p (t d h)"), ps[:, 32:48], DH ** -0.5, None, ALU.mult))
            step(ve.tensor_copy(c_nM.rearrange("p t d h -> p (t d h)"), ps[:, 0:24]))
            step(ve.tensor_copy(c_wk, ps[:, 72:80]))
            ve.tensor_copy(c_fl.rearrange("p t d h -> p (t d h)"), ps[:, 48:72]).then_inc(read("col"), 1)
            dve.wait_ge(read("col"), 1)
            settle()

            TILES = ((0, 0, P), (1, P, TS), (2, P + TS, TS))

            def strip(d, t):
                s = (strip_f, strip_b)[d]
                return s[:, P:2 * P] if t == 0 else s[:, P:3 * P] if t == 1 else s[:, 0:2 * P]

            def weights(h):
                E = a_E[:, h % 2]
                if h >= 2:
                    dve.wait_ge(filled, group["pTP", h - 2][1])
                for d in range(2):
                    ps = await_bank(dve, "abc", 2 * h + d)
                    for t, o, n in TILES:
                        src = ps[:, 0:TP] if t == 0 else ps[:, TP:T]
                        ins = ve.scalar_tensor_tensor(out=E[:, d, o:o + n], in0=src, scalar=c_nM[:, t, d, h:h + 1],
                                                      in1=strip(d, t), op0=ALU.add, op1=ALU.min)
                    ins.then_inc(read("abc"), 1)
                for t, o, n in TILES:
                    b = await_bank(dve, "scP" if t == 0 else "scS", h)
                    src = b[:, 0:TP] if t == 0 else b[:, TS * (t - 1):TS * t]
                    for d in range(2):
                        if t == 0:
                            dve.wait_ge(sem("e_ready"), 2 * h + d + 1)
                        ins = ve.scalar_tensor_tensor(out=E[:, d, o:o + n], in0=src, scalar=DH ** -0.5,
                                                      in1=E[:, d, o:o + n], op0=ALU.mult, op1=ALU.mult,
                                                      accum_out=den[:, 2 * t + d:2 * t + d + 1])
                        if d and t == 0:
                            ins.then_inc(read("scP"), 1)
                        elif d and t == 2:
                            ins.then_inc(read("scS"), 1)
                dve.wait_ge(read("scS"), h + 1)
                dve.wait_ge(read("scP"), h + 1)
                ps = await_bank(dve, "qn", h)
                wi = c_wi[:, :, :, h]
                ve.tensor_tensor(out=qn.rearrange("p (t d) -> p t d", d=2),
                                 in0=ps[:, 0:4].rearrange("p (t d) -> p t d", d=2),
                                 in1=wi, op=ALU.mult).then_inc(read("qn"), 1)
                dve.wait_ge(read("qn"), h + 1)
                settle()
                link(ve.tensor_tensor(out=den[:, 2:6], in0=den[:, 2:6], in1=qn, op=ALU.add))
                link(ve.scalar_tensor_tensor(out=den[:, :], in0=den[:, :], scalar=-1.0, in1=den[:, :], op0=ALU.mult,
                                             op1=ALU.max))
                link(ve.tensor_tensor(out=den.rearrange("p (t d) -> p t d", d=2),
                                      in0=den.rearrange("p (t d) -> p t d", d=2), in1=c_fl[:, :, :, h], op=ALU.max))
                link(ve.reciprocal(rden, den))
                ve.tensor_tensor(out=cwt[:, h, :].rearrange("p (t d) -> p t d", d=2),
                                 in0=rden[:, 2:6].rearrange("p (t d) -> p t d", d=2), in1=wi,
                                 op=ALU.mult).then_inc(sem("cw_ready"), 1)
                for t, o, n in TILES:
                    ins = ve.tensor_scalar(E[:, 0, o:o + n], E[:, 0, o:o + n], rden[:, 2 * t:2 * t + 1], None, ALU.mult)
                link(ins)
                for t, o, n in TILES:
                    ins = ve.scalar_tensor_tensor(out=E[:, 0, o:o + n], in0=E[:, 1, o:o + n],
                                                  scalar=rden[:, 2 * t + 1:2 * t + 2], in1=E[:, 0, o:o + n],
                                                  op0=ALU.mult, op1=ALU.add)
                ins.then_inc(sem("p_ready"), 1)

            weights(0)
            for h in range(H):
                if h + 1 < H:
                    weights(h + 1)
                dve.wait_ge(sem("cw_ready"), h + 1)
                for t in range(2):
                    dve.wait_ge(read("qc0"), 2 * h + t + 1)
                    ps = await_bank(dve, "qc1", 2 * h + t)
                    ve.scalar_tensor_tensor(out=a_tmp[:, t, :], in0=ps[:, :], scalar=cw(h, t, 1), in1=a_tmp[:, t, :],
                                            op0=ALU.mult, op1=ALU.add).then_inc(read("qc1"), 1)
                ps = await_bank(dve, "kt", h)
                if h:
                    dve.wait_ge(filled, group["nn", h - 1][1])
                for d in range(2):
                    ve.tensor_scalar(a_kw[:, d, :], ps[:, :], c_wk[:, 4 * d + h:4 * d + h + 1], None,
                                     ALU.mult).then_inc(read("kt"), 1)
                for t in range(NT):
                    ps = await_bank(dve, "pv", NT * h + t)
                    out = a_h[:, t, DH * h:DH * h + DH]
                    if t == 0:
                        ve.tensor_copy(out, ps[:, :]).then_inc(read("pv"), 1)
                    else:
                        dve.wait_ge(read("qc1"), 2 * h + t)
                        ve.tensor_tensor(out=out, in0=ps[:, :], in1=a_tmp[:, t - 1, :], op=ALU.add).then_inc(read("pv"), 1)
                for t in range(NT):
                    dve.wait_ge(read("pv"), NT * h + t + 1)
                    link(ve.bn_stats(bst[:, 0:6], a_h[:, t, DH * h:DH * h + DH]))
                    link(ve.bn_aggr(h_mv[:, NT * h + t, :], bst[:, 0:6]))
                ps = await_bank(dve, "nn", h)
                ve.tensor_copy(nT[:, :, h, :], ps[:, 0:8].rearrange("p (d j) -> p d j", d=2)).then_inc(read("nn"), 1)
            ve.tensor_scalar(h_rs, h_mv[:, :, 1], EPS, None, ALU.add).then_inc(sem("hvar_ready"), 1)
            ps = await_bank(dve, "nrow", 0)
            ve.tensor_copy(nrow[:, :], ps[0:32, 0:P]).then_inc(read("nrow"), 1)
            dve.wait_ge(sem("hsqrt"), 1)
            link(ve.reciprocal(h_rs, h_rs))
            for h in range(H):
                for t in range(NT):
                    n = NT * h + t
                    hh = a_h[:, t, DH * h:DH * h + DH]
                    ve.tensor_scalar(hh, hh, h_mv[:, n, 0:1], h_rs[:, n:n + 1], ALU.subtract,
                                     ALU.mult).then_inc(sem("hn_ready"), 1)
            dve.wait_ge(sem("skip_ready"), KE)
            for c in range(KE):
                ps = await_bank(dve, "hn", c)
                xc = a_xc[:, c, :]
                ve.scalar_tensor_tensor(out=xc, in0=ps[:, 0:T], scalar=a_nw(c), in1=xc, op0=ALU.mult,
                                        op1=ALU.add).then_inc(read("hn"), 1)
                dve.wait_ge(read("hn"), c + 1)
                dve.wait_ge(read("z"), c + 1)
                ve.tensor_tensor(out=xc, in0=xc, in1=a_sz[:, c, :], op=ALU.mult).then_inc(sem("gA_ready"), 1)

            def residual(n, l, gate, m, src, done, permuted=False):
                dve.wait_ge(sem("x_scaled"), KD * n + m + 1)
                for v, (t0, t1) in enumerate(STREAMS):
                    x, s = xT[:, m, t0:t1], src[:, t0:t1]
                    if permuted and v:
                        x = x.rearrange("p (r w) -> p r w", r=ROWS)
                        s = s.rearrange("p (w r) -> p r w", r=ROWS)
                    ins = ve.scalar_tensor_tensor(out=x, in0=s, scalar=mod[:, l, gate + m, v:v + 1], in1=x, op0=ALU.mult,
                                                  op1=ALU.add)
                ins.then_inc(done, 1)

            def layer_norm(n, l, i, after):
                if after:
                    lm, shift, _ = after
                    b = par[:, 2, 32 + 16 * l + 8 * i:40 + 16 * l + 8 * i]
                    step(ve.tensor_scalar(ln_ab, b, ALPHA, None, ALU.mult))
                    link(ve.tensor_tensor(out=h_bias, in0=b.unsqueeze(2).to_broadcast([P, KD, 2]),
                                          in1=mod[:, lm, shift + 8:shift + 16, :], op=ALU.mult))
                    link(ve.tensor_tensor(out=h_bias, in0=h_bias, in1=mod[:, lm, shift:shift + 8, :], op=ALU.add))
                ps = await_bank(dve, "mean", n)
                dve.wait_ge(sem("r_ready"), KD * n + KD)
                for k in range(KD):
                    ve.tensor_tensor(out=xT[:, k, :], in0=xT[:, k, :], in1=ps[:, 0:T],
                                     op=ALU.subtract).then_inc(read("mean"), 1)
                dve.wait_ge(read("var"), n + 1)
                dve.wait_ge(read("mean"), KD * n + KD)
                dve.wait_ge(sem("sq_ready"), KD * n + KD)
                link(ve.reciprocal(l_rs, l_rs))
                for k in range(KD):
                    ve.scalar_tensor_tensor(out=xT[:, k, :], in0=xT[:, k, :], scalar=ln_w(l, i, k), in1=l_rs,
                                            op0=ALU.mult, op1=ALU.mult).then_inc(sem("xn_ready"), 1)

            def bc(ap, n):
                return ap.unsqueeze(len(ap.shape)).to_broadcast(list(ap.shape) + [n])

            rk = rank[:, :].unsqueeze(1).to_broadcast([P, NT, 4])

            def first_max(src, mx, out, tmp):
                link(ve.tensor_reduce(mx, src, X, ALU.max))
                link(ve.tensor_tensor(out=tmp, in0=src, in1=bc(mx, 4), op=ALU.is_equal))
                link(ve.tensor_tensor(out=tmp, in0=tmp, in1=rk, op=ALU.mult))
                link(ve.tensor_reduce(r_mp, tmp, X, ALU.max))
                link(ve.tensor_tensor(out=out, in0=tmp, in1=bc(r_mp, 4), op=ALU.is_equal))

            def moe(l):
                L = f"_{l}"
                ps = await_bank(dve, "rows", l)
                ve.tensor_copy(m_rows, ps[:, 0:T]).then_inc(read("rows"), 1)
                ps = await_bank(dve, "route", l)
                ve.tensor_copy(m_L.rearrange("p t c -> p (t c)"), ps[:, 0:60]).then_inc(read("route"), 1)
                dve.wait_ge(read("route"), l + 1)
                lg, le = m_L[:, :, 0:4], m_L[:, :, 4:20].rearrange("p t (g e) -> p t g e", g=NG)
                first_max(lg, r_mx, r_ohg, r_t4)
                ve.tensor_tensor(out=r_eg, in0=lg, in1=bc(r_mx, 4), op=ALU.subtract).then_inc(sem("route_a"), 1)
                for t in range(NT):
                    ins = ve.tensor_tensor(out=r_t16[:, t], in0=le[:, t], in1=bc(r_ohg[:, t], 4), op=ALU.mult)
                link(ins)
                link(ve.tensor_reduce(r_sel, r_t16.rearrange("p t g e -> p t e g"), X, ALU.add))
                first_max(r_sel, r_m1, r_oh1, r_t4)
                link(ve.scalar_tensor_tensor(out=r_sel, in0=r_oh1, scalar=-BIG, in1=r_sel, op0=ALU.mult, op1=ALU.add))
                first_max(r_sel, r_m2, r_oh2, r_t4)
                ve.tensor_tensor(out=r_e2, in0=r_m2, in1=r_m1, op=ALU.subtract).then_inc(sem("route_a"), 1)
                for i, oh in enumerate((r_oh1, r_oh2)):
                    for t in range(NT):
                        ins = ve.tensor_tensor(out=m_F[:, i, t, :].rearrange("p (g e) -> p g e", g=NG),
                                               in0=bc(r_ohg[:, t], 4), in1=oh[:, t].unsqueeze(1).to_broadcast([P, NG, NE]),
                                               op=ALU.mult)
                link(ins)
                ve.tensor_tensor(out=m_A, in0=m_F[:, 0], in1=m_F[:, 1], op=ALU.add).then_inc(sem("chosen"), 1)
                ps = await_bank(dve, "count", l)
                ve.tensor_copy(m_sl.rearrange("p t e -> p (t e)"), ps[:, 0:48])
                ve.tensor_copy(m_cnt, ps[:, 48:64]).then_inc(read("count"), 1)
                dve.wait_ge(read("count"), l + 1)
                link(ve.tensor_scalar(m_n, m_cnt, 0.0, None, ALU.is_gt))
                for j in range(1, T // CH):
                    link(ve.scalar_tensor_tensor(out=m_n, in0=m_cnt, scalar=float(CH * j), in1=m_n, op0=ALU.is_gt,
                                                 op1=ALU.add))
                link(ve.tensor_tensor_scan(out=m_end, data0=ones[:, 0:1].to_broadcast([P, NEXP]), data1=m_n,
                                           initial=0.0, op0=ALU.mult, op1=ALU.add))
                link(ve.tensor_tensor(out=m_base, in0=m_end, in1=m_n, op=ALU.subtract))
                for t in range(NT):
                    ins = ve.scalar_tensor_tensor(out=m_sl[:, t, :], in0=m_base, scalar=float(CH), in1=m_sl[:, t, :],
                                                  op0=ALU.mult, op1=ALU.add)
                link(ins)
                for i in range(2):
                    ins = ve.tensor_tensor(out=m_F[:, i], in0=m_F[:, i], in1=m_sl, op=ALU.mult)
                link(ins)
                for i in range(2):
                    ins = ve.tensor_reduce(m_sf[:, i, :], m_F[:, i], X, ALU.add)
                link(ins)
                ve.tensor_copy(slots[:, :], m_sf.rearrange("p i t -> p (i t)")).then_inc(sem("slots_ready"), 1)
                link(ve.tensor_tensor(out=m_cmp, in0=m_end[0:1, :].unsqueeze(1).to_broadcast([1, 2 * MAXP, NEXP]),
                                      in1=bc(chunk_no[:, :], NEXP), op=ALU.is_le))
                link(ve.tensor_reduce(m_eq, m_cmp, X, ALU.add))
                link(ve.tensor_scalar(m_eq, m_eq, float(NEXP - 1), None, ALU.min))
                ve.tensor_copy(plan[0:1, 0:2 * MAXP], m_eq)
                even = chunk_no[:, :].rearrange("o (p u) -> o p u", u=2)[:, :, 0]
                link(ve.tensor_tensor(out=m_even, in0=even,
                                      in1=m_end[0:1, NEXP - 1:NEXP].to_broadcast([1, MAXP]), op=ALU.is_lt))
                link(ve.tensor_reduce(m_eq[:, 0:1], m_even, X, ALU.add))
                ve.tensor_copy(plan[0:1, 2 * MAXP:2 * MAXP + 1], m_eq[:, 0:1]).then_inc(sem("planned"), 1)

                dve.wait_ge(sem("route_b"), 2 * l + 2)
                link(ve.tensor_reduce(r_gs, r_eg, X, ALU.add))
                link(ve.scalar_tensor_tensor(out=r_w1, in0=r_e2, scalar=1.0, in1=r_gs, op0=ALU.add, op1=ALU.mult))
                link(ve.reciprocal(r_w1, r_w1))
                link(ve.tensor_tensor(out=r_w2, in0=r_w1, in1=r_e2, op=ALU.mult))

                def pair(p, first):
                    for u in (0, 1):
                        dve.wait_ge(sem("mgate_read" + L), p * 2 + (u + 1))
                        dve.wait_ge(sem("mfill" + L), p * 10 + (4 + 2 * u))
                        ve.tensor_tensor(out=m_a[:, u].rearrange("p f c -> p (f c)"), in0=m_sg[:, u, :],
                                         in1=banks[4 + u][:, 2 * CH:4 * CH], op=ALU.mult).then_inc(sem("mup_read" + L), 1)

                pairs = dve.value_load(plan[0:1, 2 * MAXP:2 * MAXP + 1], min_val=MINP, max_val=MAXP)
                pair(0, True)
                with dve.Fori(1, pairs) as p:
                    pair(p, False)
                for t in range(NT):
                    dve.wait_ge(sem(f"gathered{t}"), 32 * (l + 1))
                    link(ve.tensor_scalar(m_y[:, 0, t, :], m_y[:, 0, t, :], r_w1[:, t:t + 1], None, ALU.mult))
                    ve.scalar_tensor_tensor(out=m_y[:, 0, t, :], in0=m_y[:, 1, t, :], scalar=r_w2[:, t:t + 1],
                                            in1=m_y[:, 0, t, :], op0=ALU.mult, op1=ALU.add).then_inc(sem("moe_sum"), 1)
                for m in range(KD):
                    residual(2 * l + 1, l, 40, m, await_bank(dve, "yt", KD * l + m)[:, 0:T], sem("r_ready"))

            dve.wait_ge(sem("out_n"), 16)
            for m in range(KD):
                residual(0, 0, 16, m, await_bank(dve, "yA", m)[:, 0:T], sem("r_ready"))
            ada(2, 1, 0, 48)
            layer_norm(0, 0, 0, (0, 24, False))
            moe(0)
            layer_norm(1, 0, 1, (1, 0, True))

            ps = await_bank(dve, "dt", 0)
            ve.tensor_scalar(b_dt, ps[0:64, 0:T], dt_bias[:, :], None, ALU.add).then_inc(read("dt"), 1)
            dve.wait_ge(read("dt"), 1)
            ve.scalar_tensor_tensor(out=b_u, in0=b_dt, scalar=-1.0, in1=b_dt, op0=ALU.mult,
                                    op1=ALU.min).then_inc(sem("dt_x"), 1)
            dve.wait_ge(sem("dt_ln"), 1)
            link(ve.tensor_scalar(b_es, b_u, 1.0, None, ALU.add))
            link(ve.tensor_scalar(b_eq, b_es, 1.0, None, ALU.is_equal))
            step(ve.scalar_tensor_tensor(out=b_es, in0=b_es, scalar=-1.0, in1=b_eq, op0=ALU.add, op1=ALU.add))
            link(ve.tensor_tensor(out=b_l, in0=b_l, in1=b_eq, op=ALU.add))
            link(ve.reciprocal(b_es, b_es))
            link(ve.tensor_tensor(out=b_l, in0=b_l, in1=b_es, op=ALU.mult))
            link(ve.tensor_tensor(out=b_l, in0=b_l, in1=b_u, op=ALU.mult))
            link(ve.scalar_tensor_tensor(out=b_dt, in0=b_dt, scalar=0.0, in1=b_l, op0=ALU.max, op1=ALU.add))
            dve.wait_ge(sem("dt_a"), 1)
            link(ve.tensor_scalar(b_l, b_dt, a_neg[:, :], -1.0, ALU.mult, ALU.mult))
            for d in range(2):
                q = slice(32 * d, 32 * d + 32)
                for t0, t1 in STREAMS:
                    view = (lambda ap: ap[q, t0:t1]) if d == 0 else (lambda ap: ap[q, t0:t1][:, ::-1])
                    step(ve.tensor_tensor_scan(out=view(b_acs), data0=ones[q, 0:1].to_broadcast([32, t1 - t0]),
                                               data1=view(b_l), initial=0.0, op0=ALU.mult, op1=ALU.add))
            settle()
            for d in range(2):
                q = slice(32 * d, 32 * d + 32)
                end = TP - 1 if d == 0 else 0
                ins = ve.tensor_copy(acs_end[q, :], b_acs[q, end:end + 1])
            ins.then_inc(sem("acs_ready"), 1)
            link(ve.tensor_copy(ident_b, ident[0:64, 0:64]))
            link(ve.tensor_copy(b_l, b_acs))
            for i in range(3):
                link(ve.tensor_copy(acs_parts[:, i, :], b_l))
                if i < 2:
                    link(ve.tensor_tensor(out=b_l, in0=b_l, in1=acs_parts[:, i, :], op=ALU.subtract))

            def rows_done():
                dve.wait_ge(sem("wr_exp"), 1)
                dve.wait_ge(sem("es_exp"), 1)
                ve.tensor_tensor(out=b_es[:, 0:TP], in0=b_u[:, 0:TP], in1=b_dt[:, 0:TP],
                                 op=ALU.mult).then_inc(sem("brows_ready"), 1)

            for c in range(24):
                w = 16 + c if c < 8 else c - 8
                dve.wait_ge(read("xbc"), c + 1)
                if c >= 2:
                    dve.wait_ge(sem("xs_ready"), c - 1)
                conv(c, b_pre[:, c % 4, :], b_cbuf[:, c % 2, :], lambda j: b_cw(j, w), "bconv_ready")
            rows_done()
            ps = await_bank(dve, "bcol0", 0)
            step(ve.tensor_scalar(b_col[:, 0:192], ps[:, 0:192], -1.0, None, ALU.mult))
            ve.tensor_copy(b_col[:, 192:384], ps[:, 192:384]).then_inc(read("bcol0"), 1)
            ps = await_bank(dve, "bcol1", 0)
            step(ve.tensor_copy(b_col[:, 512:576], ps[:, 0:64]))
            ve.tensor_copy(b_col[:, 384:512], ps[:, 64:192]).then_inc(read("bcol1"), 1)
            dve.wait_ge(read("bcol0"), 1)
            dve.wait_ge(read("bcol1"), 1)
            settle()
            nacs = lambda t, r: b_col[:, 64 * t + r:64 * t + r + 1]
            dtc = lambda t, r: b_col[:, 192 + 64 * t + r:193 + 64 * t + r]

            def segments(g, d):
                cb = b_cb[:, g % 2, :]
                if d == 0:
                    return ((0, 0, P, 0, strip_b[:, P:2 * P], cb[:, 0:P]),
                            (1, P, 2 * P, TP, strip_b[:, P:3 * P], cb[:, P:3 * P]),
                            (2, 3 * P, P, 2 * P, strip_b[:, P:2 * P], cb[:, 4 * P:5 * P]))
                return ((0, 0, P, 0, strip_f[:, P:2 * P], cb[:, 0:P]),
                        (1, P, P, TP, strip_f[:, P:2 * P], cb[:, P:2 * P]),
                        (2, 2 * P, 2 * P, TP, strip_f[:, 0:2 * P], cb[:, 3 * P:5 * P]))

            def args(n):
                head, d = divmod(n, 2)
                if n >= 4:
                    dve.wait_ge(filled, group["w_used", n - 4])
                ps = await_bank(dve, "acsb", n)
                for t, o, w, s0, mask, _ in segments(0, d):
                    ins = ve.scalar_tensor_tensor(out=b_E[:, head % 2, d, o:o + w], in0=ps[:, s0:s0 + w],
                                                  scalar=nacs(t, 32 * d + head), in1=mask, op0=ALU.add, op1=ALU.min)
                ins.then_inc(read("acsb"), 1)

            def cached(g, i):
                d, t = i // 2, i % 2 + 1
                if d and (g or i > 2):
                    dve.wait_ge(sem("inter_ready"), 2 * g + i - 2)
                ps = await_bank(dve, "inter", 4 * g + i)
                c0 = 384 + 64 * (t - 1) + 32 * d + HG * g
                out = b_part if d else b_inter[:, g % 2, t - 1, :]
                ve.tensor_tensor(out=out.rearrange("p (h c) -> p h c", h=HG), in0=ps.rearrange("p (h c) -> p h c", h=HG),
                                 in1=bc(b_col[:, c0:c0 + HG], PH), op=ALU.mult).then_inc(read("inter"), 1)
                if d:
                    dve.wait_ge(read("inter"), 4 * g + i + 1)
                    both = b_inter[:, g % 2, t - 1, :]
                    ve.tensor_tensor(out=both, in0=both, in1=b_part, op=ALU.add).then_inc(sem("inter_ready"), 1)

            def gated(c):
                ps = await_bank(dve, "y", c)
                xs = b_xs[:, c, :]
                ve.scalar_tensor_tensor(out=xs, in0=xs, scalar=d_skip[:, c:c + 1], in1=ps[:, 0:T], op0=ALU.mult,
                                        op1=ALU.add).then_inc(read("y"), 1)
                dve.wait_ge(read("y"), c + 1)
                dve.wait_ge(read("zb"), c + 1)
                ve.tensor_tensor(out=xs, in0=xs, in1=b_z[:, c, :], op=ALU.mult).then_inc(sem("g_ready"), 1)

            for i in range(4):
                cached(0, i)
            args(0)
            args(1)
            for n in range(2 * G * HG):
                if n + 2 < 2 * G * HG:
                    args(n + 2)
                head, d = divmod(n, 2)
                g, u = divmod(n, 2 * HG)
                if u == 0:
                    dve.wait_ge(read("cbP"), g + 1)
                    dve.wait_ge(read("cbS"), g + 1)
                dve.wait_ge(sem("be_ready"), n + 1)
                for t, o, w, _, _, cbs in segments(g, d):
                    e = b_E[:, head % 2, d, o:o + w]
                    ins = ve.scalar_tensor_tensor(out=e, in0=e, scalar=dtc(t, 32 * d + head), in1=cbs, op0=ALU.mult,
                                                  op1=ALU.mult)
                ins.then_inc(sem("w_ready"), 1)
                if g + 1 < G and u in (3, 5, 7, 9):
                    cached(g + 1, (u - 3) // 2)
                if n % 4 == 2 and n > 4:
                    gated(n // 4 - 1)
            gated(KE - 1)
            for s in range(2):
                dve.wait_ge(sem(f"out{s}"), 16 * (OUT_C + OUT_S))
            ps = await_bank(dve, "msq", 0)
            ve.tensor_scalar(l_v, ps[:, 0:T], float(D) / E2, EPS, ALU.mult, ALU.add).then_inc(read("msq"), 1)
            dve.wait_ge(sem("rms_sqrt"), 1)
            link(ve.reciprocal(l_rs, l_rs))
            for m in range(KD):
                ps = await_bank(dve, "yB", m)
                if m >= 2:
                    dve.wait_ge(sem("r_ready"), 2 * KD + m - 1)
                ve.tensor_tensor(out=b_t[:, m % 2, 0:T], in0=ps[:, 0:T], in1=l_rs, op=ALU.mult).then_inc(read("yB"), 1)
                dve.wait_ge(read("yB"), m + 1)
                residual(2, 1, 16, m, b_t[:, m % 2, 0:T], sem("r_ready"), permuted=True)
            layer_norm(2, 1, 0, (1, 24, False))
            moe(1)
            layer_norm(3, 1, 1, None)


_INS = ["x_prompt", "x_sample", "state_mlstm_C", "state_mlstm_n", "state_mlstm_m", "state_ssd", "c", "c_ctx",
        "ada_w", "ada_b", "ln_w", "ln_b", "a_w_in", "a_conv_w", "a_conv_b", "a_w_q", "a_w_k", "a_w_v", "a_w_gates",
        "a_b_gates", "a_norm_w", "a_skip", "a_w_down", "b_w_in", "b_conv_w", "b_conv_b", "b_dt_bias", "b_a_log",
        "b_d_skip", "b_norm_w", "b_w_out", "moe_w_rg", "moe_b_rg", "moe_w_re", "moe_b_re", "moe_w_gate",
        "moe_w_up", "moe_w_down"]
_OUTS = {"yp": (1, TP, D), "ys": (1, TS, D), "C": (1, 1, 2, H, DH, DH), "n": (1, 1, 2, H, DH), "m": (1, 1, 2, H),
         "s": (1, 1, 2, G * HG, PH, P)}


def kernel(**inputs):
    import numpy as np
    import concourse.bacc as bacc
    from concourse.bass_utils import run_bass_kernel_spmd

    nc = bacc.Bacc("TRN2", target_bir_lowering=False, num_devices=1)
    arrays, ins, outs = {}, {}, {}
    for name in _INS:
        a = np.ascontiguousarray(inputs[name])
        arrays["in_" + name] = a
        ins[name] = nc.dram_tensor("in_" + name, a.shape, mybir.dt.from_np(a.dtype), kind="ExternalInput").ap()
    for name, shape in _OUTS.items():
        outs[name] = nc.dram_tensor("out_" + name, shape, F32, kind="ExternalOutput").ap()
    program(nc, ins, outs)
    r = run_bass_kernel_spmd(nc, [arrays], core_ids=[0]).results[0]
    return tuple(r["out_" + name] for name in _OUTS)
```
